# Optimizing a Trainium2 kernel written in Bass

```python
import jax, jax.numpy as jnp
from jax import lax
import numpy as np

D_MODEL = 1024
BATCH = 1
SEQ = 1024
DEPTH = 1

HEAD_DIM = 64
SWA_Q_HEADS = 8
SWA_KV_HEADS = 2
SWA_GROUP = SWA_Q_HEADS // SWA_KV_HEADS
WINDOW = 128
BLOCK = 128
FOX_HEADS = 8
SWA_WIDTH = SWA_Q_HEADS * HEAD_DIM
SWA_KV_WIDTH = SWA_KV_HEADS * HEAD_DIM
FOX_WIDTH = FOX_HEADS * HEAD_DIM
NUM_BUCKETS = 32
MAX_DISTANCE = 128
PEER_HEADS = 8
N_KEYS = 128
N_EXPERTS = N_KEYS * N_KEYS
PEER_TOPK = 16
PEER_QDIM = 128
PEER_HALF = PEER_QDIM // 2
PEER_CHUNK = 128
N_MOD = 6
EPS = 1e-6
NEG = -1e30
IN_SPLITS = (SWA_WIDTH, SWA_KV_WIDTH, SWA_KV_WIDTH, FOX_WIDTH, FOX_WIDTH, FOX_WIDTH, FOX_HEADS, D_MODEL, D_MODEL)
IN_WIDTH = sum(IN_SPLITS)
IN_OFFSETS = tuple(int(o) for o in np.cumsum(IN_SPLITS)[:-1])

kernel_name = "gated_swa_fox_peer_hybrid"

def _rmsnorm(x, g):
    xf = x.astype(jnp.float32)
    xf = xf * lax.rsqrt(jnp.mean(xf * xf, axis=-1, keepdims=True) + EPS)
    return xf.astype(x.dtype) * g

def _modulate(h, shift, scale):
    return h * (1 + scale[:, None, :]) + shift[:, None, :]

def _t5_bucket(dist):
    dist = np.clip(dist, 0, None)
    max_exact = NUM_BUCKETS // 2
    large = max_exact + (np.log(np.maximum(dist, 1) / max_exact) / np.log(MAX_DISTANCE / max_exact)
                         * (NUM_BUCKETS - max_exact)).astype(np.int32)
    large = np.minimum(large, NUM_BUCKETS - 1)
    return np.where(dist < max_exact, dist, large).astype(np.int32)

def _swa_attention(q, k, v, sinks, rel_bias):
    B, S = q.shape[0], q.shape[1]
    nb = S // BLOCK
    q = q.reshape(B, nb, BLOCK, SWA_KV_HEADS, SWA_GROUP, HEAD_DIM)
    k = k.reshape(B, S, SWA_KV_HEADS, HEAD_DIM)
    v = v.reshape(B, S, SWA_KV_HEADS, HEAD_DIM)

    def band(t):
        tp = jnp.pad(t, ((0, 0), (BLOCK, 0), (0, 0), (0, 0)))
        prev = tp[:, :S].reshape(B, nb, BLOCK, SWA_KV_HEADS, HEAD_DIM)
        return jnp.concatenate([prev, t.reshape(B, nb, BLOCK, SWA_KV_HEADS, HEAD_DIM)], axis=2)

    kb, vb = band(k), band(v)
    logits = jnp.einsum('bnqhgd,bnkhd->bnhgqk', q, kb).astype(jnp.float32) * (HEAD_DIM ** -0.5)
    qi = np.arange(BLOCK)[:, None]
    kj = np.arange(2 * BLOCK)[None, :]
    dist = qi + BLOCK - kj
    in_band = (dist >= 0) & (dist < WINDOW)
    key_exists = (np.arange(nb)[:, None, None] * BLOCK + kj[None] - BLOCK) >= 0
    valid = in_band[None] & key_exists
    bias = rel_bias[_t5_bucket(dist)].astype(jnp.float32)
    bias = jnp.transpose(bias, (2, 0, 1)).reshape(SWA_KV_HEADS, SWA_GROUP, BLOCK, 2 * BLOCK)
    logits = logits + bias[None, None]
    logits = jnp.where(valid[None, :, None, None], logits, NEG)
    sink = jnp.broadcast_to(sinks.astype(jnp.float32).reshape(SWA_KV_HEADS, SWA_GROUP, 1, 1),
                            logits.shape[:-1] + (1,))
    p = jax.nn.softmax(jnp.concatenate([logits, sink], axis=-1), axis=-1)[..., :-1]
    o = jnp.einsum('bnhgqk,bnkhd->bnqhgd', p.astype(v.dtype), vb)
    return o.reshape(B, S, SWA_WIDTH)

def _fox_attention(q, k, v, log_f):
    B, S = q.shape[0], q.shape[1]
    nb = S // BLOCK
    q = q.reshape(B, S, FOX_HEADS, HEAD_DIM)
    k = k.reshape(B, S, FOX_HEADS, HEAD_DIM)
    v = v.reshape(B, S, FOX_HEADS, HEAD_DIM)
    F = jnp.transpose(jnp.cumsum(log_f, axis=1), (0, 2, 1))
    qb = jnp.transpose(q.reshape(B, nb, BLOCK, FOX_HEADS, HEAD_DIM), (1, 0, 2, 3, 4))
    Fb = jnp.transpose(F.reshape(B, FOX_HEADS, nb, BLOCK), (2, 0, 1, 3))
    kpos = jnp.arange(S)

    def block(args):
        qi, Fi, n = args
        s = jnp.einsum('bqhd,bkhd->bhqk', qi, k).astype(jnp.float32) * (HEAD_DIM ** -0.5)
        s = s + Fi[..., :, None] - F[:, :, None, :]
        qpos = n * BLOCK + jnp.arange(BLOCK)
        s = jnp.where((kpos[None, :] <= qpos[:, None])[None, None], s, NEG)
        p = jax.nn.softmax(s, axis=-1)
        return jnp.einsum('bhqk,bkhd->bqhd', p.astype(v.dtype), v)

    out = lax.map(block, (qb, Fb, jnp.arange(nb)))
    return jnp.transpose(out, (1, 0, 2, 3, 4)).reshape(B, S, FOX_WIDTH)

def _peer(h, w_query, sub_keys, expert_down, expert_up):
    B, S, D = h.shape
    ht = h.reshape(-1, PEER_CHUNK, D)

    def chunk(xc):
        T = xc.shape[0]
        q = (xc @ w_query).reshape(T, PEER_HEADS, 2, PEER_HALF)
        s = jnp.einsum('thpd,hpkd->thpk', q, sub_keys).astype(jnp.float32)
        s1, i1 = lax.top_k(s[:, :, 0], PEER_TOPK)
        s2, i2 = lax.top_k(s[:, :, 1], PEER_TOPK)
        cand = (s1[..., :, None] + s2[..., None, :]).reshape(T, PEER_HEADS, PEER_TOPK * PEER_TOPK)
        cidx = (i1[..., :, None] * N_KEYS + i2[..., None, :]).reshape(T, PEER_HEADS, PEER_TOPK * PEER_TOPK)
        top, pos = lax.top_k(cand, PEER_TOPK)
        idx = jnp.take_along_axis(cidx, pos, axis=-1)
        g = jax.nn.softmax(top, axis=-1).astype(xc.dtype)
        u = expert_down[idx]
        act = jax.nn.gelu(jnp.einsum('td,thkd->thk', xc, u), approximate=False)
        vv = expert_up[idx]
        return jnp.einsum('thk,thkd->td', g * act, vv)

    return lax.map(chunk, ht).reshape(B, S, D)

def setup_inputs(seed: int = 0) -> dict:
    key = jax.random.key(seed)
    ks = jax.random.split(key, 20)
    f32 = jnp.float32
    nrm = lambda k, shape, s: jax.random.normal(k, shape, f32) * s
    return {
        "x": nrm(ks[0], (BATCH, SEQ, D_MODEL), 1.0),
        "c": nrm(ks[1], (BATCH, D_MODEL), 1.0),
        "norm_mix_g": 1.0 + nrm(ks[2], (DEPTH, D_MODEL), 0.02),
        "norm_ffn_g": 1.0 + nrm(ks[3], (DEPTH, D_MODEL), 0.02),
        "w_ada": nrm(ks[4], (DEPTH, D_MODEL, N_MOD * D_MODEL), 0.5 * D_MODEL ** -0.5),
        "b_ada": nrm(ks[5], (DEPTH, N_MOD * D_MODEL), 0.02),
        "w_in": nrm(ks[6], (DEPTH, D_MODEL, IN_WIDTH), D_MODEL ** -0.5),
        "b_forget": 2.0 + nrm(ks[7], (DEPTH, FOX_HEADS), 0.5),
        "sinks": nrm(ks[8], (DEPTH, SWA_Q_HEADS), 0.5),
        "w_branch_a": nrm(ks[9], (DEPTH, SWA_WIDTH, D_MODEL), SWA_WIDTH ** -0.5),
        "w_branch_b": nrm(ks[10], (DEPTH, FOX_WIDTH, D_MODEL), FOX_WIDTH ** -0.5),
        "w_out": nrm(ks[11], (DEPTH, D_MODEL, D_MODEL), D_MODEL ** -0.5),
        "rel_bias": nrm(ks[12], (NUM_BUCKETS, SWA_Q_HEADS), 0.5),
        "w_query": nrm(ks[13], (DEPTH, D_MODEL, PEER_HEADS * PEER_QDIM), D_MODEL ** -0.5),
        "sub_keys": nrm(ks[14], (DEPTH, PEER_HEADS, 2, N_KEYS, PEER_HALF), PEER_HALF ** -0.5),
        "expert_down": nrm(ks[15], (DEPTH, N_EXPERTS, D_MODEL), D_MODEL ** -0.5),
        "expert_up": nrm(ks[16], (DEPTH, N_EXPERTS, D_MODEL), 0.3),
        "final_norm_g": 1.0 + nrm(ks[17], (D_MODEL,), 0.02),
    }

def reference(x, c, norm_mix_g, norm_ffn_g, w_ada, b_ada, w_in, b_forget, sinks, w_branch_a,
              w_branch_b, w_out, rel_bias, w_query, sub_keys, expert_down, expert_up, final_norm_g):
    c_act = jax.nn.silu(c)
    for l in range(DEPTH):
        mod = c_act @ w_ada[l] + b_ada[l]
        sh1, sc1, gt1, sh2, sc2, gt2 = jnp.split(mod, N_MOD, axis=-1)

        h = _modulate(_rmsnorm(x, norm_mix_g[l]), sh1, sc1)
        proj = h @ w_in[l]
        qa, ka, va, qb, kb, vb, fl, gla, glb = jnp.split(proj, IN_OFFSETS, axis=-1)
        log_f = jax.nn.log_sigmoid((fl + b_forget[l]).astype(jnp.float32))
        oa = _swa_attention(qa, ka, va, sinks[l], rel_bias)
        ob = _fox_attention(qb, kb, vb, log_f)
        mixed = jax.nn.sigmoid(gla) * (oa @ w_branch_a[l]) + jax.nn.sigmoid(glb) * (ob @ w_branch_b[l])
        x = x + gt1[:, None, :] * (mixed @ w_out[l])

        h2 = _modulate(_rmsnorm(x, norm_ffn_g[l]), sh2, sc2)
        x = x + gt2[:, None, :] * _peer(h2, w_query[l], sub_keys[l], expert_down[l], expert_up[l])
    return _rmsnorm(x, final_norm_g)


_drawn_inputs = setup_inputs


def setup_inputs(seed=0):
    import zlib

    import numpy as np

    out = dict(_drawn_inputs(seed))
    spreads = {}
    factors = {'norm_mix_g': 8.0,
     'norm_ffn_g': 7.541,
     'b_ada': 4.055,
     'b_forget': 2.716,
     'sinks': 104.297,
     'rel_bias': 3.675,
     'final_norm_g': 22.616}
    for name, (base, spread) in spreads.items():
        noise = np.random.default_rng([zlib.crc32(name.encode()), seed]).standard_normal(out[name].shape)
        drawn = base * np.exp(spread * noise) if base else spread * noise
        out[name] = __import__('jax').numpy.asarray(drawn.astype(out[name].dtype))
    for name, factor in factors.items():
        out[name] = (out[name] * factor).astype(out[name].dtype)
    return out
```

```python
from contextlib import ExitStack

import numpy as np

import concourse.bass as bass
from concourse import mybir

F32 = mybir.dt.float32
F32R = mybir.dt.float32r
U32 = mybir.dt.uint32
ALU = mybir.AluOpType
ACT = mybir.ActivationFunctionType
AX = mybir.AxisListType

P = 128
D = 1024
KT = D // P
S = 1024
TT = S // P
HALF = 512
NH = S // HALF
HD = 64
QKV_CHUNKS = 18
FL_COL = 2304
GATE_COL = 2312
FOX_HEADS = 8
PAIRS = 4
WINDOW = 128
BUCKETS = 32
LINE = 384
PEER_HEADS = 8
TOPK = 16
N_KEYS = 128
N_CHUNKS = N_KEYS
EPS = 1e-6
NEG = -1e30
TAKEN = -3e38
SCALE = HD ** -0.5

SBUF_BASE = 16512


def bucket_of_line():
    dist = 255 - np.arange(LINE)
    ok = (dist >= 0) & (dist < WINDOW)
    d = np.clip(dist, 0, None)
    exact = BUCKETS // 2
    large = exact + (np.log(np.maximum(d, 1) / exact) / np.log(128 / exact) * (BUCKETS - exact)).astype(np.int32)
    return np.where(d < exact, d, np.minimum(large, BUCKETS - 1)).astype(np.int32), ok


def line_constants():
    bucket, ok = bucket_of_line()
    c = np.zeros((BUCKETS + 1, LINE), np.float32)
    for m in range(LINE):
        if ok[m]:
            c[bucket[m], m] = 1.0
        else:
            c[BUCKETS, m] = NEG
    return c


class Memory:

    def __init__(self, nc, ctx):
        self.nc, self.ctx = nc, ctx
        self.psum = ctx.enter_context(nc.psum_tensor("psum", [P, 8, HALF], F32))
        self.count = 0

    def at(self, name, shape, kb, dt=F32):
        return self.nc.alloc_sbuf_tensor_at(name, shape, dt, offset=SBUF_BASE + int(kb * 1024))

    def sem(self, name):
        return self.nc.alloc_semaphore(name)

    def stage(self, fn, *args):
        with self.nc.cleanup_on_exit():
            fn(self.nc, self, *args)

    def dram(self, name, shape):
        return self.nc.dram_tensor(name, shape, F32, kind="Internal").ap()


def peeled(eng, first, count, unroll, body):
    for u in range(unroll):
        body(first + u, u)
    with eng.Fori(1, count // unroll) as i:
        for u in range(unroll):
            body(i * unroll + (first + u), u)


def looped(eng, first, count, unroll, body):
    with eng.Fori(0, count // unroll) as i:
        for u in range(unroll):
            body(i * unroll + (first + u), u)


def constants(nc, m, t):
    zeroed = m.sem("const_zeroed")
    made = m.sem("const_made")
    with nc.Block() as block:
        @block.gpsimd
        def _(pool):
            nc.gpsimd.memset(t.ident[:], 0.0).then_inc(zeroed, 1)
            nc.gpsimd.memset(t.mask[:], 0.0).then_inc(zeroed, 1)
            nc.gpsimd.memset(t.ones[:], 1.0).then_inc(zeroed, 1)
            pool.wait_ge(zeroed, 3)
            nc.gpsimd.affine_select(out=t.ident[:], in_=t.ident[:], compare_op=ALU.not_equal, fill=1.0, base=0,
                                    pattern=[[-1, P]], channel_multiplier=1).then_inc(made, 1)
            nc.gpsimd.affine_select(out=t.mask[:], in_=t.mask[:], compare_op=ALU.is_ge, fill=NEG, base=0,
                                    pattern=[[-1, P]], channel_multiplier=1).then_inc(made, 1)
            nc.gpsimd.iota(t.iota[:], pattern=[[1, P]], base=0, channel_multiplier=0,
                           allow_small_or_imprecise_dtypes=True).then_inc(made, 1)
            pool.wait_ge(made, 3)


def modulation(nc, m, t, a):
    w = m.at("mod_w", [P, 2, KT, D], 84)
    acc = m.at("mod_acc", [P, 2, D], 148)
    sig = m.at("mod_sig", [P, KT], 156)
    small = m.sem("mod_small_landed")
    landed = [m.sem(f"mod_w_landed{i}") for i in range(2)]
    act = m.sem("mod_sigmoid")
    silu = m.sem("mod_silu")
    step = m.sem("mod_acc_step")
    summed = m.sem("mod_summed")
    cols = m.sem("mod_cols")
    rows = m.at("mod_rows", [9 * KT, P], 157)
    turned = m.sem("mod_turned")
    columns = m.sem("mod_columns")
    with nc.Block() as block:
        @block.sync
        def _(sp):
            for j in range(2):
                sp.dma_start(w[:, j], a.w_ada[0, :, j * D:(j + 1) * D].rearrange("(k p) n -> p k n", p=P)) \
                    .then_inc(landed[j], 16)

        @block.gpsimd
        def _(pool):
            at = 0
            for src, n in ((a.c, 1), (a.b_ada, 6), (a.norm_mix_g, 1), (a.norm_ffn_g, 1)):
                pool.dma_start(rows[at:at + n * KT, :], src[0].rearrange("(k p) -> k p", p=P)).then_inc(small, 16)
                at += n * KT
            pool.wait_ge(small, 64)

        @block.scalar
        def _(act_e):
            act_e.wait_ge(turned, 1)
            nc.scalar.activation(t.cols[:], m.psum[:, 1, 0:9 * KT], ACT.Copy).then_inc(columns, 1)
            act_e.wait_ge(columns, 1)
            nc.scalar.activation(sig[:], t.ccol[:], ACT.Sigmoid).then_inc(act, 1)

        @block.vector
        def _(dve):
            dve.wait_ge(act, 1)
            nc.vector.tensor_tensor(t.cact[:], t.ccol[:], sig[:], ALU.mult).then_inc(silu, 1)
            dve.wait_ge(silu, 1)
            for k in range(KT):
                for j in range(2):
                    if k == 0:
                        dve.wait_ge(landed[j], 16)
                        nc.vector.tensor_scalar(acc[:, j], w[:, j, k], t.cact[:, k:k + 1], None, ALU.mult) \
                            .then_inc(step, 1)
                    else:
                        dve.wait_ge(step, 2 * k - 1 + j)
                        nc.vector.scalar_tensor_tensor(out=acc[:, j], in0=w[:, j, k], scalar=t.cact[:, k:k + 1],
                                                       in1=acc[:, j], op0=ALU.mult, op1=ALU.add).then_inc(step, 1)
            dve.wait_ge(summed, 1)
            nc.vector.tensor_tensor(t.shift[:, 0], m.psum[:, 0, 0:KT], t.bcol[:, 0:KT], ALU.add).then_inc(cols, 1)
            nc.vector.tensor_tensor(t.gain[:, 0], m.psum[:, 0, KT:2 * KT], t.bcol[:, KT:2 * KT], ALU.add) \
                .then_inc(cols, 1)
            dve.wait_ge(cols, 2)
            nc.vector.scalar_tensor_tensor(out=t.gain[:, 0], in0=t.gain[:, 0], scalar=1.0, in1=t.gcol[:, 0],
                                           op0=ALU.add, op1=ALU.mult).then_inc(cols, 1)

        @block.tensor
        def _(pe):
            pe.wait_ge(small, 64)
            nc.tensor.transpose(m.psum[:, 1, 0:9 * KT], rows[:], t.ident[0:9 * KT, 0:9 * KT]).then_inc(turned, 1)
            pe.wait_ge(step, 2 * KT)
            for j in range(2):
                for k in range(KT):
                    mm = nc.tensor.matmul(m.psum[:, 0, j * KT + k:j * KT + k + 1], acc[:, j, k * P:(k + 1) * P],
                                          t.ones[:, 0:1], start=True, stop=True)
            mm.then_inc(summed, 1)


def norm(nc, m, t, which, src):
    n = f"n{which}_"
    GRP = 4
    xin = m.at(n + "x", [P, GRP, D], 84)
    xn = m.at(n + "xn", [P, GRP, D], 100)
    junk = m.at(n + "junk", [P, 2, D], 116)
    full = m.at(n + "full", [P, 2, HALF], 124)
    ssq = m.at(n + "ssq", [P, TT], 129)
    std = m.at(n + "std", [P, TT], 130)
    rstd = m.at(n + "rstd", [P, TT], 131)
    landed = [m.sem(f"{n}landed{i}") for i in range(GRP)]
    squared = m.sem(n + "squared")
    mean = m.sem(n + "mean")
    root = m.sem(n + "root")
    inv = m.sem(n + "inv")
    scaled = m.sem(n + "scaled")
    turned = m.sem(n + "turned")
    affine = m.sem(n + "affine")
    hi = m.sem(n + "hi")
    lo = m.sem(n + "lo")
    with nc.Block() as block:
        @block.sync
        def _(sp):
            for i in range(TT):
                if i >= GRP:
                    sp.wait_ge(scaled, i - GRP + 1)
                sp.dma_start(xin[:, i % GRP], src[i * P:(i + 1) * P, :]).then_inc(landed[i % GRP], 16)

        @block.scalar
        def _(act):
            for g in range(NH):
                for i in range(GRP * g, GRP * g + GRP):
                    act.wait_ge(landed[i % GRP], 16 * (i // GRP + 1))
                    if i >= 2:
                        act.wait_ge(squared, i - 1)
                    nc.scalar.activation(junk[:, i % 2], xin[:, i % GRP], ACT.Square,
                                         accum_out=ssq[:, i:i + 1]).then_inc(squared, 1)
                act.wait_ge(mean, g + 1)
                nc.scalar.activation(std[:, GRP * g:GRP * g + GRP], ssq[:, GRP * g:GRP * g + GRP], ACT.Sqrt) \
                    .then_inc(root, 1)
                for k in range(KT):
                    u = g * KT + k
                    act.wait_ge(affine, u + 1)
                    nc.scalar.activation(t.hT_hi[:, k, g * HALF:(g + 1) * HALF], full[:, u % 2], ACT.Copy) \
                        .then_inc(hi, 1)

        @block.vector
        def _(dve):
            for g in range(NH):
                cols = slice(GRP * g, GRP * g + GRP)
                dve.wait_ge(squared, GRP * (g + 1))
                nc.vector.tensor_scalar(ssq[:, cols], ssq[:, cols], 1.0 / D, EPS, ALU.mult, ALU.add) \
                    .then_inc(mean, 1)
                dve.wait_ge(root, g + 1)
                nc.vector.reciprocal(rstd[:, cols], std[:, cols]).then_inc(inv, 1)
                dve.wait_ge(inv, g + 1)
                if g >= 1:
                    dve.wait_ge(turned, KT * g)
                for i in range(GRP * g, GRP * g + GRP):
                    nc.vector.tensor_scalar(xn[:, i % GRP], xin[:, i % GRP], rstd[:, i:i + 1], None, ALU.mult) \
                        .then_inc(scaled, 1)
                for k in range(KT):
                    u = g * KT + k
                    dve.wait_ge(turned, u + 1)
                    if u >= 2:
                        dve.wait_ge(lo, u - 1)
                    nc.vector.tensor_scalar(full[:, u % 2], m.psum[:, u % 4], t.gain[:, which, k:k + 1],
                                            t.shift[:, which, k:k + 1], ALU.mult, ALU.add).then_inc(affine, 1)

        @block.gpsimd
        def _(pool):
            for g in range(NH):
                for k in range(KT):
                    u = g * KT + k
                    pool.wait_ge(hi, u + 1)
                    cols = slice(g * HALF, (g + 1) * HALF)
                    nc.gpsimd.tensor_tensor(t.hT_lo[:, k, cols], full[:, u % 2],
                                            t.hT_hi[:, k, cols].bitcast(F32), ALU.subtract).then_inc(lo, 1)

        @block.tensor
        def _(pe):
            for g in range(NH):
                pe.wait_ge(scaled, GRP * (g + 1))
                for k in range(KT):
                    u = g * KT + k
                    if u >= 4:
                        pe.wait_ge(affine, u - 3)
                    for i in range(GRP):
                        mm = nc.tensor.transpose(m.psum[:, u % 4, i * P:(i + 1) * P],
                                                 xn[:, i, k * P:(k + 1) * P], t.ident[:])
                    mm.then_inc(turned, 1)


def three_pass(nc, out, l_hi, l_lo, r_hi, r_lo, steps):
    for k in range(steps):
        nc.tensor.matmul(out, l_hi(k), r_hi(k), start=k == 0, stop=False)
        nc.tensor.matmul(out, l_hi(k), r_lo(k), start=False, stop=False)
        mm = nc.tensor.matmul(out, l_lo(k), r_hi(k), start=False, stop=k == steps - 1)
    return mm


def projections(nc, m, t, a):
    raw = m.at("pw_raw", [P, 2, KT, P], 156)
    w_hi = m.at("pw_hi", [P, 2, KT, P], 164, F32R)
    w_lo = m.at("pw_lo", [P, 2, KT, P], 172, F32R)
    adaw = m.at("p_adaw", [P, 2, D], 180)
    acc = [t.gate1, m.at("p_acc_shift", [P, D], 188), m.at("p_acc_scale", [P, D], 192), t.gate2]
    sg = m.at("p_sigmoid", [P, 2, D], 196)
    tmp = m.at("p_adatmp", [P, 896], 204)
    fl = m.at("p_fl", [FOX_HEADS, D], 188)
    fe = m.at("p_fe", [FOX_HEADS, D], 192)
    bfl = t.bfl
    landed = [m.sem(f"p_w_landed{i}") for i in range(2)]
    hi = m.sem("p_hi")
    lo = m.sem("p_lo")
    done = m.sem("p_done")
    out = m.sem("p_out")
    stored = [m.sem(f"p_stored{i}") for i in range(2)]
    ada_landed = [m.sem(f"p_ada_landed{i}") for i in range(2)]
    weighed = m.sem("p_weighed")
    added = m.sem("p_added")
    summed = m.sem("p_summed")
    taken = m.sem("p_taken")
    small = m.sem("p_small")
    fx = m.sem("p_forget_act")
    fv = m.sem("p_forget_dve")
    MODS = 4
    NQ, NG = QKV_CHUNKS, 2 * KT
    FL = NQ + NG
    PART = 512

    with nc.Block() as block:
        @block.sync
        def _(sp):
            w_q = a.w_in[0, :, 0:NQ * P].rearrange("(k p) (c n) -> c p k n", p=P, n=P)
            w_g = a.w_in[0, :, GATE_COL:GATE_COL + NG * P].rearrange("(k p) (c n) -> c p k n", p=P, n=P)

            def load_q(g, u):
                if isinstance(g, int):
                    pass
                else:
                    sp.wait_ge(lo, g - 1)
                sp.dma_start(raw[:, u], w_q[g]).then_inc(landed[u], 16)

            def load_g(g, u):
                sp.wait_ge(lo, g - 1)
                sp.dma_start(raw[:, u], w_g[g - NQ]).then_inc(landed[u], 16)

            peeled(sp, 0, NQ, 2, load_q)
            looped(sp, NQ, NG, 2, load_g)
            sp.wait_ge(lo, FL - 1)
            sp.dma_start(raw[:, 0, :, 0:FOX_HEADS],
                         a.w_in[0, :, FL_COL:FL_COL + FOX_HEADS].rearrange("(k p) n -> p k n", p=P)) \
                .then_inc(landed[0], 16)

        @block.scalar
        def _(act):
            def split(g, u, n=P):
                act.wait_ge(landed[u], (g - u) * 8 + 16)
                if not (isinstance(g, int) and g < 2):
                    act.wait_ge(done, g - 1)
                nc.scalar.activation(w_hi[:, u, :, 0:n], raw[:, u, :, 0:n], ACT.Copy).then_inc(hi, 1)

            def q_step(g, u):
                split(g + 1, 1 - u)
                act.wait_ge(done, g + 1)
                nc.scalar.activation(t.qkvT[:, g], m.psum[:, 2 * u:2 * u + 2], ACT.Copy).then_inc(out, 1)

            def g_step(g, u, last=False):
                if not last:
                    split(g + 1, 1 - u)
                act.wait_ge(done, g + 1)
                if not (isinstance(g, int) and g < NQ + 2):
                    act.wait_ge(stored[u], (g - u - NQ) * 8)
                nc.scalar.activation(sg[:, u], m.psum[:, 2 * u:2 * u + 2], ACT.Sigmoid).then_inc(out, 1)
                act.wait_ge(out, g + 1)
                act.dma_start(t.gates[g - NQ], sg[:, u]).then_inc(stored[u], 16)

            split(0, 0)
            peeled(act, 0, NQ, 2, q_step)
            g_step(NQ, 0)
            g_step(NQ + 1, 1)
            with act.Fori(1, NG // 2 - 1) as i:
                for u in range(2):
                    g_step(i * 2 + (NQ + u), u)
            g_step(FL - 2, 0)
            g_step(FL - 1, 1, last=True)
            split(FL, 0, FOX_HEADS)
            act.wait_ge(fv, 1)
            nc.scalar.activation(fe[:], fl[:], ACT.Abs).then_inc(fx, 1)
            act.wait_ge(fx, 1)
            nc.scalar.activation(fe[:], fe[:], ACT.Exp, scale=-1.0).then_inc(fx, 1)
            act.wait_ge(fx, 2)
            nc.scalar.activation(fe[:], fe[:], ACT.Ln, bias=1.0).then_inc(fx, 1)
            for u in range(2):
                act.wait_ge(stored[u], NG * 8)

        @block.vector
        def _(dve):
            def rest(g, u, n=P):
                dve.wait_ge(hi, g + 1)
                nc.vector.tensor_tensor(w_lo[:, u, :, 0:n], raw[:, u, :, 0:n], w_hi[:, u, :, 0:n].bitcast(F32),
                                        ALU.subtract).then_inc(lo, 1)
            looped(dve, 0, FL, 2, rest)
            rest(FL, 0, FOX_HEADS)
            dve.wait_ge(summed, 1)
            nc.vector.tensor_tensor(t.shift[:, 1], m.psum[:, 4, 0:KT], t.bcol[:, 3 * KT:4 * KT], ALU.add) \
                .then_inc(taken, 1)
            nc.vector.tensor_tensor(t.gain[:, 1], m.psum[:, 4, KT:2 * KT], t.bcol[:, 4 * KT:5 * KT], ALU.add) \
                .then_inc(taken, 1)
            dve.wait_ge(taken, 2)
            nc.vector.scalar_tensor_tensor(out=t.gain[:, 1], in0=t.gain[:, 1], scalar=1.0, in1=t.gcol[:, 1],
                                           op0=ALU.add, op1=ALU.mult).then_inc(taken, 1)
            dve.wait_ge(small, 48)
            dve.wait_ge(summed, 2)
            nc.vector.tensor_tensor(t.gate1[:], adaw[:, 0], m.psum[:, 5:7], ALU.add).then_inc(taken, 1)
            dve.wait_ge(taken, 4)
            dve.wait_ge(summed, 3)
            nc.vector.tensor_tensor(t.gate2[:], adaw[:, 1], m.psum[:, 5:7], ALU.add).then_inc(taken, 1)
            dve.wait_ge(done, FL + 1)
            z = m.psum[0:FOX_HEADS, 0:2]
            nc.vector.tensor_scalar(fl[:], z, bfl[:, 0:1], None, ALU.add).then_inc(fv, 1)
            dve.wait_ge(fv, 1)
            dve.wait_ge(fx, 1)
            nc.vector.tensor_scalar(fl[:], fl[:], -1.0, 0.0, ALU.mult, ALU.max).then_inc(fv, 1)
            dve.wait_ge(fv, 2)
            dve.wait_ge(fx, 3)
            nc.vector.tensor_tensor(fe[:], fe[:], fl[:], ALU.add).then_inc(fv, 1)
            dve.wait_ge(fv, 3)
            nc.vector.memset(fl[:], 1.0).then_inc(fv, 1)
            dve.wait_ge(fv, 4)
            nc.vector.tensor_tensor_scan(t.negF[:], fl[:], fe[:], 0.0, ALU.mult, ALU.add).then_inc(fv, 1)

        @block.gpsimd
        def _(pool):
            order = [2, 3, 4, 5]
            pool.dma_start(bfl[:, 0:1], a.b_forget.rearrange("a h -> h a")).then_inc(small, 16)

            def load(n):
                j, k = divmod(n, KT)
                pool.dma_start(adaw[:, n % 2], a.w_ada[0, k * P:(k + 1) * P, order[j] * D:(order[j] + 1) * D]) \
                    .then_inc(ada_landed[n % 2], 16)
            load(0)
            steps = 0
            for n in range(MODS * KT):
                j, k = divmod(n, KT)
                if n + 1 < MODS * KT:
                    if n >= 1:
                        pool.wait_ge(weighed, 2 * n)
                    load(n + 1)
                pool.wait_ge(ada_landed[n % 2], 16 * (n // 2 + 1))
                for h in range(2):
                    cols = slice(h * PART, (h + 1) * PART)
                    if k == 0:
                        nc.gpsimd.tensor_scalar(acc[j][:, cols], adaw[:, n % 2, cols], t.cact[:, k:k + 1], None,
                                                ALU.mult).then_inc(weighed, 1)
                        continue
                    if steps >= 1:
                        pool.wait_ge(added, steps)
                    nc.gpsimd.tensor_scalar(tmp[:, 0:PART], adaw[:, n % 2, cols], t.cact[:, k:k + 1], None,
                                            ALU.mult).then_inc(weighed, 1)
                    pool.wait_ge(weighed, 2 * n + h + 1)
                    nc.gpsimd.tensor_tensor(acc[j][:, cols], acc[j][:, cols], tmp[:, 0:PART], ALU.add) \
                        .then_inc(added, 1)
                    steps += 1
            pool.wait_ge(weighed, 2 * MODS * KT)
            for s, j in ((0, 2), (1, 5)):
                pool.dma_start(adaw[:, s], a.b_ada[:, j * D:(j + 1) * D].partition_broadcast(P)) \
                    .then_inc(small, 16)
            pool.wait_ge(small, 48)

        @block.tensor
        def _(pe):
            def chunk(g, u, n=P):
                pe.wait_ge(lo, g + 1)
                if not (isinstance(g, int) and g < 2):
                    pe.wait_ge(out, g - 1)
                for h in range(NH):
                    cols = slice(h * HALF, (h + 1) * HALF)
                    mm = three_pass(nc, m.psum[0:n, 2 * u + h], lambda k: w_hi[:, u, k, 0:n],
                                    lambda k: w_lo[:, u, k, 0:n], lambda k: t.hT_hi[:, k, cols],
                                    lambda k: t.hT_lo[:, k, cols], KT)
                mm.then_inc(done, 1)
            peeled(pe, 0, FL, 2, chunk)
            chunk(FL, 0, FOX_HEADS)
            pe.wait_ge(weighed, 2 * MODS * KT)
            pe.wait_ge(added, 2 * MODS * (KT - 1))
            for j in range(2):
                for k in range(KT):
                    mm = nc.tensor.matmul(m.psum[:, 4, j * KT + k:j * KT + k + 1],
                                          acc[1 + j][:, k * P:(k + 1) * P], t.ones[:, 0:1], start=True, stop=True)
            mm.then_inc(summed, 1)
            for n, gate in enumerate((t.gate1, t.gate2)):
                if n:
                    pe.wait_ge(taken, 4)
                for h in range(2):
                    mm = nc.tensor.matmul(m.psum[:, 5 + h], t.ones[:], gate[:, h * HALF:(h + 1) * HALF],
                                          start=True, stop=True)
                mm.then_inc(summed, 1)


def values(nc, m, t, a):
    pick = m.at("v_pick", [BUCKETS, LINE], 178)
    outside = m.at("v_outside", [FOX_HEADS, LINE], 180)
    rel = m.at("v_rel", [BUCKETS, FOX_HEADS], 182)
    line = m.at("v_line", [FOX_HEADS, LINE], 183)
    small = m.sem("v_small")
    turned = m.sem("v_turned")
    copied = m.sem("v_copied")
    lined = m.sem("v_lined")
    linec = m.sem("v_line_copied")
    wrote = m.sem("v_line_written")
    bands = m.sem("v_bands")
    vchunks = [5, 14, 15, 16, 17]
    with nc.Block() as block:
        @block.sync
        def _(sp):
            sp.dma_start(pick[:], a.line_const[0:BUCKETS, :]).then_inc(small, 16)
            sp.dma_start(outside[:], a.line_const[BUCKETS:BUCKETS + 1, :].partition_broadcast(FOX_HEADS)) \
                .then_inc(small, 16)
            sp.dma_start(rel[:], a.rel_bias).then_inc(small, 16)
            for g in range(2):
                for half in range(2):
                    sp.dma_start(t.kdup[half * HD:(half + 1) * HD, g], t.qkvT[g * HD:(g + 1) * HD, 4]) \
                        .then_inc(bands, 16)
            sp.dma_start(t.negsink[:], a.sinks.partition_broadcast(P)).then_inc(bands, 16)
            sp.wait_ge(linec, 1)
            sp.dma_start(t.line_dram, line[:].unsqueeze(1).to_broadcast([FOX_HEADS, P, LINE])).then_inc(wrote, 16)
            sp.wait_ge(wrote, 16)
            for h in range(FOX_HEADS):
                src = bass.AP(t.line_dram.tensor, h * P * LINE + P - 1, [[LINE - 1, P], [1, 2 * P]])
                sp.dma_start(t.band[:, h], src).then_inc(bands, 16)
            sp.wait_ge(bands, 16 * (5 + FOX_HEADS))

        @block.tensor
        def _(pe):
            pe.wait_ge(small, 48)
            nc.tensor.matmul(m.psum[0:FOX_HEADS, 7, 0:LINE], rel[:], pick[:], start=True, stop=True) \
                .then_inc(lined, 1)
            for n, c in enumerate(vchunks):
                for q in range(2):
                    u = 2 * n + q
                    if u >= 4:
                        pe.wait_ge(copied, u - 3)
                    for i in range(4):
                        mm = nc.tensor.transpose(m.psum[:, u % 4, i * P:(i + 1) * P],
                                                 t.qkvT[:, c, (4 * q + i) * P:(4 * q + i + 1) * P], t.ident[:])
                    mm.then_inc(turned, 1)

        @block.vector
        def _(dve):
            dve.wait_ge(lined, 1)
            dve.wait_ge(small, 48)
            nc.vector.tensor_tensor(line[:], m.psum[0:FOX_HEADS, 7, 0:LINE], outside[:], ALU.add) \
                .then_inc(linec, 1)
            for n in range(len(vchunks)):
                for q in range(2):
                    u = 2 * n + q
                    dve.wait_ge(turned, u + 1)
                    nc.vector.tensor_copy(t.v[:, 4 * q:4 * q + 4, n * P:(n + 1) * P],
                                          m.psum[:, u % 4].rearrange("p (i c) -> p i c", c=P)).then_inc(copied, 1)
            dve.wait_ge(bands, 16 * (5 + FOX_HEADS))
            nc.vector.tensor_scalar(t.negsink[:], t.negsink[:], -1.0, None, ALU.mult).then_inc(copied, 1)


def hold(eng, t):
    eng.sem_inc(t.passed, 1)


def attention(nc, m, t):
    JOBS = [(br, par, n) for br in (0, 1) for par in (0, 1) for n in range(TT)]
    NJ = len(JOBS)
    q_st = m.at("at_q", [P, 2, S], 52)
    k_st = m.at("at_k", [P, 2, S], 60)
    nf = m.at("at_negF", [P, 2, S], 176)
    sc = m.at("at_scores", [P, 2, S], 184)
    pT = m.at("at_pT", [P, 2, S], 192)
    b_st = m.at("at_band", [P, 2, 2 * P], 200)
    mx = m.at("at_max", [P, NJ], 202)
    nm = m.at("at_negmax", [P, NJ], 202.25)
    rs = m.at("at_rowsum", [P, NJ], 202.5)
    se = m.at("at_sinkexp", [P, NJ], 202.75)
    dn = m.at("at_denominator", [P, NJ], 203)
    rc = m.at("at_reciprocal", [P, NJ], 203.25)
    flat = m.psum[:].rearrange("p b n -> p (b n)")
    q_ready = m.sem("at_staged_q")
    k_ready = m.sem("at_staged_k")
    negf_out = m.sem("at_negF_out")
    negf_in = [m.sem(f"at_negF_in{i}") for i in range(2)]
    scored = m.sem("at_scored")
    maxed = m.sem("at_maxed")
    negated = m.sem("at_negated")
    expd = m.sem("at_exp")
    sunk = m.sem("at_sink_exp")
    turned = m.sem("at_turned")
    copied_a = m.sem("at_copied_act")
    copied_v = m.sem("at_copied_dve")
    weighted = m.sem("at_weighted")
    dens = m.sem("at_denominators")
    inv = m.sem("at_inverted")
    normed = m.sem("at_normed")

    def keys(job):
        br, par, n = job
        return list(range(0 if br == 0 else max(n - 1, 0), n + 1))

    groups = [[keys(j)[x:x + 4] for x in range(0, len(keys(j)), 4)] for j in JOBS]
    before = [sum(len(g) for g in groups[:j]) for j in range(NJ + 1)]
    NGR = before[NJ]
    assert NGR % 2 == 0
    NC = NGR // 2
    NS = sum(1 for j in JOBS if j[0] == 1)
    LIVE = 2

    def copies(eng, copy, mine, sem, i, j):
        for x, grp in enumerate(groups[j]):
            G = before[j] + x
            if G % 2 != mine:
                continue
            after(eng, turned, i * NGR + (G + 1))
            if j >= LIVE:
                after(eng, weighted, i * NJ + (j - 1))
            w = len(grp) * P
            copy(pT[:, j % 2, x * HALF:x * HALF + w], flat[:, (4 + G % 2) * HALF:(4 + G % 2) * HALF + w]) \
                .then_inc(sem, 1)

    def after(eng, sem, count):
        eng.wait_ge(sem, count + 1)

    with nc.Block() as block:
        @block.sync
        def _(sp):
            sp.dma_start(t.negf_dram, t.negF[:]).then_inc(negf_out, 16)
            sp.wait_ge(negf_out, 16)
            with sp.Fori(0, PAIRS) as i:
                for par in range(2):
                    after(sp, maxed, i * NJ)
                    sp.dma_start(nf[:, par], t.negf_dram[i * 2 + par:i * 2 + (par + 1), :].partition_broadcast(P)
                                 if isinstance(i, int) else
                                 t.negf_dram[bass.ds(i * 2 + par, 1), :].partition_broadcast(P)) \
                        .then_inc(negf_in[par], 16)

        @block.gpsimd
        def _(pool):
            with pool.Fori(0, PAIRS) as i:
                after(pool, scored, i * NJ)
                hold(pool, t)
                nc.gpsimd.tensor_copy(k_st[:, 0], t.qkvT[:, i + 10]).then_inc(k_ready, 1)
                nc.gpsimd.tensor_copy(k_st[:, 1], t.kdup[:, i // 2]).then_inc(k_ready, 1)
                after(pool, maxed, i * NJ)
                hold(pool, t)
                for par in range(2):
                    nc.gpsimd.tensor_copy(b_st[:, par], t.band[:, i * 2 + par]).then_inc(k_ready, 1)

        @block.tensor
        def _(pe):
            for sem in (scored, turned, weighted):
                pe.sem_inc(sem, 1)
            with pe.Fori(0, PAIRS) as i:
                def score(j):
                    br, par, n = JOBS[j]
                    rows = slice(par * HD, (par + 1) * HD)
                    if j == 0:
                        pe.wait_ge(q_ready, i * 2 + 2)
                        pe.wait_ge(k_ready, i * 4 + 2)
                    after(pe, maxed, i * NJ + max(j - 1, 0))
                    ks = keys(JOBS[j])
                    k0, w = ks[0] * P, len(ks) * P
                    for h in range(0, w, HALF):
                        x = min(HALF, w - h)
                        diag = h + x == w and br == 0
                        o = (2 * (j % 2)) * HALF + h
                        mm = nc.tensor.matmul(flat[:, o:o + x], q_st[rows, br, n * P:(n + 1) * P],
                                              k_st[rows, br, k0 + h:k0 + h + x], start=True, stop=not diag)
                        if diag:
                            mm = nc.tensor.matmul(flat[:, o + x - P:o + x], t.ident[:], t.mask[:],
                                                  start=False, stop=True)
                    mm.then_inc(scored, 1)

                def turn(j):
                    pe.wait_ge(expd, i * NJ + (j + 1))
                    k0 = keys(JOBS[j])[0]
                    for x, grp in enumerate(groups[j]):
                        G = before[j] + x
                        after(pe, copied_v if G % 2 else copied_a, i * NC + G // 2)
                        for y, kt in enumerate(grp):
                            o = (4 + G % 2) * HALF + y * P
                            mm = nc.tensor.transpose(flat[:, o:o + P],
                                                     sc[:, j % 2, (kt - k0) * P:(kt - k0 + 1) * P], t.ident[:])
                        mm.then_inc(turned, 1)

                def weigh(j):
                    br, par, n = JOBS[j]
                    G = before[j + 1]
                    after(pe, copied_a, i * NC + (G + 1) // 2)
                    after(pe, copied_v, i * NC + G // 2)
                    after(pe, normed, i * NJ + max(j - 1, 0))
                    ks = keys(JOBS[j])
                    for y, kt in enumerate(ks):
                        col = i * P + (P + par * HD) if br == 0 else (i // 2) * HD
                        mm = nc.tensor.matmul(m.psum[:, 6 + j % 2, 0:HD], pT[:, j % 2, y * P:(y + 1) * P],
                                              t.v[:, kt, bass.ds(col, HD)], start=y == 0, stop=y == len(ks) - 1)
                    mm.then_inc(weighted, 1)

                for j in range(NJ + 2):
                    if j < NJ:
                        score(j)
                    if 1 <= j <= NJ:
                        turn(j - 1)
                    if j >= 2:
                        weigh(j - 2)

        @block.scalar
        def _(act):
            act.sem_inc(copied_a, 1)
            with act.Fori(0, PAIRS) as i:
                after(act, scored, i * NJ)
                hold(act, t)
                nc.scalar.activation(q_st[:, 0], t.qkvT[:, i + 6], ACT.Copy, scale=SCALE).then_inc(q_ready, 1)
                nc.scalar.activation(q_st[:, 1], t.qkvT[:, i], ACT.Copy, scale=SCALE).then_inc(q_ready, 1)
                for j in range(NJ + 1):
                    if j < NJ:
                        br, par, n = JOBS[j]
                        w = len(keys(JOBS[j])) * P
                        act.wait_ge(negated, i * NJ + (j + 1))
                        nc.scalar.activation(sc[:, j % 2, 0:w], sc[:, j % 2, 0:w], ACT.Exp,
                                             bias=nm[:, j:j + 1], accum_out=rs[:, j:j + 1]).then_inc(expd, 1)
                        if br == 1:
                            nc.scalar.activation(se[:, j:j + 1], t.negsink[:, bass.ds(i * 2 + par, 1)], ACT.Exp,
                                                 bias=nm[:, j:j + 1], scale=-1.0).then_inc(sunk, 1)
                    if j >= 1:
                        copies(act, lambda o, x: nc.scalar.activation(o, x, ACT.Copy), 0, copied_a, i, j - 1)

        @block.vector
        def _(dve):
            for sem in (maxed, copied_v, normed):
                dve.sem_inc(sem, 1)
            with dve.Fori(0, PAIRS) as i:
                def maximum(j):
                    br, par, n = JOBS[j]
                    w = len(keys(JOBS[j])) * P
                    if br == 0 and n == 0:
                        dve.wait_ge(negf_in[par], i * 16 + 16)
                    if j == NJ - NS:
                        dve.wait_ge(k_ready, i * 4 + 4)
                    after(dve, turned, i * NGR + before[max(j - 1, 0)])
                    after(dve, scored, i * NJ + (j + 1))
                    hold(dve, t)
                    bias = nf[:, par, 0:w] if br == 0 else b_st[:, par, 2 * P - w:2 * P]
                    nc.vector.tensor_tensor_reduce(sc[:, j % 2, 0:w], flat[:, 2 * (j % 2) * HALF:][:, 0:w], bias,
                                                   1.0, -3e38, ALU.add, ALU.max, mx[:, j:j + 1]).then_inc(maxed, 1)
                    after(dve, maxed, i * NJ + (j + 1))
                    if br == 0:
                        nc.vector.tensor_scalar(nm[:, j:j + 1], mx[:, j:j + 1], -1.0, None, ALU.mult) \
                            .then_inc(negated, 1)
                    else:
                        nc.vector.tensor_scalar(nm[:, j:j + 1], mx[:, j:j + 1], -1.0,
                                                t.negsink[:, bass.ds(i * 2 + par, 1)], ALU.mult, ALU.min) \
                            .then_inc(negated, 1)

                def divide(j):
                    br, par, n = JOBS[j]
                    dve.wait_ge(expd, i * NJ + (j + 1))
                    den = rs
                    if br == 1:
                        w = j - (NJ - NS)
                        dve.wait_ge(sunk, i * NS + (w + 1))
                        nc.vector.tensor_tensor(dn[:, j:j + 1], rs[:, j:j + 1], se[:, j:j + 1], ALU.add) \
                            .then_inc(dens, 1)
                        dve.wait_ge(dens, i * NS + (w + 1))
                        den = dn
                    nc.vector.reciprocal(rc[:, j:j + 1], den[:, j:j + 1]).then_inc(inv, 1)
                    dve.wait_ge(inv, i * NJ + (j + 1))
                    after(dve, weighted, i * NJ + (j + 1))
                    nc.vector.tensor_scalar(t.o[:, 1 - br, n, bass.ds(i * P + par * HD, HD)],
                                            m.psum[:, 6 + j % 2, 0:HD], rc[:, j:j + 1], None, ALU.mult) \
                        .then_inc(normed, 1)

                for j in range(NJ + 2):
                    if j < NJ:
                        maximum(j)
                    if 1 <= j <= NJ:
                        copies(dve, nc.vector.tensor_copy, 1, copied_v, i, j - 1)
                    if j >= 2:
                        divide(j - 2)


def mixing(nc, m, t, a):
    KB = 4
    oT_hi = m.at("mx_oT_hi", [P, 2 * KB, S], 52, F32R)
    oT_lo = m.at("mx_oT_lo", [P, 2 * KB, S], 84, F32R)
    raw = m.at("mx_raw", [P, 2, 2 * KB, P], 180)
    w_hi = m.at("mx_w_hi", [P, 2, 2 * KB, P], 188, F32R)
    w_lo = m.at("mx_w_lo", [P, 2, 2 * KB, P], 196, F32R)
    gate = m.at("mx_gate", [P, 2, 2, S], 20)
    part = m.at("mx_part", [P, 2, S], 36)
    mix = m.at("mx_sum", [P, 2, S], 44)
    landed = [m.sem(f"mx_w_landed{i}") for i in range(2)]
    gated = [m.sem(f"mx_gate_landed{i}") for i in range(2)]
    turned = m.sem("mx_turned")
    o_hi = m.sem("mx_o_hi")
    o_lo = m.sem("mx_o_lo")
    hi = m.sem("mx_hi")
    lo = m.sem("mx_lo")
    done = m.sem("mx_done")
    scaled = m.sem("mx_scaled")
    summed = m.sem("mx_summed")
    m_hi = m.sem("mx_m_hi")
    m_lo = m.sem("mx_m_lo")
    UNITS = 2 * KB * NH
    with nc.Block() as block:
        @block.sync
        def _(sp):
            w_a = a.w_branch_a[0].rearrange("(k p) (c n) -> c p k n", p=P, n=P)
            w_b = a.w_branch_b[0].rearrange("(k p) (c n) -> c p k n", p=P, n=P)

            def load(g, u):
                if not isinstance(g, int):
                    sp.wait_ge(lo, g - 1)
                sp.dma_start(raw[:, u, 0:KB], w_a[g]).then_inc(landed[u], 16)
                sp.dma_start(raw[:, u, KB:2 * KB], w_b[g]).then_inc(landed[u], 16)
                if isinstance(g, int):
                    if g == 0:
                        sp.wait_ge(turned, UNITS)
                else:
                    sp.wait_ge(scaled, g * 2 - 2)
                sp.dma_start(gate[:, u, 0], t.gates[g]).then_inc(gated[u], 16)
                sp.dma_start(gate[:, u, 1], t.gates[g + KT]).then_inc(gated[u], 16)
            peeled(sp, 0, KT, 2, load)

        @block.tensor
        def _(pe):
            for x in range(UNITS):
                c, h = divmod(x, NH)
                if x >= 8:
                    pe.wait_ge(o_lo, x - 7)
                for i in range(4):
                    mm = nc.tensor.transpose(m.psum[:, x % 8, i * P:(i + 1) * P],
                                             t.o[:, c // KB, 4 * h + i, (c % KB) * P:(c % KB + 1) * P], t.ident[:])
                mm.then_inc(turned, 1)
            pe.wait_ge(o_lo, UNITS)

            def chunk(g, u):
                pe.wait_ge(lo, g + 1)
                if not (isinstance(g, int) and g < 2):
                    pe.wait_ge(scaled, g * 2 - 2)
                for br in range(2):
                    for h in range(NH):
                        cols = slice(h * HALF, (h + 1) * HALF)
                        mm = three_pass(nc, m.psum[:, 4 * u + 2 * br + h],
                                        lambda k: w_hi[:, u, br * KB + k], lambda k: w_lo[:, u, br * KB + k],
                                        lambda k: oT_hi[:, br * KB + k, cols],
                                        lambda k: oT_lo[:, br * KB + k, cols], KB)
                mm.then_inc(done, 1)
            peeled(pe, 0, KT, 2, chunk)

        @block.scalar
        def _(act):
            for x in range(UNITS):
                c, h = divmod(x, NH)
                act.wait_ge(turned, x + 1)
                nc.scalar.activation(oT_hi[:, c, h * HALF:(h + 1) * HALF], m.psum[:, x % 8], ACT.Copy) \
                    .then_inc(o_hi, 1)

            def split(g, u):
                act.wait_ge(landed[u], (g - u) * 16 + 32)
                if not (isinstance(g, int) and g < 2):
                    act.wait_ge(done, g - 1)
                nc.scalar.activation(w_hi[:, u], raw[:, u], ACT.Copy).then_inc(hi, 1)

            def step(g, u, last=False):
                if not last:
                    split(g + 1, 1 - u)
                act.wait_ge(summed, g + 1)
                hold(act, t)
                nc.scalar.activation(t.mixT_hi[:, g], mix[:, u], ACT.Copy).then_inc(m_hi, 1)
            split(0, 0)
            step(0, 0)
            step(1, 1)
            with act.Fori(1, KT // 2 - 1) as i:
                for u in range(2):
                    step(i * 2 + u, u)
            step(KT - 2, 0)
            step(KT - 1, 1, last=True)

        @block.vector
        def _(dve):
            for x in range(UNITS):
                c, h = divmod(x, NH)
                cols = slice(h * HALF, (h + 1) * HALF)
                dve.wait_ge(o_hi, x + 1)
                nc.vector.tensor_tensor(oT_lo[:, c, cols], m.psum[:, x % 8], oT_hi[:, c, cols].bitcast(F32),
                                        ALU.subtract).then_inc(o_lo, 1)

            def step(g, u):
                dve.wait_ge(done, g + 1)
                dve.wait_ge(gated[u], (g - u) * 16 + 32)
                for br in range(2):
                    if not (isinstance(g, int) and g == 0):
                        dve.wait_ge(summed, g)
                    b = 4 * u + 2 * br
                    nc.vector.tensor_tensor(part[:, br], m.psum[:, b:b + 2].rearrange("p b n -> p (b n)"),
                                            gate[:, u, br], ALU.mult).then_inc(scaled, 1)
                dve.wait_ge(scaled, g * 2 + 2)
                if not (isinstance(g, int) and g < 2):
                    dve.wait_ge(m_lo, g - 1)
                nc.vector.tensor_tensor(mix[:, u], part[:, 0], part[:, 1], ALU.add).then_inc(summed, 1)
            peeled(dve, 0, KT, 2, step)

        @block.gpsimd
        def _(pool):
            def rest(g, u):
                pool.wait_ge(hi, g + 1)
                nc.gpsimd.tensor_tensor(w_lo[:, u], raw[:, u], w_hi[:, u].bitcast(F32), ALU.subtract) \
                    .then_inc(lo, 1)

            def step(g, u, last=False):
                if not last:
                    rest(g + 1, 1 - u)
                pool.wait_ge(m_hi, g + 1)
                hold(pool, t)
                nc.gpsimd.tensor_tensor(t.mixT_lo[:, g], mix[:, u], t.mixT_hi[:, g].bitcast(F32), ALU.subtract) \
                    .then_inc(m_lo, 1)
            rest(0, 0)
            looped(pool, 0, KT - 2, 2, step)
            step(KT - 2, 0)
            step(KT - 1, 1, last=True)


def out_projection(nc, m, t, a):
    raw = m.at("op_raw", [P, 2, KT, HALF], 20)
    w_hi = m.at("op_hi", [P, KT, HALF], 52, F32R)
    w_lo = m.at("op_lo", [P, KT, HALF], 68, F32R)
    xin = m.at("op_x", [P, TT, HALF], 84)
    y = m.at("op_y", [P, 4, HALF], 100)
    z = m.at("op_z", [P, 4, HALF], 108)
    landed = [m.sem(f"op_w_landed{i}") for i in range(NH)]
    xl = [m.sem(f"op_x_landed{i}") for i in range(NH)]
    hi = m.sem("op_hi_done")
    lo = m.sem("op_lo_done")
    done = m.sem("op_done")
    gated = m.sem("op_gated")
    added = m.sem("op_added")
    stored = [m.sem(f"op_stored{i}") for i in range(4)]
    with nc.Block() as block:
        @block.sync
        def _(sp):
            for h in range(NH):
                cols = slice(h * HALF, (h + 1) * HALF)
                sp.dma_start(raw[:, h], a.w_out[0, :, cols].rearrange("(k p) n -> p k n", p=P)) \
                    .then_inc(landed[h], 16)
                if h:
                    sp.wait_ge(added, TT * h)
                sp.dma_start(xin[:], a.x[0, :, cols].rearrange("(i p) n -> p i n", p=P)).then_inc(xl[h], 16)

        @block.scalar
        def _(act):
            for h in range(NH):
                act.wait_ge(landed[h], 16)
                if h:
                    act.wait_ge(done, TT * h)
                for k in range(KT):
                    nc.scalar.activation(w_hi[:, k], raw[:, h, k], ACT.Copy).then_inc(hi, 1)

        @block.gpsimd
        def _(pool):
            for h in range(NH):
                for k in range(KT):
                    pool.wait_ge(hi, h * KT + k + 1)
                    nc.gpsimd.tensor_tensor(w_lo[:, k], raw[:, h, k], w_hi[:, k].bitcast(F32), ALU.subtract) \
                        .then_inc(lo, 1)
            for g in range(NH * TT):
                h, i = divmod(g, TT)
                pool.wait_ge(added, g + 1)
                pool.dma_start(t.x1[i * P:(i + 1) * P, h * HALF:(h + 1) * HALF], z[:, g % 4]) \
                    .then_inc(stored[g % 4], 16)
            for s in range(4):
                pool.wait_ge(stored[s], 16 * NH * TT // 4)

        @block.tensor
        def _(pe):
            for g in range(NH * TT):
                h, i = divmod(g, TT)
                pe.wait_ge(lo, KT * (h + 1))
                if g >= 8:
                    pe.wait_ge(gated, g - 7)
                rows = slice(i * P, (i + 1) * P)
                three_pass(nc, m.psum[:, g % 8], lambda k: t.mixT_hi[:, k, rows], lambda k: t.mixT_lo[:, k, rows],
                           lambda k: w_hi[:, k], lambda k: w_lo[:, k], KT).then_inc(done, 1)

        @block.vector
        def _(dve):
            for g in range(NH * TT):
                h, i = divmod(g, TT)
                dve.wait_ge(done, g + 1)
                if g >= 4:
                    dve.wait_ge(added, g - 3)
                nc.vector.tensor_tensor(y[:, g % 4], m.psum[:, g % 8], t.gate1[:, h * HALF:(h + 1) * HALF],
                                        ALU.mult).then_inc(gated, 1)
                dve.wait_ge(gated, g + 1)
                dve.wait_ge(xl[h], 16)
                if g >= 4:
                    dve.wait_ge(stored[g % 4], 16 * (g // 4))
                nc.vector.tensor_tensor(z[:, g % 4], y[:, g % 4], xin[:, i], ALU.add).then_inc(added, 1)


def routing(nc, m, t, a):
    raw = m.at("r_raw", [P, 2, KT, P], 84)
    w_hi = m.at("r_hi", [P, 2, KT, P], 92, F32R)
    w_lo = m.at("r_lo", [P, 2, KT, P], 100, F32R)
    qT = m.at("r_qT", [P, 2, S], 108)
    knat = m.at("r_keys", [P, 2 * PEER_HEADS, HD], 116)
    kT = m.at("r_keysT", [P, PEER_HEADS, P], 120)
    kst = m.at("r_keys_staged", [P, 2, P], 170)
    left = m.at("r_left", [P, 4, P], 124)
    best = m.at("r_best", [P, TT, 2, TOPK], 126)
    where = m.at("r_where", [P, TT, 2, TOPK], 127, U32)
    cand = m.at("r_cand", [P, 2, TOPK * TOPK], 128)
    cleft = m.at("r_cand_left", [P, 2, TOPK * TOPK], 130)
    top = m.at("r_top", [P, TT, TOPK], 132)
    pos = m.at("r_pos", [P, TT, TOPK], 132.5, U32)
    ab = m.at("r_ab", [P, 2, P], 133, U32)
    abf = m.at("r_ab_float", [P, 2, P], 134)
    wf = m.at("r_where_float", [P, TT, 2, TOPK], 135)
    less = m.at("r_less", [P, TT, TOPK], 136)
    ex = m.at("r_exp", [P, TT, TOPK], 136.5)
    rsum = m.at("r_sum", [P, TT], 137)
    rinv = m.at("r_inv", [P, TT], 137.25)
    hot = m.at("r_hot", [P, 2, TT * TOPK, TOPK], 138)
    val = m.at("r_val", [P, 2, TT * TOPK, TOPK], 154)
    landed = [m.sem(f"r_w_landed{i}") for i in range(2)]
    keysl = m.sem("r_keys_landed")
    kturned = m.sem("r_keys_turned")
    kcopied = m.sem("r_keys_copied")
    kstaged = m.sem("r_keys_staged_done")
    hi = m.sem("r_hi_done")
    lo = m.sem("r_lo_done")
    queried = m.sem("r_queried")
    qcopied = m.sem("r_q_copied")
    scored = m.sem("r_scored")
    v1 = m.sem("r_first_values")
    x1 = m.sem("r_first_places")
    l1 = m.sem("r_left_made")
    v2 = m.sem("r_second_values")
    x2 = m.sem("r_second_places")
    cd = m.sem("r_cands")
    cv1 = m.sem("r_cand_first")
    cx1 = m.sem("r_cand_first_places")
    cl1 = m.sem("r_cand_left_made")
    cv2 = m.sem("r_cand_second")
    cx2 = m.sem("r_cand_second_places")
    ints = m.sem("r_ints")
    floats = m.sem("r_floats")
    lessd = m.sem("r_lessed")
    expd = m.sem("r_expd")
    sums = m.sem("r_sums")
    invd = m.sem("r_invd")
    hotd = m.sem("r_hotd")
    vald = m.sem("r_vald")
    outd = m.sem("r_outd")
    H = PEER_HEADS
    N = TT * TOPK

    def score_at(i, s):
        return m.psum[:, 4 + 2 * ((i // 2) % 2) + s, (i % 2) * P:(i % 2 + 1) * P]

    with nc.Block() as block:
        @block.sync
        def _(sp):
            sp.dma_start(knat[:], a.sub_keys[0].rearrange("h s k d -> k (h s) d")).then_inc(keysl, 16)
            w_q = a.w_query[0].rearrange("(k p) (c n) -> c p k n", p=P, n=P)

            def load(g, u):
                if not isinstance(g, int):
                    sp.wait_ge(lo, g - 1)
                sp.dma_start(raw[:, u], w_q[g]).then_inc(landed[u], 16)
            peeled(sp, 0, H, 2, load)

        @block.tensor
        def _(pe):
            pe.wait_ge(keysl, 16)
            for q in range(2):
                for i in range(4):
                    h = 4 * q + i
                    mm = nc.tensor.transpose(m.psum[:, 2 + q, i * P:(i + 1) * P],
                                             knat[:, 2 * h:2 * h + 2].rearrange("p s d -> p (s d)"), t.ident[:])
                mm.then_inc(kturned, 1)
            pe.wait_ge(kcopied, 2)

            def query(g, u):
                pe.wait_ge(lo, g + 1)
                if not (isinstance(g, int) and g == 0):
                    pe.wait_ge(qcopied, g)
                for h in range(NH):
                    cols = slice(h * HALF, (h + 1) * HALF)
                    mm = three_pass(nc, m.psum[:, h], lambda k: w_hi[:, u, k], lambda k: w_lo[:, u, k],
                                    lambda k: t.hT_hi[:, k, cols], lambda k: t.hT_lo[:, k, cols], KT)
                mm.then_inc(queried, 1)

            def score(g, u):
                pe.wait_ge(kstaged, g + 1)
                pe.wait_ge(qcopied, g + 1)
                for pair in range(TT // 2):
                    if not (isinstance(g, int) and g == 0 and pair < 2):
                        pe.wait_ge(x1, g * 2 * TT + (4 * pair - 4))
                        pe.wait_ge(l1, g * 2 * TT + (4 * pair - 4))
                    for i in (2 * pair, 2 * pair + 1):
                        for s in range(2):
                            rows = slice(s * HD, (s + 1) * HD)
                            mm = nc.tensor.matmul(score_at(i, s), qT[rows, u, i * P:(i + 1) * P], kst[rows, u],
                                                  start=True, stop=True)
                    mm.then_inc(scored, 1)

            def both(g, u):
                query(g, u)
                score(g, u)
            peeled(pe, 0, H, 2, both)

        @block.scalar
        def _(act):
            for q in range(2):
                act.wait_ge(kturned, q + 1)
                nc.scalar.activation(kT[:, 4 * q:4 * q + 4], m.psum[:, 2 + q].rearrange("p (h k) -> p h k", k=P),
                                     ACT.Copy).then_inc(kcopied, 1)

            def split(g, u):
                act.wait_ge(landed[u], (g - u) * 8 + 16)
                if not (isinstance(g, int) and g < 2):
                    act.wait_ge(queried, g - 1)
                nc.scalar.activation(w_hi[:, u], raw[:, u], ACT.Copy).then_inc(hi, 1)

            def step(g, u, last=False):
                if not last:
                    split(g + 1, 1 - u)
                act.wait_ge(queried, g + 1)
                if not (isinstance(g, int) and g < 2):
                    act.wait_ge(scored, g * (TT // 2) - TT // 2)
                hold(act, t)
                nc.scalar.activation(kst[:, u], kT[:, g], ACT.Copy).then_inc(kstaged, 1)
                nc.scalar.activation(qT[:, u], m.psum[:, 0:2].rearrange("p b n -> p (b n)"), ACT.Copy) \
                    .then_inc(qcopied, 1)
                act.wait_ge(lessd, g + 1)
                nc.scalar.activation(ex[:], less[:], ACT.Exp).then_inc(expd, 1)
            act.wait_ge(kcopied, 2)
            split(0, 0)
            step(0, 0)
            step(1, 1)
            with act.Fori(1, H // 2 - 1) as i:
                for u in range(2):
                    step(i * 2 + u, u)
            step(H - 2, 0)
            step(H - 1, 1, last=True)

        @block.vector
        def _(dve):
            def held(g):
                if not isinstance(g, int):
                    hold(dve, t)

            def first_level(g, pair):
                tiles = (2 * pair, 2 * pair + 1)
                jobs = [(i, s) for i in tiles for s in range(2)]

                def n(i, s):
                    return g * 2 * TT + (2 * i + s + 1)
                sc = {(i, s): score_at(i, s) for i, s in jobs}
                lf = {(i, s): left[:, 2 * (i % 2) + s] for i, s in jobs}
                for i, s in jobs:
                    if s == 0 and i % 2 == 0:
                        dve.wait_ge(scored, g * (TT // 2) + (pair + 1))
                    held(g)
                    nc.vector.max(best[:, i, s, 0:8], sc[i, s]).then_inc(v1, 1)
                for i, s in jobs:
                    dve.wait_ge(v1, n(i, s))
                    held(g)
                    nc.vector.max_index(where[:, i, s, 0:8], best[:, i, s, 0:8], sc[i, s]).then_inc(x1, 1)
                for i, s in jobs:
                    if not (isinstance(g, int) and g == 0 and pair == 0):
                        dve.wait_ge(x2, n(i, s) - 4)
                    held(g)
                    nc.vector.match_replace(lf[i, s], best[:, i, s, 0:8], sc[i, s], TAKEN).then_inc(l1, 1)
                for i, s in jobs:
                    dve.wait_ge(l1, n(i, s))
                    held(g)
                    nc.vector.max(best[:, i, s, 8:16], lf[i, s]).then_inc(v2, 1)
                for i, s in jobs:
                    dve.wait_ge(v2, n(i, s))
                    held(g)
                    nc.vector.max_index(where[:, i, s, 8:16], best[:, i, s, 8:16], lf[i, s]).then_inc(x2, 1)

            def second_level(g, pair):
                tiles = (2 * pair, 2 * pair + 1)

                def n(i):
                    return g * TT + (i + 1)
                for i in tiles:
                    if not (isinstance(g, int) and g == 0 and pair == 0):
                        dve.wait_ge(cl1, n(i) - 2)
                        dve.wait_ge(cx1, n(i) - 2)
                    s1 = best[:, i, 0, :].unsqueeze(2).to_broadcast([P, TOPK, TOPK])
                    s2 = best[:, i, 1, :].unsqueeze(1).to_broadcast([P, TOPK, TOPK])
                    nc.vector.tensor_tensor(cand[:, i % 2].rearrange("p (x y) -> p x y", y=TOPK), s1, s2,
                                            ALU.add).then_inc(cd, 1)
                for i in tiles:
                    dve.wait_ge(cd, n(i))
                    held(g)
                    nc.vector.max(top[:, i, 0:8], cand[:, i % 2]).then_inc(cv1, 1)
                for i in tiles:
                    dve.wait_ge(cv1, n(i))
                    held(g)
                    nc.vector.max_index(pos[:, i, 0:8], top[:, i, 0:8], cand[:, i % 2]).then_inc(cx1, 1)
                for i in tiles:
                    if not (isinstance(g, int) and g == 0 and pair == 0):
                        dve.wait_ge(cx2, n(i) - 2)
                    held(g)
                    nc.vector.match_replace(cleft[:, i % 2], top[:, i, 0:8], cand[:, i % 2], TAKEN) \
                        .then_inc(cl1, 1)
                for i in tiles:
                    dve.wait_ge(cl1, n(i))
                    held(g)
                    nc.vector.max(top[:, i, 8:16], cleft[:, i % 2]).then_inc(cv2, 1)
                for i in tiles:
                    dve.wait_ge(cv2, n(i))
                    held(g)
                    nc.vector.max_index(pos[:, i, 8:16], top[:, i, 8:16], cleft[:, i % 2]).then_inc(cx2, 1)

            def head(g, u):
                if not (isinstance(g, int) and g == 0):
                    dve.wait_ge(outd, g * 3)
                for pair in range(TT // 2):
                    first_level(g, pair)
                    if pair:
                        second_wait(g, pair - 1)
                        second_level(g, pair - 1)
                second_wait(g, TT // 2 - 1)
                second_level(g, TT // 2 - 1)
                dve.wait_ge(cv2, g * TT + TT)
                nc.vector.tensor_tensor(less[:], top[:], top[:, :, 0:1].to_broadcast([P, TT, TOPK]),
                                        ALU.subtract).then_inc(lessd, 1)
                dve.wait_ge(cx2, g * TT + TT)
                flatpos = pos[:].rearrange("p i k -> p (i k)")
                nc.vector.tensor_scalar(ab[:, 0], flatpos, 4, None, ALU.logical_shift_right).then_inc(ints, 1)
                nc.vector.tensor_scalar(ab[:, 1], flatpos, 15, None, ALU.bitwise_and).then_inc(ints, 1)
                dve.wait_ge(x2, g * 2 * TT + 2 * TT)
                nc.vector.tensor_copy(wf[:], where[:]).then_inc(floats, 1)
                dve.wait_ge(ints, g * 2 + 2)
                nc.vector.tensor_copy(abf[:], ab[:]).then_inc(floats, 1)
                dve.wait_ge(floats, g * 2 + 2)
                for s in range(2):
                    row = t.iota[:, 0:TOPK].unsqueeze(1).to_broadcast([P, N, TOPK])
                    mine = abf[:, s].unsqueeze(2).to_broadcast([P, N, TOPK])
                    nc.vector.tensor_tensor(hot[:, s], mine, row, ALU.is_equal).then_inc(hotd, 1)
                dve.wait_ge(expd, g + 1)
                nc.vector.tensor_reduce(rsum[:], ex[:], AX.X, ALU.add).then_inc(sums, 1)
                dve.wait_ge(sums, g + 1)
                nc.vector.reciprocal(rinv[:], rsum[:]).then_inc(invd, 1)
                dve.wait_ge(invd, g + 1)
                nc.vector.tensor_tensor(t.route[:, 2, :, bass.ds(g * TOPK, TOPK)], ex[:],
                                        rinv[:].unsqueeze(2).to_broadcast([P, TT, TOPK]), ALU.mult) \
                    .then_inc(outd, 1)
                for s in range(2):
                    dve.wait_ge(vald, g * 2 + (s + 1))
                    nc.vector.tensor_reduce(t.route[:, s, :, bass.ds(g * TOPK, TOPK)],
                                            val[:, s].rearrange("p (i k) j -> p i k j", k=TOPK), AX.X, ALU.add) \
                        .then_inc(outd, 1)

            def second_wait(g, pair):
                dve.wait_ge(v2, g * 2 * TT + (4 * pair + 4))
            peeled(dve, 0, H, 1, head)

        @block.gpsimd
        def _(pool):
            def rest(g, u):
                pool.wait_ge(hi, g + 1)
                nc.gpsimd.tensor_tensor(w_lo[:, u], raw[:, u], w_hi[:, u].bitcast(F32), ALU.subtract) \
                    .then_inc(lo, 1)

            def step(g, u, last=False):
                if not last:
                    rest(g + 1, 1 - u)
                for s in range(2):
                    pool.wait_ge(hotd, g * 2 + (s + 1))
                    lists = wf[:, :, s, :].unsqueeze(2).to_broadcast([P, TT, TOPK, TOPK])
                    nc.gpsimd.tensor_tensor(val[:, s].rearrange("p (i k) j -> p i k j", k=TOPK),
                                            hot[:, s].rearrange("p (i k) j -> p i k j", k=TOPK), lists,
                                            ALU.mult).then_inc(vald, 1)
            rest(0, 0)
            step(0, 0)
            step(1, 1)
            with pool.Fori(1, H // 2 - 1) as i:
                for u in range(2):
                    step(i * 2 + u, u)
            step(H - 2, 0)
            step(H - 1, 1, last=True)


def gate_table(nc, m, t):
    TB = 64
    GT = 4
    NG = S // GT
    out = m.at("g_table", [P, 2, P, TB], 84)
    rT = m.at("g_routeT", [P, 3, S], 148)
    g_hi = m.at("g_hi", [P, S], 160, F32R)
    g_lo = m.at("g_lo", [P, S], 164, F32R)
    hot = m.at("g_hot", [P, 2, GT, 3, P], 168, F32R)
    turned = m.sem("g_turned")
    copied = m.sem("g_copied")
    hi = m.sem("g_hi_done")
    lo = m.sem("g_lo_done")
    hots = m.sem("g_hots")
    done = m.sem("g_done")
    out_s = m.sem("g_out")
    stored = [m.sem(f"g_stored{i}") for i in range(2)]
    NB = S // TB
    GB = TB // GT

    with nc.Block() as block:
        @block.tensor
        def _(pe):
            for x in range(6):
                c, h = divmod(x, NH)
                for i in range(4):
                    mm = nc.tensor.transpose(m.psum[:, x, i * P:(i + 1) * P], t.route[:, c, 4 * h + i], t.ident[:])
                mm.then_inc(turned, 1)
            pe.wait_ge(copied, 6)

            def group(g, u):
                pe.wait_ge(hots, g + 1)
                if not (isinstance(g, int) and g < 4):
                    pe.wait_ge(out_s, g - 3)
                for c in range(GT):
                    oh = hot[:, u % 2, c]
                    nc.tensor.matmul(m.psum[:, u, c * P:(c + 1) * P], oh[:, 0], oh[:, 1], start=True, stop=False)
                    mm = nc.tensor.matmul(m.psum[:, u, c * P:(c + 1) * P], oh[:, 0], oh[:, 2], start=False,
                                          stop=True)
                mm.then_inc(done, 1)
            peeled(pe, 0, NG, 4, group)

        @block.vector
        def _(dve):
            for x in range(6):
                c, h = divmod(x, NH)
                dve.wait_ge(turned, x + 1)
                nc.vector.tensor_copy(rT[:, c, h * HALF:(h + 1) * HALF], m.psum[:, x]).then_inc(copied, 1)
            dve.wait_ge(hi, 1)
            nc.vector.tensor_tensor(g_lo[:], rT[:, 2], g_hi[:].bitcast(F32), ALU.subtract).then_inc(lo, 1)
            dve.wait_ge(lo, 1)

            def group(g, u):
                if not (isinstance(g, int) and g < 2):
                    dve.wait_ge(done, g - 1)
                for c in range(GT):
                    tok = g * GT + c
                    col = (lambda x, k=None: (x[:, tok:tok + 1] if isinstance(tok, int) else x[:, bass.ds(tok, 1)]))
                    oh = hot[:, u % 2, c]
                    nc.vector.tensor_scalar(oh[:, 0], t.iota[:], col(rT[:, 1]), None, ALU.is_equal)
                    nc.vector.tensor_scalar(oh[:, 1], t.iota[:], col(rT[:, 0]), col(g_hi[:].bitcast(F32)),
                                            ALU.is_equal, ALU.mult)
                    last = nc.vector.tensor_scalar(oh[:, 2], t.iota[:], col(rT[:, 0]), col(g_lo[:].bitcast(F32)),
                                                   ALU.is_equal, ALU.mult)
                last.then_inc(hots, 1)
            peeled(dve, 0, NG, 4, group)

        @block.scalar
        def _(act):
            act.wait_ge(copied, 6)
            nc.scalar.activation(g_hi[:], rT[:, 2], ACT.Copy).then_inc(hi, 1)
            for buf in range(2):
                act.sem_inc(stored[buf], 16)
            with act.Fori(0, NB // 2) as b:
                for buf in range(2):
                    act.wait_ge(stored[buf], b * 16 + 16)
                    with act.Fori(0, GB // 4) as x:
                        for u in range(4):
                            act.wait_ge(done, b * (2 * GB) + x * 4 + (buf * GB + u + 1))
                            hold(act, t)
                            nc.scalar.activation(
                                out[:, buf, :, bass.ds(x * (4 * GT) + u * GT, GT)],
                                m.psum[:, u].rearrange("p (c e) -> p e c", e=P), ACT.Copy).then_inc(out_s, 1)

        @block.sync
        def _(sp):
            with sp.Fori(0, NB // 2) as b:
                for buf in range(2):
                    sp.wait_ge(out_s, b * (2 * GB) + (buf + 1) * GB)
                    sp.dma_start(t.table[:, :, bass.ds(b * (2 * TB) + buf * TB, TB)].rearrange("e p c -> p e c"),
                                 out[:, buf]).then_inc(stored[buf], 16)
            for buf in range(2):
                sp.wait_ge(stored[buf], 16 * NB // 2 + 16)


def experts(nc, m, t, a):
    acc = t.acc
    W_hi = m.at("e_w_hi", [P, 4, S], 116, F32R)
    W_lo = m.at("e_w_lo", [P, 4, S], 132, F32R)
    U_hi = m.at("e_u_hi", [P, 4, D], 148, F32R)
    U_lo = m.at("e_u_lo", [P, 4, D], 164, F32R)
    Draw = m.at("e_down", [P, 2, D], 180)
    DT_hi = m.at("e_downT_hi", [P, KT, P], 188, F32R)
    DT_lo = m.at("e_downT_lo", [P, KT, P], 192, F32R)
    Uraw = m.at("e_up", [P, 2, D], 196)
    Gc = m.at("e_table", [P, 2, S], 7)
    Wg = m.at("e_gelu", [P, S], 15)
    d_land = [m.sem(f"e_down_landed{i}") for i in range(2)]
    u_land = [m.sem(f"e_up_landed{i}") for i in range(2)]
    g_land = [m.sem(f"e_table_landed{i}") for i in range(2)]
    turned = m.sem("e_turned")
    dt_hi = m.sem("e_dt_hi")
    dt_lo = m.sem("e_dt_lo")
    a_done = m.sem("e_a_done")
    gelu = m.sem("e_gelu_done")
    mul = m.sem("e_mul")
    w_hi = m.sem("e_w_hi_done")
    w_lo = m.sem("e_w_lo_done")
    u_hi = m.sem("e_u_hi_done")
    u_lo = m.sem("e_u_lo_done")
    b_grp = m.sem("e_b_group")
    acc_d = m.sem("e_acc")
    NG = N_CHUNKS
    GROUPS = 16

    def at_least(eng, sem, value):
        if not (isinstance(value, int) and value <= 0):
            eng.wait_ge(sem, value)

    def steps(eng, body):
        for g in range(4):
            body(g, g)
        with eng.Fori(1, NG // 4 - 1) as r:
            for q in range(4):
                body(r * 4 + q, q)
        for q in range(4):
            body(NG - 4 + q, q)

    def is_last(g):
        return isinstance(g, int) and g == NG - 1

    with nc.Block() as block:
        @block.sync
        def _(sp):
            def chunk(src, g):
                return src[0, g * P:(g + 1) * P, :] if isinstance(g, int) else src[0, bass.ds(g * P, P), :]

            def load_down(g, u):
                at_least(sp, turned, g - 1)
                sp.dma_start(Draw[:, u], chunk(a.expert_down, g)).then_inc(d_land[u], 16)

            def step(g, q):
                u = q % 2
                if not is_last(g):
                    load_down(g + 1, 1 - u)
                at_least(sp, mul_free, g - 1)
                sp.dma_start(Gc[:, u], t.table[g] if isinstance(g, int) else
                             t.table[bass.ds(g, 1), :, :].rearrange("o p c -> (o p) c")).then_inc(g_land[u], 16)
                at_least(sp, u_lo, g - 1)
                sp.dma_start(Uraw[:, u], chunk(a.expert_up, g)).then_inc(u_land[u], 16)
            mul_free = w_lo
            load_down(0, 0)
            steps(sp, step)

        @block.tensor
        def _(pe):
            def turn(g, u):
                pe.wait_ge(d_land[u], (g - u) * 8 + 16)
                for k in range(KT):
                    mm = nc.tensor.transpose(m.psum[:, 2 + k // 4, (k % 4) * P:(k % 4 + 1) * P],
                                             Draw[:, u, k * P:(k + 1) * P], t.ident[:])
                mm.then_inc(turned, 1)

            def activations(g):
                pe.wait_ge(dt_lo, g + 1)
                for h in range(NH):
                    at_least(pe, gelu, g * 2 + (h - 1))
                    cols = slice(h * HALF, (h + 1) * HALF)
                    three_pass(nc, m.psum[:, h], lambda k: DT_hi[:, k], lambda k: DT_lo[:, k],
                               lambda k: t.hT_hi[:, k, cols], lambda k: t.hT_lo[:, k, cols], KT) \
                        .then_inc(a_done, 1)

            def up_part(g, q):
                c, pair = q % 2, 2 * ((q // 2) ^ 1)
                pe.wait_ge(w_lo, g - c)
                pe.wait_ge(u_lo, g - c)
                for j in range(8 * c, 8 * c + 8):
                    at_least(pe, acc_d, g * 8 + (j - 3 - 8 * (c + 2)))
                    rows = slice((j // 2) * P, (j // 2 + 1) * P)
                    cols = slice((j % 2) * HALF, (j % 2 + 1) * HALF)
                    three_pass(nc, m.psum[:, 4 + j % 4], lambda k: W_hi[:, pair + k, rows],
                               lambda k: W_lo[:, pair + k, rows], lambda k: U_hi[:, pair + k, cols],
                               lambda k: U_lo[:, pair + k, cols], 2).then_inc(b_grp, 1)

            def step(g, q):
                activations(g)
                if not is_last(g):
                    turn(g + 1, (q + 1) % 2)
                if not (isinstance(g, int) and g < 2):
                    up_part(g, q)
            turn(0, 0)
            steps(pe, step)
            up_part(NG, 0)
            up_part(NG + 1, 1)

        @block.scalar
        def _(act):
            def downT(g):
                act.wait_ge(turned, g + 1)
                at_least(act, a_done, g * 2)
                nc.scalar.activation(DT_hi[:].rearrange("p k n -> p (k n)"),
                                     m.psum[:, 2:4].rearrange("p b n -> p (b n)"), ACT.Copy).then_inc(dt_hi, 1)

            def step(g, q):
                for h in range(NH):
                    act.wait_ge(a_done, g * 2 + (h + 1))
                    at_least(act, mul, g * 2 + (h - 1))
                    nc.scalar.activation(Wg[:, h * HALF:(h + 1) * HALF], m.psum[:, h], ACT.Gelu).then_inc(gelu, 1)
                if not is_last(g):
                    downT(g + 1)
                free = 1 if not (isinstance(g, int) and g < 4) else 0
                act.wait_ge(mul, g * 2 + 2)
                if free:
                    act.wait_ge(b_grp, g * 8 - 8 * (q % 2 + 2))
                nc.scalar.activation(W_hi[:, q], Gc[:, q % 2], ACT.Copy).then_inc(w_hi, 1)
                act.wait_ge(u_land[q % 2], (g - q % 2) * 8 + 16)
                nc.scalar.activation(U_hi[:, q], Uraw[:, q % 2], ACT.Copy).then_inc(u_hi, 1)
            downT(0)
            steps(act, step)

        @block.vector
        def _(dve):
            def downT(g):
                dve.wait_ge(dt_hi, g + 1)
                nc.vector.tensor_tensor(DT_lo[:].rearrange("p k n -> p (k n)"),
                                        m.psum[:, 2:4].rearrange("p b n -> p (b n)"),
                                        DT_hi[:].rearrange("p k n -> p (k n)").bitcast(F32),
                                        ALU.subtract).then_inc(dt_lo, 1)

            def add_part(g, q):
                c = q % 2
                for j in range(8 * c, 8 * c + 8):
                    J = g * 8 + (j - 8 * (c + 2))
                    dve.wait_ge(b_grp, J + 1)
                    at_least(dve, acc_d, J - (GROUPS - 1))
                    out = acc[:, j // 2, (j % 2) * HALF:(j % 2 + 1) * HALF]
                    if isinstance(g, int) and g < 4:
                        nc.vector.tensor_copy(out, m.psum[:, 4 + j % 4]).then_inc(acc_d, 1)
                    else:
                        nc.vector.tensor_tensor(out, out, m.psum[:, 4 + j % 4], ALU.add).then_inc(acc_d, 1)

            def step(g, q):
                u = q % 2
                dve.wait_ge(g_land[u], (g - u) * 8 + 16)
                for h in range(NH):
                    dve.wait_ge(gelu, g * 2 + (h + 1))
                    cols = slice(h * HALF, (h + 1) * HALF)
                    nc.vector.tensor_tensor(Gc[:, u, cols], Wg[:, cols], Gc[:, u, cols], ALU.mult) \
                        .then_inc(mul, 1)
                if not is_last(g):
                    downT(g + 1)
                if not (isinstance(g, int) and g < 2):
                    add_part(g, q)
            downT(0)
            steps(dve, step)
            add_part(NG, 0)
            add_part(NG + 1, 1)

        @block.gpsimd
        def _(pool):
            def step(g, q):
                pool.wait_ge(w_hi, g + 1)
                nc.gpsimd.tensor_tensor(W_lo[:, q], Gc[:, q % 2], W_hi[:, q].bitcast(F32), ALU.subtract) \
                    .then_inc(w_lo, 1)
                pool.wait_ge(u_hi, g + 1)
                nc.gpsimd.tensor_tensor(U_lo[:, q], Uraw[:, q % 2], U_hi[:, q].bitcast(F32), ALU.subtract) \
                    .then_inc(u_lo, 1)
            steps(pool, step)


def final(nc, m, t, a, out):
    xin = m.at("f_x", [P, 4, D], 20)
    prod = m.at("f_prod", [P, 2, D], 36)
    junk = m.at("f_junk", [P, 2, D], 44)
    res = m.at("f_out", [P, 2, D], 52)
    gf = m.at("f_gain", [P, D], 60)
    ssq = m.at("f_ssq", [P, TT], 64)
    mean = m.at("f_mean", [P, TT], 64.25)
    std = m.at("f_std", [P, TT], 64.5)
    rstd = m.at("f_rstd", [P, TT], 64.75)
    landed = [m.sem(f"f_landed{i}") for i in range(4)]
    gl = m.sem("f_gain_landed")
    gated = m.sem("f_gated")
    added = m.sem("f_added")
    squared = m.sem("f_squared")
    meand = m.sem("f_meaned")
    root = m.sem("f_root")
    inv = m.sem("f_inv")
    ready = m.sem("f_ready")
    stored = [m.sem(f"f_stored{i}") for i in range(2)]
    with nc.Block() as block:
        @block.sync
        def _(sp):
            sp.dma_start(gf[:], a.final_norm_g.rearrange("(o d) -> o d", o=1).partition_broadcast(P)) \
                .then_inc(gl, 16)
            for i in range(TT):
                if i >= 4:
                    sp.wait_ge(added, i - 3)
                sp.dma_start(xin[:, i % 4], t.x1[i * P:(i + 1) * P, :]).then_inc(landed[i % 4], 16)
            for i in range(TT):
                sp.wait_ge(ready, i + 1)
                sp.dma_start(out[0, i * P:(i + 1) * P, :], res[:, i % 2]).then_inc(stored[i % 2], 16)
            for s in range(2):
                sp.wait_ge(stored[s], 16 * TT // 2)

        @block.scalar
        def _(act):
            for i in range(TT):
                act.wait_ge(added, i + 1)
                if i >= 2:
                    act.wait_ge(squared, i - 1)
                nc.scalar.activation(junk[:, i % 2], t.acc[:, i], ACT.Square, accum_out=ssq[:, i:i + 1]) \
                    .then_inc(squared, 1)
            act.wait_ge(meand, 1)
            nc.scalar.activation(std[:], mean[:], ACT.Sqrt).then_inc(root, 1)

        @block.vector
        def _(dve):
            for i in range(TT):
                if i >= 2:
                    dve.wait_ge(added, i - 1)
                nc.vector.tensor_tensor(prod[:, i % 2], t.acc[:, i], t.gate2[:], ALU.mult).then_inc(gated, 1)
                dve.wait_ge(gated, i + 1)
                dve.wait_ge(landed[i % 4], 16 * (i // 4 + 1))
                nc.vector.tensor_tensor(t.acc[:, i], prod[:, i % 2], xin[:, i % 4], ALU.add).then_inc(added, 1)
            dve.wait_ge(squared, TT)
            nc.vector.tensor_scalar(mean[:], ssq[:], 1.0 / D, EPS, ALU.mult, ALU.add).then_inc(meand, 1)
            dve.wait_ge(root, 1)
            nc.vector.reciprocal(rstd[:], std[:]).then_inc(inv, 1)
            dve.wait_ge(inv, 1)
            dve.wait_ge(gl, 16)
            for i in range(TT):
                if i >= 2:
                    dve.wait_ge(stored[i % 2], 16 * (i // 2))
                nc.vector.scalar_tensor_tensor(out=res[:, i % 2], in0=t.acc[:, i], scalar=rstd[:, i:i + 1],
                                               in1=gf[:], op0=ALU.mult, op1=ALU.mult).then_inc(ready, 1)


class Arrays:

    def __init__(self, args, line_const):
        self.x = args["x"]
        self.c = args["c"]
        self.norm_mix_g = args["norm_mix_g"]
        self.norm_ffn_g = args["norm_ffn_g"]
        self.w_ada = args["w_ada"]
        self.b_ada = args["b_ada"]
        self.w_in = args["w_in"]
        self.b_forget = args["b_forget"]
        self.sinks = args["sinks"]
        self.w_branch_a = args["w_branch_a"]
        self.w_branch_b = args["w_branch_b"]
        self.w_out = args["w_out"]
        self.rel_bias = args["rel_bias"]
        self.w_query = args["w_query"]
        self.sub_keys = args["sub_keys"]
        self.expert_down = args["expert_down"]
        self.expert_up = args["expert_up"]
        self.final_norm_g = args["final_norm_g"]
        self.line_const = line_const


class Tensors:
    pass


def build(nc, args, line_const, out):
    a = Arrays(args, line_const)
    with ExitStack() as ctx:
        m = Memory(nc, ctx)
        t = Tensors()
        t.passed = m.sem("passed_waits")
        t.ident = m.at("ident", [P, P], 0)
        t.ones = m.at("ones", [P, P], 0.5)
        t.iota = m.at("iota", [P, P], 1)
        t.mask = m.at("mask", [P, P], 1.5)
        t.cols = m.at("cols", [P, 9 * KT], 2)
        t.ccol = t.cols[:, 0:KT]
        t.bcol = t.cols[:, KT:7 * KT]
        t.gcol = t.cols[:, 7 * KT:9 * KT].rearrange("p (n k) -> p n k", k=KT)
        t.cact = m.at("cact", [P, KT], 2.3125)
        t.shift = m.at("shift", [P, 2, KT], 2.5)
        t.gain = m.at("gain", [P, 2, KT], 2.625)
        t.negsink = m.at("negsink", [P, FOX_HEADS], 2.75)
        t.bfl = m.at("bfl", [FOX_HEADS, 1], 2.8125)
        t.gate2 = m.at("gate2", [P, D], 3)
        t.gate1 = m.at("gate1", [P, D], 7)
        t.negF = m.at("negF", [FOX_HEADS, S], 15)
        t.hT_hi = m.at("hT_hi", [P, KT, S], 20, F32R)
        t.hT_lo = m.at("hT_lo", [P, KT, S], 52, F32R)
        t.qkvT = m.at("qkvT", [P, QKV_CHUNKS, S], 84)
        t.v = m.at("v", [P, TT, 5 * P], 156)
        t.kdup = m.at("kdup", [P, 2, S], 68)
        t.band = m.at("band", [P, FOX_HEADS, 2 * P], 76)
        t.o = m.at("o", [P, 2, TT, HALF], 20)
        t.mixT_hi = m.at("mixT_hi", [P, KT, S], 116, F32R)
        t.mixT_lo = m.at("mixT_lo", [P, KT, S], 148, F32R)
        t.route = m.at("route", [P, 3, TT, P], 192)
        t.acc = m.at("acc", [P, TT, D], 84)
        t.gates = m.dram("gates", [2 * KT, P, S])
        t.line_dram = m.dram("bias_line", [FOX_HEADS, P, LINE])
        t.negf_dram = m.dram("negf_rows", [FOX_HEADS, S])
        t.x1 = m.dram("x1", [S, D])
        t.table = m.dram("gate_table", [N_CHUNKS, P, S])

        m.stage(constants, t)
        m.stage(modulation, t, a)
        m.stage(norm, t, 0, a.x[0])
        m.stage(projections, t, a)
        m.stage(values, t, a)
        m.stage(attention, t)
        m.stage(mixing, t, a)
        m.stage(out_projection, t, a)
        m.stage(norm, t, 1, t.x1)
        m.stage(routing, t, a)
        m.stage(gate_table, t)
        m.stage(experts, t, a)
        m.stage(final, t, a, out)


_INS = ["x", "c", "norm_mix_g", "norm_ffn_g", "w_ada", "b_ada", "w_in", "b_forget", "sinks", "w_branch_a",
        "w_branch_b", "w_out", "rel_bias", "w_query", "sub_keys", "expert_down", "expert_up", "final_norm_g"]


def kernel(**inputs):
    import numpy as _np
    import concourse.bacc as _bacc
    from concourse import mybir as _mybir
    from concourse.bass_utils import run_bass_kernel_spmd as _run

    nc = _bacc.Bacc("TRN2", target_bir_lowering=False, num_devices=1)
    arrays, args = {}, {}
    for name in _INS:
        arr = _np.ascontiguousarray(inputs[name])
        arrays[f"in_{name}"] = arr
        args[name] = nc.dram_tensor(f"in_{name}", arr.shape, _mybir.dt.from_np(arr.dtype),
                                    kind="ExternalInput").ap()
    line = line_constants()
    arrays["line_const"] = line
    lc = nc.dram_tensor("line_const", line.shape, _mybir.dt.float32, kind="ExternalInput").ap()
    out = nc.dram_tensor("out", (1, S, D), _mybir.dt.float32, kind="ExternalOutput").ap()
    build(nc, args, lc, out)
    r = _run(nc, [arrays], core_ids=[0])
    return r.results[0]["out"]
```

```python
from contextlib import ExitStack

import numpy as np

import concourse.bass as bass
from concourse import mybir

F32 = mybir.dt.float32
F32R = mybir.dt.float32r
U32 = mybir.dt.uint32
BF16 = mybir.dt.bfloat16
ALU = mybir.AluOpType
ACT = mybir.ActivationFunctionType
AX = mybir.AxisListType

P = 128
D = 1024
KT = D // P
S = 1024
TT = S // P
HALF = 512
NH = S // HALF
HD = 64
QKV_CHUNKS = 18
FL_COL = 2304
GATE_COL = 2312
FOX_HEADS = 8
PAIRS = 4
WINDOW = 128
BUCKETS = 32
LINE = 384
PEER_HEADS = 8
TOPK = 16
N_KEYS = 128
TABLE_TOKENS = 64
N_CHUNKS = N_KEYS
EPS = 1e-6
NEG = -1e30
TAKEN = -3e38
SCALE = HD ** -0.5

SBUF_BASE = 16512


def bucket_of_line():
    dist = 255 - np.arange(LINE)
    ok = (dist >= 0) & (dist < WINDOW)
    d = np.clip(dist, 0, None)
    exact = BUCKETS // 2
    large = exact + (np.log(np.maximum(d, 1) / exact) / np.log(128 / exact) * (BUCKETS - exact)).astype(np.int32)
    return np.where(d < exact, d, np.minimum(large, BUCKETS - 1)).astype(np.int32), ok


def line_constants():
    bucket, ok = bucket_of_line()
    c = np.zeros((BUCKETS + 1, LINE), np.float32)
    for m in range(LINE):
        if ok[m]:
            c[bucket[m], m] = 1.0
        else:
            c[BUCKETS, m] = NEG
    return c


class Memory:

    def __init__(self, nc, ctx):
        self.nc, self.ctx = nc, ctx
        self.psum = ctx.enter_context(nc.psum_tensor("psum", [P, 8, HALF], F32))
        self.count = 0

    def at(self, name, shape, kb, dt=F32):
        return self.nc.alloc_sbuf_tensor_at(name, shape, dt, offset=SBUF_BASE + int(kb * 1024))

    def sem(self, name):
        return self.nc.alloc_semaphore(name)

    def stage(self, fn, *args):
        with self.nc.cleanup_on_exit():
            fn(self.nc, self, *args)

    def dram(self, name, shape):
        return self.nc.dram_tensor(name, shape, F32, kind="Internal").ap()


def peeled(eng, first, count, unroll, body):
    for u in range(unroll):
        body(first + u, u)
    with eng.Fori(1, count // unroll) as i:
        for u in range(unroll):
            body(i * unroll + (first + u), u)


def looped(eng, first, count, unroll, body):
    with eng.Fori(0, count // unroll) as i:
        for u in range(unroll):
            body(i * unroll + (first + u), u)


def constants(nc, m, t):
    zeroed = m.sem("const_zeroed")
    made = m.sem("const_made")
    with nc.Block() as block:
        @block.gpsimd
        def _(pool):
            nc.gpsimd.memset(t.ident[:], 0.0).then_inc(zeroed, 1)
            nc.gpsimd.memset(t.mask[:], 0.0).then_inc(zeroed, 1)
            nc.gpsimd.memset(t.ones[:], 1.0).then_inc(zeroed, 1)
            pool.wait_ge(zeroed, 3)
            nc.gpsimd.affine_select(out=t.ident[:], in_=t.ident[:], compare_op=ALU.not_equal, fill=1.0, base=0,
                                    pattern=[[-1, P]], channel_multiplier=1).then_inc(made, 1)
            nc.gpsimd.affine_select(out=t.mask[:], in_=t.mask[:], compare_op=ALU.is_ge, fill=NEG, base=0,
                                    pattern=[[-1, P]], channel_multiplier=1).then_inc(made, 1)
            nc.gpsimd.iota(t.iota[:], pattern=[[1, P]], base=0, channel_multiplier=0,
                           allow_small_or_imprecise_dtypes=True).then_inc(made, 1)
            pool.wait_ge(made, 3)


def modulation(nc, m, t, a):
    w = m.at("mod_w", [P, 2, KT, D], 84)
    acc = m.at("mod_acc", [P, 2, D], 148)
    sig = m.at("mod_sig", [P, KT], 156)
    small = m.sem("mod_small_landed")
    landed = [m.sem(f"mod_w_landed{i}") for i in range(2)]
    act = m.sem("mod_sigmoid")
    silu = m.sem("mod_silu")
    step = m.sem("mod_acc_step")
    summed = m.sem("mod_summed")
    cols = m.sem("mod_cols")
    rows = m.at("mod_rows", [9 * KT, P], 157)
    turned = m.sem("mod_turned")
    columns = m.sem("mod_columns")
    with nc.Block() as block:
        @block.sync
        def _(sp):
            for j in range(2):
                sp.dma_start(w[:, j], a.w_ada[0, :, j * D:(j + 1) * D].rearrange("(k p) n -> p k n", p=P)) \
                    .then_inc(landed[j], 16)

        @block.gpsimd
        def _(pool):
            at = 0
            for src, n in ((a.c, 1), (a.b_ada, 6), (a.norm_mix_g, 1), (a.norm_ffn_g, 1)):
                pool.dma_start(rows[at:at + n * KT, :], src[0].rearrange("(k p) -> k p", p=P)).then_inc(small, 16)
                at += n * KT
            pool.wait_ge(small, 64)

        @block.scalar
        def _(act_e):
            act_e.wait_ge(turned, 1)
            nc.scalar.activation(t.cols[:], m.psum[:, 1, 0:9 * KT], ACT.Copy).then_inc(columns, 1)
            act_e.wait_ge(columns, 1)
            nc.scalar.activation(sig[:], t.ccol[:], ACT.Sigmoid).then_inc(act, 1)

        @block.vector
        def _(dve):
            dve.wait_ge(act, 1)
            nc.vector.tensor_tensor(t.cact[:], t.ccol[:], sig[:], ALU.mult).then_inc(silu, 1)
            dve.wait_ge(silu, 1)
            for k in range(KT):
                for j in range(2):
                    if k == 0:
                        dve.wait_ge(landed[j], 16)
                        nc.vector.tensor_scalar(acc[:, j], w[:, j, k], t.cact[:, k:k + 1], None, ALU.mult) \
                            .then_inc(step, 1)
                    else:
                        dve.wait_ge(step, 2 * k - 1 + j)
                        nc.vector.scalar_tensor_tensor(out=acc[:, j], in0=w[:, j, k], scalar=t.cact[:, k:k + 1],
                                                       in1=acc[:, j], op0=ALU.mult, op1=ALU.add).then_inc(step, 1)
            dve.wait_ge(summed, 1)
            nc.vector.tensor_tensor(t.shift[:, 0], m.psum[:, 0, 0:KT], t.bcol[:, 0:KT], ALU.add).then_inc(cols, 1)
            nc.vector.tensor_tensor(t.gain[:, 0], m.psum[:, 0, KT:2 * KT], t.bcol[:, KT:2 * KT], ALU.add) \
                .then_inc(cols, 1)
            dve.wait_ge(cols, 2)
            nc.vector.scalar_tensor_tensor(out=t.gain[:, 0], in0=t.gain[:, 0], scalar=1.0, in1=t.gcol[:, 0],
                                           op0=ALU.add, op1=ALU.mult).then_inc(cols, 1)

        @block.tensor
        def _(pe):
            pe.wait_ge(small, 64)
            nc.tensor.transpose(m.psum[:, 1, 0:9 * KT], rows[:], t.ident[0:9 * KT, 0:9 * KT]).then_inc(turned, 1)
            pe.wait_ge(step, 2 * KT)
            for j in range(2):
                for k in range(KT):
                    mm = nc.tensor.matmul(m.psum[:, 0, j * KT + k:j * KT + k + 1], acc[:, j, k * P:(k + 1) * P],
                                          t.ones[:, 0:1], start=True, stop=True)
            mm.then_inc(summed, 1)


def norm(nc, m, t, which, src):
    n = f"n{which}_"
    GRP = 4
    xin = m.at(n + "x", [P, GRP, D], 84)
    xn = m.at(n + "xn", [P, GRP, D], 100)
    junk = m.at(n + "junk", [P, 2, D], 116)
    full = m.at(n + "full", [P, 2, HALF], 124)
    ssq = m.at(n + "ssq", [P, TT], 129)
    std = m.at(n + "std", [P, TT], 130)
    rstd = m.at(n + "rstd", [P, TT], 131)
    landed = [m.sem(f"{n}landed{i}") for i in range(GRP)]
    squared = m.sem(n + "squared")
    mean = m.sem(n + "mean")
    root = m.sem(n + "root")
    inv = m.sem(n + "inv")
    scaled = m.sem(n + "scaled")
    turned = m.sem(n + "turned")
    affine = m.sem(n + "affine")
    hi = m.sem(n + "hi")
    lo = m.sem(n + "lo")
    with nc.Block() as block:
        @block.sync
        def _(sp):
            for i in range(TT):
                if i >= GRP:
                    sp.wait_ge(scaled, i - GRP + 1)
                sp.dma_start(xin[:, i % GRP], src[i * P:(i + 1) * P, :]).then_inc(landed[i % GRP], 16)

        @block.scalar
        def _(act):
            for g in range(NH):
                for i in range(GRP * g, GRP * g + GRP):
                    act.wait_ge(landed[i % GRP], 16 * (i // GRP + 1))
                    if i >= 2:
                        act.wait_ge(squared, i - 1)
                    nc.scalar.activation(junk[:, i % 2], xin[:, i % GRP], ACT.Square,
                                         accum_out=ssq[:, i:i + 1]).then_inc(squared, 1)
                act.wait_ge(mean, g + 1)
                nc.scalar.activation(std[:, GRP * g:GRP * g + GRP], ssq[:, GRP * g:GRP * g + GRP], ACT.Sqrt) \
                    .then_inc(root, 1)
                for k in range(KT):
                    u = g * KT + k
                    act.wait_ge(affine, u + 1)
                    nc.scalar.activation(t.hT_hi[:, k, g * HALF:(g + 1) * HALF], full[:, u % 2], ACT.Copy) \
                        .then_inc(hi, 1)

        @block.vector
        def _(dve):
            for g in range(NH):
                cols = slice(GRP * g, GRP * g + GRP)
                dve.wait_ge(squared, GRP * (g + 1))
                nc.vector.tensor_scalar(ssq[:, cols], ssq[:, cols], 1.0 / D, EPS, ALU.mult, ALU.add) \
                    .then_inc(mean, 1)
                dve.wait_ge(root, g + 1)
                nc.vector.reciprocal(rstd[:, cols], std[:, cols]).then_inc(inv, 1)
                dve.wait_ge(inv, g + 1)
                if g >= 1:
                    dve.wait_ge(turned, KT * g)
                for i in range(GRP * g, GRP * g + GRP):
                    nc.vector.tensor_scalar(xn[:, i % GRP], xin[:, i % GRP], rstd[:, i:i + 1], None, ALU.mult) \
                        .then_inc(scaled, 1)
                for k in range(KT):
                    u = g * KT + k
                    dve.wait_ge(turned, u + 1)
                    if u >= 2:
                        dve.wait_ge(lo, u - 1)
                    nc.vector.tensor_scalar(full[:, u % 2], m.psum[:, u % 4], t.gain[:, which, k:k + 1],
                                            t.shift[:, which, k:k + 1], ALU.mult, ALU.add).then_inc(affine, 1)

        @block.gpsimd
        def _(pool):
            for g in range(NH):
                for k in range(KT):
                    u = g * KT + k
                    pool.wait_ge(hi, u + 1)
                    cols = slice(g * HALF, (g + 1) * HALF)
                    nc.gpsimd.tensor_tensor(t.hT_lo[:, k, cols], full[:, u % 2],
                                            t.hT_hi[:, k, cols].bitcast(F32), ALU.subtract).then_inc(lo, 1)

        @block.tensor
        def _(pe):
            for g in range(NH):
                pe.wait_ge(scaled, GRP * (g + 1))
                for k in range(KT):
                    u = g * KT + k
                    if u >= 4:
                        pe.wait_ge(affine, u - 3)
                    for i in range(GRP):
                        mm = nc.tensor.transpose(m.psum[:, u % 4, i * P:(i + 1) * P],
                                                 xn[:, i, k * P:(k + 1) * P], t.ident[:])
                    mm.then_inc(turned, 1)


def three_pass(nc, out, l_hi, l_lo, r_hi, r_lo, steps):
    for k in range(steps):
        nc.tensor.matmul(out, l_hi(k), r_hi(k), start=k == 0, stop=False)
        nc.tensor.matmul(out, l_hi(k), r_lo(k), start=False, stop=False)
        mm = nc.tensor.matmul(out, l_lo(k), r_hi(k), start=False, stop=k == steps - 1)
    return mm


def projections(nc, m, t, a):
    raw = m.at("pw_raw", [P, 2, KT, P], 156)
    w_hi = m.at("pw_hi", [P, 2, KT, P], 164, F32R)
    w_lo = m.at("pw_lo", [P, 2, KT, P], 172, F32R)
    adaw = m.at("p_adaw", [P, 2, D], 180)
    acc = [t.gate1, m.at("p_acc_shift", [P, D], 188), m.at("p_acc_scale", [P, D], 192), t.gate2]
    sg = m.at("p_sigmoid", [P, 2, D], 196)
    tmp = m.at("p_adatmp", [P, 896], 204)
    fl = m.at("p_fl", [FOX_HEADS, D], 188)
    fe = m.at("p_fe", [FOX_HEADS, D], 192)
    bfl = t.bfl
    landed = [m.sem(f"p_w_landed{i}") for i in range(2)]
    hi = m.sem("p_hi")
    lo = m.sem("p_lo")
    done = m.sem("p_done")
    out = m.sem("p_out")
    stored = [m.sem(f"p_stored{i}") for i in range(2)]
    ada_landed = [m.sem(f"p_ada_landed{i}") for i in range(2)]
    weighed = m.sem("p_weighed")
    added = m.sem("p_added")
    summed = m.sem("p_summed")
    taken = m.sem("p_taken")
    small = m.sem("p_small")
    fx = m.sem("p_forget_act")
    fv = m.sem("p_forget_dve")
    MODS = 4
    NQ, NG = QKV_CHUNKS, 2 * KT
    FL = NQ + NG
    PART = 512

    with nc.Block() as block:
        @block.sync
        def _(sp):
            w_q = a.w_in[0, :, 0:NQ * P].rearrange("(k p) (c n) -> c p k n", p=P, n=P)
            w_g = a.w_in[0, :, GATE_COL:GATE_COL + NG * P].rearrange("(k p) (c n) -> c p k n", p=P, n=P)

            def load_q(g, u):
                if isinstance(g, int):
                    pass
                else:
                    sp.wait_ge(lo, g - 1)
                sp.dma_start(raw[:, u], w_q[g]).then_inc(landed[u], 16)

            def load_g(g, u):
                sp.wait_ge(lo, g - 1)
                sp.dma_start(raw[:, u], w_g[g - NQ]).then_inc(landed[u], 16)

            peeled(sp, 0, NQ, 2, load_q)
            looped(sp, NQ, NG, 2, load_g)
            sp.wait_ge(lo, FL - 1)
            sp.dma_start(raw[:, 0, :, 0:FOX_HEADS],
                         a.w_in[0, :, FL_COL:FL_COL + FOX_HEADS].rearrange("(k p) n -> p k n", p=P)) \
                .then_inc(landed[0], 16)

        @block.scalar
        def _(act):
            def split(g, u, n=P):
                act.wait_ge(landed[u], (g - u) * 8 + 16)
                if not (isinstance(g, int) and g < 2):
                    act.wait_ge(done, g - 1)
                nc.scalar.activation(w_hi[:, u, :, 0:n], raw[:, u, :, 0:n], ACT.Copy).then_inc(hi, 1)

            def q_step(g, u):
                split(g + 1, 1 - u)
                act.wait_ge(done, g + 1)
                nc.scalar.activation(t.qkvT[:, g], m.psum[:, 2 * u:2 * u + 2], ACT.Copy).then_inc(out, 1)

            def g_step(g, u, last=False):
                if not last:
                    split(g + 1, 1 - u)
                act.wait_ge(done, g + 1)
                if not (isinstance(g, int) and g < NQ + 2):
                    act.wait_ge(stored[u], (g - u - NQ) * 8)
                nc.scalar.activation(sg[:, u], m.psum[:, 2 * u:2 * u + 2], ACT.Sigmoid).then_inc(out, 1)
                act.wait_ge(out, g + 1)
                act.dma_start(t.gates[g - NQ], sg[:, u]).then_inc(stored[u], 16)

            split(0, 0)
            peeled(act, 0, NQ, 2, q_step)
            g_step(NQ, 0)
            g_step(NQ + 1, 1)
            with act.Fori(1, NG // 2 - 1) as i:
                for u in range(2):
                    g_step(i * 2 + (NQ + u), u)
            g_step(FL - 2, 0)
            g_step(FL - 1, 1, last=True)
            split(FL, 0, FOX_HEADS)
            act.wait_ge(fv, 1)
            nc.scalar.activation(fe[:], fl[:], ACT.Abs).then_inc(fx, 1)
            act.wait_ge(fx, 1)
            nc.scalar.activation(fe[:], fe[:], ACT.Exp, scale=-1.0).then_inc(fx, 1)
            act.wait_ge(fx, 2)
            nc.scalar.activation(fe[:], fe[:], ACT.Ln, bias=1.0).then_inc(fx, 1)
            for u in range(2):
                act.wait_ge(stored[u], NG * 8)

        @block.vector
        def _(dve):
            def rest(g, u, n=P):
                dve.wait_ge(hi, g + 1)
                nc.vector.tensor_tensor(w_lo[:, u, :, 0:n], raw[:, u, :, 0:n], w_hi[:, u, :, 0:n].bitcast(F32),
                                        ALU.subtract).then_inc(lo, 1)
            looped(dve, 0, FL, 2, rest)
            rest(FL, 0, FOX_HEADS)
            dve.wait_ge(summed, 1)
            nc.vector.tensor_tensor(t.shift[:, 1], m.psum[:, 4, 0:KT], t.bcol[:, 3 * KT:4 * KT], ALU.add) \
                .then_inc(taken, 1)
            nc.vector.tensor_tensor(t.gain[:, 1], m.psum[:, 4, KT:2 * KT], t.bcol[:, 4 * KT:5 * KT], ALU.add) \
                .then_inc(taken, 1)
            dve.wait_ge(taken, 2)
            nc.vector.scalar_tensor_tensor(out=t.gain[:, 1], in0=t.gain[:, 1], scalar=1.0, in1=t.gcol[:, 1],
                                           op0=ALU.add, op1=ALU.mult).then_inc(taken, 1)
            dve.wait_ge(small, 48)
            dve.wait_ge(summed, 2)
            nc.vector.tensor_tensor(t.gate1[:], adaw[:, 0], m.psum[:, 5:7], ALU.add).then_inc(taken, 1)
            dve.wait_ge(taken, 4)
            dve.wait_ge(summed, 3)
            nc.vector.tensor_tensor(t.gate2[:], adaw[:, 1], m.psum[:, 5:7], ALU.add).then_inc(taken, 1)
            dve.wait_ge(done, FL + 1)
            z = m.psum[0:FOX_HEADS, 0:2]
            nc.vector.tensor_scalar(fl[:], z, bfl[:, 0:1], None, ALU.add).then_inc(fv, 1)
            dve.wait_ge(fv, 1)
            dve.wait_ge(fx, 1)
            nc.vector.tensor_scalar(fl[:], fl[:], -1.0, 0.0, ALU.mult, ALU.max).then_inc(fv, 1)
            dve.wait_ge(fv, 2)
            dve.wait_ge(fx, 3)
            nc.vector.tensor_tensor(fe[:], fe[:], fl[:], ALU.add).then_inc(fv, 1)
            dve.wait_ge(fv, 3)
            nc.vector.memset(fl[:], 1.0).then_inc(fv, 1)
            dve.wait_ge(fv, 4)
            nc.vector.tensor_tensor_scan(t.negF[:], fl[:], fe[:], 0.0, ALU.mult, ALU.add).then_inc(fv, 1)

        @block.gpsimd
        def _(pool):
            order = [2, 3, 4, 5]
            pool.dma_start(bfl[:, 0:1], a.b_forget.rearrange("a h -> h a")).then_inc(small, 16)

            def load(n):
                j, k = divmod(n, KT)
                pool.dma_start(adaw[:, n % 2], a.w_ada[0, k * P:(k + 1) * P, order[j] * D:(order[j] + 1) * D]) \
                    .then_inc(ada_landed[n % 2], 16)
            load(0)
            steps = 0
            for n in range(MODS * KT):
                j, k = divmod(n, KT)
                if n + 1 < MODS * KT:
                    if n >= 1:
                        pool.wait_ge(weighed, 2 * n)
                    load(n + 1)
                pool.wait_ge(ada_landed[n % 2], 16 * (n // 2 + 1))
                for h in range(2):
                    cols = slice(h * PART, (h + 1) * PART)
                    if k == 0:
                        nc.gpsimd.tensor_scalar(acc[j][:, cols], adaw[:, n % 2, cols], t.cact[:, k:k + 1], None,
                                                ALU.mult).then_inc(weighed, 1)
                        continue
                    if steps >= 1:
                        pool.wait_ge(added, steps)
                    nc.gpsimd.tensor_scalar(tmp[:, 0:PART], adaw[:, n % 2, cols], t.cact[:, k:k + 1], None,
                                            ALU.mult).then_inc(weighed, 1)
                    pool.wait_ge(weighed, 2 * n + h + 1)
                    nc.gpsimd.tensor_tensor(acc[j][:, cols], acc[j][:, cols], tmp[:, 0:PART], ALU.add) \
                        .then_inc(added, 1)
                    steps += 1
            pool.wait_ge(weighed, 2 * MODS * KT)
            for s, j in ((0, 2), (1, 5)):
                pool.dma_start(adaw[:, s], a.b_ada[:, j * D:(j + 1) * D].partition_broadcast(P)) \
                    .then_inc(small, 16)
            pool.wait_ge(small, 48)

        @block.tensor
        def _(pe):
            def chunk(g, u, n=P):
                pe.wait_ge(lo, g + 1)
                if not (isinstance(g, int) and g < 2):
                    pe.wait_ge(out, g - 1)
                for h in range(NH):
                    cols = slice(h * HALF, (h + 1) * HALF)
                    mm = three_pass(nc, m.psum[0:n, 2 * u + h], lambda k: w_hi[:, u, k, 0:n],
                                    lambda k: w_lo[:, u, k, 0:n], lambda k: t.hT_hi[:, k, cols],
                                    lambda k: t.hT_lo[:, k, cols], KT)
                mm.then_inc(done, 1)
            peeled(pe, 0, FL, 2, chunk)
            chunk(FL, 0, FOX_HEADS)
            pe.wait_ge(weighed, 2 * MODS * KT)
            pe.wait_ge(added, 2 * MODS * (KT - 1))
            for j in range(2):
                for k in range(KT):
                    mm = nc.tensor.matmul(m.psum[:, 4, j * KT + k:j * KT + k + 1],
                                          acc[1 + j][:, k * P:(k + 1) * P], t.ones[:, 0:1], start=True, stop=True)
            mm.then_inc(summed, 1)
            for n, gate in enumerate((t.gate1, t.gate2)):
                if n:
                    pe.wait_ge(taken, 4)
                for h in range(2):
                    mm = nc.tensor.matmul(m.psum[:, 5 + h], t.ones[:], gate[:, h * HALF:(h + 1) * HALF],
                                          start=True, stop=True)
                mm.then_inc(summed, 1)


def values(nc, m, t, a):
    pick = m.at("v_pick", [BUCKETS, LINE], 178)
    outside = m.at("v_outside", [FOX_HEADS, LINE], 180)
    rel = m.at("v_rel", [BUCKETS, FOX_HEADS], 182)
    line = m.at("v_line", [FOX_HEADS, LINE], 183)
    small = m.sem("v_small")
    turned = m.sem("v_turned")
    copied = m.sem("v_copied")
    lined = m.sem("v_lined")
    linec = m.sem("v_line_copied")
    wrote = m.sem("v_line_written")
    bands = m.sem("v_bands")
    vchunks = [5, 14, 15, 16, 17]
    with nc.Block() as block:
        @block.sync
        def _(sp):
            sp.dma_start(pick[:], a.line_const[0:BUCKETS, :]).then_inc(small, 16)
            sp.dma_start(outside[:], a.line_const[BUCKETS:BUCKETS + 1, :].partition_broadcast(FOX_HEADS)) \
                .then_inc(small, 16)
            sp.dma_start(rel[:], a.rel_bias).then_inc(small, 16)
            for g in range(2):
                for half in range(2):
                    sp.dma_start(t.kdup[half * HD:(half + 1) * HD, g], t.qkvT[g * HD:(g + 1) * HD, 4]) \
                        .then_inc(bands, 16)
            sp.dma_start(t.negsink[:], a.sinks.partition_broadcast(P)).then_inc(bands, 16)
            sp.wait_ge(linec, 1)
            sp.dma_start(t.line_dram, line[:].unsqueeze(1).to_broadcast([FOX_HEADS, P, LINE])).then_inc(wrote, 16)
            sp.wait_ge(wrote, 16)
            for h in range(FOX_HEADS):
                src = bass.AP(t.line_dram.tensor, h * P * LINE + P - 1, [[LINE - 1, P], [1, 2 * P]])
                sp.dma_start(t.band[:, h], src).then_inc(bands, 16)
            sp.wait_ge(bands, 16 * (5 + FOX_HEADS))

        @block.tensor
        def _(pe):
            pe.wait_ge(small, 48)
            nc.tensor.matmul(m.psum[0:FOX_HEADS, 7, 0:LINE], rel[:], pick[:], start=True, stop=True) \
                .then_inc(lined, 1)
            for n, c in enumerate(vchunks):
                for q in range(2):
                    u = 2 * n + q
                    if u >= 4:
                        pe.wait_ge(copied, u - 3)
                    for i in range(4):
                        mm = nc.tensor.transpose(m.psum[:, u % 4, i * P:(i + 1) * P],
                                                 t.qkvT[:, c, (4 * q + i) * P:(4 * q + i + 1) * P], t.ident[:])
                    mm.then_inc(turned, 1)

        @block.vector
        def _(dve):
            dve.wait_ge(lined, 1)
            dve.wait_ge(small, 48)
            nc.vector.tensor_tensor(line[:], m.psum[0:FOX_HEADS, 7, 0:LINE], outside[:], ALU.add) \
                .then_inc(linec, 1)
            for n in range(len(vchunks)):
                for q in range(2):
                    u = 2 * n + q
                    dve.wait_ge(turned, u + 1)
                    nc.vector.tensor_copy(t.v[:, 4 * q:4 * q + 4, n * P:(n + 1) * P],
                                          m.psum[:, u % 4].rearrange("p (i c) -> p i c", c=P)).then_inc(copied, 1)
            dve.wait_ge(bands, 16 * (5 + FOX_HEADS))
            nc.vector.tensor_scalar(t.negsink[:], t.negsink[:], -1.0, None, ALU.mult).then_inc(copied, 1)


def hold(eng, t):
    eng.sem_inc(t.passed, 1)


def attention(nc, m, t):
    JOBS = [(br, par, n) for br in (0, 1) for par in (0, 1) for n in range(TT)]
    NJ = len(JOBS)
    q_st = m.at("at_q", [P, 2, S], 52)
    k_st = m.at("at_k", [P, 2, S], 60)
    nf = m.at("at_negF", [P, 2, S], 176)
    sc = m.at("at_scores", [P, 2, S], 184)
    pT = m.at("at_pT", [P, 2, S], 192)
    b_st = m.at("at_band", [P, 2, 2 * P], 200)
    mx = m.at("at_max", [P, NJ], 202)
    nm = m.at("at_negmax", [P, NJ], 202.25)
    rs = m.at("at_rowsum", [P, NJ], 202.5)
    se = m.at("at_sinkexp", [P, NJ], 202.75)
    dn = m.at("at_denominator", [P, NJ], 203)
    rc = m.at("at_reciprocal", [P, NJ], 203.25)
    flat = m.psum[:].rearrange("p b n -> p (b n)")
    q_ready = m.sem("at_staged_q")
    k_ready = m.sem("at_staged_k")
    negf_out = m.sem("at_negF_out")
    negf_in = [m.sem(f"at_negF_in{i}") for i in range(2)]
    scored = m.sem("at_scored")
    maxed = m.sem("at_maxed")
    negated = m.sem("at_negated")
    expd = m.sem("at_exp")
    sunk = m.sem("at_sink_exp")
    turned = m.sem("at_turned")
    copied_a = m.sem("at_copied_act")
    copied_v = m.sem("at_copied_dve")
    weighted = m.sem("at_weighted")
    dens = m.sem("at_denominators")
    inv = m.sem("at_inverted")
    normed = m.sem("at_normed")

    def keys(job):
        br, par, n = job
        return list(range(0 if br == 0 else max(n - 1, 0), n + 1))

    groups = [[keys(j)[x:x + 4] for x in range(0, len(keys(j)), 4)] for j in JOBS]
    before = [sum(len(g) for g in groups[:j]) for j in range(NJ + 1)]
    NGR = before[NJ]
    assert NGR % 2 == 0
    NC = NGR // 2
    NS = sum(1 for j in JOBS if j[0] == 1)
    LIVE = 2

    def copies(eng, copy, mine, sem, i, j):
        for x, grp in enumerate(groups[j]):
            G = before[j] + x
            if G % 2 != mine:
                continue
            after(eng, turned, i * NGR + (G + 1))
            if j >= LIVE:
                after(eng, weighted, i * NJ + (j - 1))
            w = len(grp) * P
            copy(pT[:, j % 2, x * HALF:x * HALF + w], flat[:, (4 + G % 2) * HALF:(4 + G % 2) * HALF + w]) \
                .then_inc(sem, 1)

    def after(eng, sem, count):
        eng.wait_ge(sem, count + 1)

    with nc.Block() as block:
        @block.sync
        def _(sp):
            sp.dma_start(t.negf_dram, t.negF[:]).then_inc(negf_out, 16)
            sp.wait_ge(negf_out, 16)
            with sp.Fori(0, PAIRS) as i:
                for par in range(2):
                    after(sp, maxed, i * NJ)
                    sp.dma_start(nf[:, par], t.negf_dram[i * 2 + par:i * 2 + (par + 1), :].partition_broadcast(P)
                                 if isinstance(i, int) else
                                 t.negf_dram[bass.ds(i * 2 + par, 1), :].partition_broadcast(P)) \
                        .then_inc(negf_in[par], 16)

        @block.gpsimd
        def _(pool):
            with pool.Fori(0, PAIRS) as i:
                after(pool, scored, i * NJ)
                hold(pool, t)
                nc.gpsimd.tensor_copy(k_st[:, 0], t.qkvT[:, i + 10]).then_inc(k_ready, 1)
                nc.gpsimd.tensor_copy(k_st[:, 1], t.kdup[:, i // 2]).then_inc(k_ready, 1)
                after(pool, maxed, i * NJ)
                hold(pool, t)
                for par in range(2):
                    nc.gpsimd.tensor_copy(b_st[:, par], t.band[:, i * 2 + par]).then_inc(k_ready, 1)

        @block.tensor
        def _(pe):
            for sem in (scored, turned, weighted):
                pe.sem_inc(sem, 1)
            with pe.Fori(0, PAIRS) as i:
                def score(j):
                    br, par, n = JOBS[j]
                    rows = slice(par * HD, (par + 1) * HD)
                    if j == 0:
                        pe.wait_ge(q_ready, i * 2 + 2)
                        pe.wait_ge(k_ready, i * 4 + 2)
                    after(pe, maxed, i * NJ + max(j - 1, 0))
                    ks = keys(JOBS[j])
                    k0, w = ks[0] * P, len(ks) * P
                    for h in range(0, w, HALF):
                        x = min(HALF, w - h)
                        diag = h + x == w and br == 0
                        o = (2 * (j % 2)) * HALF + h
                        mm = nc.tensor.matmul(flat[:, o:o + x], q_st[rows, br, n * P:(n + 1) * P],
                                              k_st[rows, br, k0 + h:k0 + h + x], start=True, stop=not diag)
                        if diag:
                            mm = nc.tensor.matmul(flat[:, o + x - P:o + x], t.ident[:], t.mask[:],
                                                  start=False, stop=True)
                    mm.then_inc(scored, 1)

                def turn(j):
                    pe.wait_ge(expd, i * NJ + (j + 1))
                    k0 = keys(JOBS[j])[0]
                    for x, grp in enumerate(groups[j]):
                        G = before[j] + x
                        after(pe, copied_v if G % 2 else copied_a, i * NC + G // 2)
                        for y, kt in enumerate(grp):
                            o = (4 + G % 2) * HALF + y * P
                            mm = nc.tensor.transpose(flat[:, o:o + P],
                                                     sc[:, j % 2, (kt - k0) * P:(kt - k0 + 1) * P], t.ident[:])
                        mm.then_inc(turned, 1)

                def weigh(j):
                    br, par, n = JOBS[j]
                    G = before[j + 1]
                    after(pe, copied_a, i * NC + (G + 1) // 2)
                    after(pe, copied_v, i * NC + G // 2)
                    after(pe, normed, i * NJ + max(j - 1, 0))
                    ks = keys(JOBS[j])
                    for y, kt in enumerate(ks):
                        col = i * P + (P + par * HD) if br == 0 else (i // 2) * HD
                        mm = nc.tensor.matmul(m.psum[:, 6 + j % 2, 0:HD], pT[:, j % 2, y * P:(y + 1) * P],
                                              t.v[:, kt, bass.ds(col, HD)], start=y == 0, stop=y == len(ks) - 1)
                    mm.then_inc(weighted, 1)

                for j in range(NJ + 2):
                    if j < NJ:
                        score(j)
                    if 1 <= j <= NJ:
                        turn(j - 1)
                    if j >= 2:
                        weigh(j - 2)

        @block.scalar
        def _(act):
            act.sem_inc(copied_a, 1)
            with act.Fori(0, PAIRS) as i:
                after(act, scored, i * NJ)
                hold(act, t)
                nc.scalar.activation(q_st[:, 0], t.qkvT[:, i + 6], ACT.Copy, scale=SCALE).then_inc(q_ready, 1)
                nc.scalar.activation(q_st[:, 1], t.qkvT[:, i], ACT.Copy, scale=SCALE).then_inc(q_ready, 1)
                for j in range(NJ + 1):
                    if j < NJ:
                        br, par, n = JOBS[j]
                        w = len(keys(JOBS[j])) * P
                        act.wait_ge(negated, i * NJ + (j + 1))
                        nc.scalar.activation(sc[:, j % 2, 0:w], sc[:, j % 2, 0:w], ACT.Exp,
                                             bias=nm[:, j:j + 1], accum_out=rs[:, j:j + 1]).then_inc(expd, 1)
                        if br == 1:
                            nc.scalar.activation(se[:, j:j + 1], t.negsink[:, bass.ds(i * 2 + par, 1)], ACT.Exp,
                                                 bias=nm[:, j:j + 1], scale=-1.0).then_inc(sunk, 1)
                    if j >= 1:
                        copies(act, lambda o, x: nc.scalar.activation(o, x, ACT.Copy), 0, copied_a, i, j - 1)

        @block.vector
        def _(dve):
            for sem in (maxed, copied_v, normed):
                dve.sem_inc(sem, 1)
            with dve.Fori(0, PAIRS) as i:
                def maximum(j):
                    br, par, n = JOBS[j]
                    w = len(keys(JOBS[j])) * P
                    if br == 0 and n == 0:
                        dve.wait_ge(negf_in[par], i * 16 + 16)
                    if j == NJ - NS:
                        dve.wait_ge(k_ready, i * 4 + 4)
                    after(dve, turned, i * NGR + before[max(j - 1, 0)])
                    after(dve, scored, i * NJ + (j + 1))
                    hold(dve, t)
                    bias = nf[:, par, 0:w] if br == 0 else b_st[:, par, 2 * P - w:2 * P]
                    nc.vector.tensor_tensor_reduce(sc[:, j % 2, 0:w], flat[:, 2 * (j % 2) * HALF:][:, 0:w], bias,
                                                   1.0, -3e38, ALU.add, ALU.max, mx[:, j:j + 1]).then_inc(maxed, 1)
                    after(dve, maxed, i * NJ + (j + 1))
                    if br == 0:
                        nc.vector.tensor_scalar(nm[:, j:j + 1], mx[:, j:j + 1], -1.0, None, ALU.mult) \
                            .then_inc(negated, 1)
                    else:
                        nc.vector.tensor_scalar(nm[:, j:j + 1], mx[:, j:j + 1], -1.0,
                                                t.negsink[:, bass.ds(i * 2 + par, 1)], ALU.mult, ALU.min) \
                            .then_inc(negated, 1)

                def divide(j):
                    br, par, n = JOBS[j]
                    dve.wait_ge(expd, i * NJ + (j + 1))
                    den = rs
                    if br == 1:
                        w = j - (NJ - NS)
                        dve.wait_ge(sunk, i * NS + (w + 1))
                        nc.vector.tensor_tensor(dn[:, j:j + 1], rs[:, j:j + 1], se[:, j:j + 1], ALU.add) \
                            .then_inc(dens, 1)
                        dve.wait_ge(dens, i * NS + (w + 1))
                        den = dn
                    nc.vector.reciprocal(rc[:, j:j + 1], den[:, j:j + 1]).then_inc(inv, 1)
                    dve.wait_ge(inv, i * NJ + (j + 1))
                    after(dve, weighted, i * NJ + (j + 1))
                    nc.vector.tensor_scalar(t.o[:, 1 - br, n, bass.ds(i * P + par * HD, HD)],
                                            m.psum[:, 6 + j % 2, 0:HD], rc[:, j:j + 1], None, ALU.mult) \
                        .then_inc(normed, 1)

                for j in range(NJ + 2):
                    if j < NJ:
                        maximum(j)
                    if 1 <= j <= NJ:
                        copies(dve, nc.vector.tensor_copy, 1, copied_v, i, j - 1)
                    if j >= 2:
                        divide(j - 2)


def mixing(nc, m, t, a):
    KB = 4
    oT_hi = m.at("mx_oT_hi", [P, 2 * KB, S], 52, F32R)
    oT_lo = m.at("mx_oT_lo", [P, 2 * KB, S], 84, F32R)
    raw = m.at("mx_raw", [P, 2, 2 * KB, P], 180)
    w_hi = m.at("mx_w_hi", [P, 2, 2 * KB, P], 188, F32R)
    w_lo = m.at("mx_w_lo", [P, 2, 2 * KB, P], 196, F32R)
    gate = m.at("mx_gate", [P, 2, 2, S], 20)
    part = m.at("mx_part", [P, 2, S], 36)
    mix = m.at("mx_sum", [P, 2, S], 44)
    landed = [m.sem(f"mx_w_landed{i}") for i in range(2)]
    gated = [m.sem(f"mx_gate_landed{i}") for i in range(2)]
    turned = m.sem("mx_turned")
    o_hi = m.sem("mx_o_hi")
    o_lo = m.sem("mx_o_lo")
    hi = m.sem("mx_hi")
    lo = m.sem("mx_lo")
    done = m.sem("mx_done")
    scaled = m.sem("mx_scaled")
    summed = m.sem("mx_summed")
    m_hi = m.sem("mx_m_hi")
    m_lo = m.sem("mx_m_lo")
    UNITS = 2 * KB * NH
    with nc.Block() as block:
        @block.sync
        def _(sp):
            w_a = a.w_branch_a[0].rearrange("(k p) (c n) -> c p k n", p=P, n=P)
            w_b = a.w_branch_b[0].rearrange("(k p) (c n) -> c p k n", p=P, n=P)

            def load(g, u):
                if not isinstance(g, int):
                    sp.wait_ge(lo, g - 1)
                sp.dma_start(raw[:, u, 0:KB], w_a[g]).then_inc(landed[u], 16)
                sp.dma_start(raw[:, u, KB:2 * KB], w_b[g]).then_inc(landed[u], 16)
                if isinstance(g, int):
                    if g == 0:
                        sp.wait_ge(turned, UNITS)
                else:
                    sp.wait_ge(scaled, g * 2 - 2)
                sp.dma_start(gate[:, u, 0], t.gates[g]).then_inc(gated[u], 16)
                sp.dma_start(gate[:, u, 1], t.gates[g + KT]).then_inc(gated[u], 16)
            peeled(sp, 0, KT, 2, load)

        @block.tensor
        def _(pe):
            for x in range(UNITS):
                c, h = divmod(x, NH)
                if x >= 8:
                    pe.wait_ge(o_lo, x - 7)
                for i in range(4):
                    mm = nc.tensor.transpose(m.psum[:, x % 8, i * P:(i + 1) * P],
                                             t.o[:, c // KB, 4 * h + i, (c % KB) * P:(c % KB + 1) * P], t.ident[:])
                mm.then_inc(turned, 1)
            pe.wait_ge(o_lo, UNITS)

            def chunk(g, u):
                pe.wait_ge(lo, g + 1)
                if not (isinstance(g, int) and g < 2):
                    pe.wait_ge(scaled, g * 2 - 2)
                for br in range(2):
                    for h in range(NH):
                        cols = slice(h * HALF, (h + 1) * HALF)
                        mm = three_pass(nc, m.psum[:, 4 * u + 2 * br + h],
                                        lambda k: w_hi[:, u, br * KB + k], lambda k: w_lo[:, u, br * KB + k],
                                        lambda k: oT_hi[:, br * KB + k, cols],
                                        lambda k: oT_lo[:, br * KB + k, cols], KB)
                mm.then_inc(done, 1)
            peeled(pe, 0, KT, 2, chunk)

        @block.scalar
        def _(act):
            for x in range(UNITS):
                c, h = divmod(x, NH)
                act.wait_ge(turned, x + 1)
                nc.scalar.activation(oT_hi[:, c, h * HALF:(h + 1) * HALF], m.psum[:, x % 8], ACT.Copy) \
                    .then_inc(o_hi, 1)

            def split(g, u):
                act.wait_ge(landed[u], (g - u) * 16 + 32)
                if not (isinstance(g, int) and g < 2):
                    act.wait_ge(done, g - 1)
                nc.scalar.activation(w_hi[:, u], raw[:, u], ACT.Copy).then_inc(hi, 1)

            def step(g, u, last=False):
                if not last:
                    split(g + 1, 1 - u)
                act.wait_ge(summed, g + 1)
                hold(act, t)
                nc.scalar.activation(t.mixT_hi[:, g], mix[:, u], ACT.Copy).then_inc(m_hi, 1)
            split(0, 0)
            step(0, 0)
            step(1, 1)
            with act.Fori(1, KT // 2 - 1) as i:
                for u in range(2):
                    step(i * 2 + u, u)
            step(KT - 2, 0)
            step(KT - 1, 1, last=True)

        @block.vector
        def _(dve):
            for x in range(UNITS):
                c, h = divmod(x, NH)
                cols = slice(h * HALF, (h + 1) * HALF)
                dve.wait_ge(o_hi, x + 1)
                nc.vector.tensor_tensor(oT_lo[:, c, cols], m.psum[:, x % 8], oT_hi[:, c, cols].bitcast(F32),
                                        ALU.subtract).then_inc(o_lo, 1)

            def step(g, u):
                dve.wait_ge(done, g + 1)
                dve.wait_ge(gated[u], (g - u) * 16 + 32)
                for br in range(2):
                    if not (isinstance(g, int) and g == 0):
                        dve.wait_ge(summed, g)
                    b = 4 * u + 2 * br
                    nc.vector.tensor_tensor(part[:, br], m.psum[:, b:b + 2].rearrange("p b n -> p (b n)"),
                                            gate[:, u, br], ALU.mult).then_inc(scaled, 1)
                dve.wait_ge(scaled, g * 2 + 2)
                if not (isinstance(g, int) and g < 2):
                    dve.wait_ge(m_lo, g - 1)
                nc.vector.tensor_tensor(mix[:, u], part[:, 0], part[:, 1], ALU.add).then_inc(summed, 1)
            peeled(dve, 0, KT, 2, step)

        @block.gpsimd
        def _(pool):
            def rest(g, u):
                pool.wait_ge(hi, g + 1)
                nc.gpsimd.tensor_tensor(w_lo[:, u], raw[:, u], w_hi[:, u].bitcast(F32), ALU.subtract) \
                    .then_inc(lo, 1)

            def step(g, u, last=False):
                if not last:
                    rest(g + 1, 1 - u)
                pool.wait_ge(m_hi, g + 1)
                hold(pool, t)
                nc.gpsimd.tensor_tensor(t.mixT_lo[:, g], mix[:, u], t.mixT_hi[:, g].bitcast(F32), ALU.subtract) \
                    .then_inc(m_lo, 1)
            rest(0, 0)
            looped(pool, 0, KT - 2, 2, step)
            step(KT - 2, 0)
            step(KT - 1, 1, last=True)


def out_projection(nc, m, t, a):
    raw = m.at("op_raw", [P, 2, KT, HALF], 20)
    w_hi = m.at("op_hi", [P, KT, HALF], 52, F32R)
    w_lo = m.at("op_lo", [P, KT, HALF], 68, F32R)
    xin = m.at("op_x", [P, TT, HALF], 84)
    y = m.at("op_y", [P, 4, HALF], 100)
    z = m.at("op_z", [P, 4, HALF], 108)
    landed = [m.sem(f"op_w_landed{i}") for i in range(NH)]
    xl = [m.sem(f"op_x_landed{i}") for i in range(NH)]
    hi = m.sem("op_hi_done")
    lo = m.sem("op_lo_done")
    done = m.sem("op_done")
    gated = m.sem("op_gated")
    added = m.sem("op_added")
    stored = [m.sem(f"op_stored{i}") for i in range(4)]
    with nc.Block() as block:
        @block.sync
        def _(sp):
            for h in range(NH):
                cols = slice(h * HALF, (h + 1) * HALF)
                sp.dma_start(raw[:, h], a.w_out[0, :, cols].rearrange("(k p) n -> p k n", p=P)) \
                    .then_inc(landed[h], 16)
                if h:
                    sp.wait_ge(added, TT * h)
                sp.dma_start(xin[:], a.x[0, :, cols].rearrange("(i p) n -> p i n", p=P)).then_inc(xl[h], 16)

        @block.scalar
        def _(act):
            for h in range(NH):
                act.wait_ge(landed[h], 16)
                if h:
                    act.wait_ge(done, TT * h)
                for k in range(KT):
                    nc.scalar.activation(w_hi[:, k], raw[:, h, k], ACT.Copy).then_inc(hi, 1)

        @block.gpsimd
        def _(pool):
            for h in range(NH):
                for k in range(KT):
                    pool.wait_ge(hi, h * KT + k + 1)
                    nc.gpsimd.tensor_tensor(w_lo[:, k], raw[:, h, k], w_hi[:, k].bitcast(F32), ALU.subtract) \
                        .then_inc(lo, 1)
            for g in range(NH * TT):
                h, i = divmod(g, TT)
                pool.wait_ge(added, g + 1)
                pool.dma_start(t.x1[i * P:(i + 1) * P, h * HALF:(h + 1) * HALF], z[:, g % 4]) \
                    .then_inc(stored[g % 4], 16)
            for s in range(4):
                pool.wait_ge(stored[s], 16 * NH * TT // 4)

        @block.tensor
        def _(pe):
            for g in range(NH * TT):
                h, i = divmod(g, TT)
                pe.wait_ge(lo, KT * (h + 1))
                if g >= 8:
                    pe.wait_ge(gated, g - 7)
                rows = slice(i * P, (i + 1) * P)
                three_pass(nc, m.psum[:, g % 8], lambda k: t.mixT_hi[:, k, rows], lambda k: t.mixT_lo[:, k, rows],
                           lambda k: w_hi[:, k], lambda k: w_lo[:, k], KT).then_inc(done, 1)

        @block.vector
        def _(dve):
            for g in range(NH * TT):
                h, i = divmod(g, TT)
                dve.wait_ge(done, g + 1)
                if g >= 4:
                    dve.wait_ge(added, g - 3)
                nc.vector.tensor_tensor(y[:, g % 4], m.psum[:, g % 8], t.gate1[:, h * HALF:(h + 1) * HALF],
                                        ALU.mult).then_inc(gated, 1)
                dve.wait_ge(gated, g + 1)
                dve.wait_ge(xl[h], 16)
                if g >= 4:
                    dve.wait_ge(stored[g % 4], 16 * (g // 4))
                nc.vector.tensor_tensor(z[:, g % 4], y[:, g % 4], xin[:, i], ALU.add).then_inc(added, 1)


def steps(eng, first, count, unroll, body):
    for u in range(unroll):
        body(first + u, u)
    if count > 2 * unroll:
        with eng.Fori(1, count // unroll - 1) as i:
            for u in range(unroll):
                body(i * unroll + (first + u), u)
    for u in range(unroll):
        body(first + count - unroll + u, u)


def at_least(eng, sem, value):
    if not (isinstance(value, int) and value <= 0):
        eng.wait_ge(sem, value)


class Ahead:

    def __init__(self, nc, m, t, a, name, first, count):
        self.nc, self.m, self.t, self.a = nc, m, t, a
        self.first, self.count = first, count
        self.full = m.at(name + "downT", [P, D], 168)
        self.raw = m.at(name + "down", [P, 2, D], 172)
        self.hi = m.at(name + "downT_hi", [P, 2, KT, P], 180, F32R)
        self.lo = [m.at(name + "downT_lo0", [P, KT, P], 188, F32R), m.at(name + "downT_lo1", [P, KT, P], 15, F32R)]
        self.out = m.at(name + "gelu", [P, 2, S], 7)
        self.landed = [m.sem(f"{name}down_landed{i}") for i in range(2)]
        self.turned = m.sem(name + "turned")
        self.hi_done = m.sem(name + "downT_hi_done")
        self.lo_done = m.sem(name + "downT_lo_done")
        self.gelued = m.sem(name + "gelu_done")
        self.stored = [m.sem(f"{name}gelu_stored{i}") for i in range(2)]

    def load(self, sp, n, u):
        at_least(sp, self.turned, n - 1)
        e = n + self.first
        rows = slice(e * P, (e + 1) * P) if isinstance(e, int) else bass.ds(e * P, P)
        sp.dma_start(self.raw[:, u], self.a.expert_down[0, rows, :]).then_inc(self.landed[u], 16)

    def store(self, sp, n, u):
        sp.wait_ge(self.gelued, n * 2 + 2)
        e = n + self.first
        dst = self.t.gelus[e] if isinstance(e, int) else self.t.gelus[bass.ds(e, 1), :, :].rearrange("o p c -> (o p) c")
        sp.dma_start(dst, self.out[:, u]).then_inc(self.stored[u], 16)

    def turn(self, pe, n, u):
        pe.wait_ge(self.landed[u], (n - u) * 8 + 16)
        at_least(pe, self.lo_done, n)
        for k in range(KT):
            mm = self.nc.tensor.transpose(self.m.psum[:, 2 + k // 4, (k % 4) * P:(k % 4 + 1) * P],
                                          self.raw[:, u, k * P:(k + 1) * P], self.t.ident[:])
        mm.then_inc(self.turned, 1)

    def split(self, act, n, u):
        act.wait_ge(self.turned, n + 1)
        at_least(act, self.lo_done, n)
        turned = self.m.psum[:, 2:4].rearrange("p b n -> p (b n)")
        self.nc.scalar.activation(self.full[:], turned, ACT.Copy).then_inc(self.hi_done, 1)
        at_least(act, self.gelued, n * 2 - 2)
        self.nc.scalar.activation(self.hi[:, u].rearrange("p k n -> p (k n)"), turned, ACT.Copy) \
            .then_inc(self.hi_done, 1)

    def rest(self, pool, n, u):
        pool.wait_ge(self.hi_done, n * 2 + 2)
        self.nc.gpsimd.tensor_tensor(self.lo[u][:].rearrange("p k n -> p (k n)"), self.full[:],
                                     self.hi[:, u].rearrange("p k n -> p (k n)").bitcast(F32), ALU.subtract) \
            .then_inc(self.lo_done, 1)

    def product(self, out, u, h, k):
        cols = slice(h * HALF, (h + 1) * HALF)
        mm = self.nc.tensor.matmul
        mm(out, self.hi[:, u, k], self.t.hT_hi[:, k, cols], start=k == 0, stop=False)
        mm(out, self.hi[:, u, k], self.t.hT_lo[:, k, cols], start=False, stop=False)
        return mm(out, self.lo[u][:, k], self.t.hT_hi[:, k, cols], start=False, stop=k == KT - 1)

    def gelu(self, act, psum, n, u, h):
        if h == 0:
            at_least(act, self.stored[u], (n - u) * 8)
        self.nc.scalar.activation(self.out[:, u, h * HALF:(h + 1) * HALF], psum, ACT.Gelu) \
            .then_inc(self.gelued, 1)

    def finish(self, sp):
        for u in range(2):
            sp.wait_ge(self.stored[u], 16 * (self.count // 2))


AHEAD_HEADS = 2 * PEER_HEADS
AHEAD_ROUTING = AHEAD_HEADS + 4
AHEAD_TABLE = 32
AHEAD = AHEAD_ROUTING + AHEAD_TABLE


def routing(nc, m, t, a):
    ah = Ahead(nc, m, t, a, "ra_", 0, AHEAD_ROUTING)
    raw = m.at("r_raw", [P, 2, KT, P], 84)
    w_hi = m.at("r_hi", [P, 2, KT, P], 92, F32R)
    w_lo = m.at("r_lo", [P, 2, KT, P], 100, F32R)
    qT = m.at("r_qT", [P, 2, S], 108)
    knat = m.at("r_keys", [P, 2 * PEER_HEADS, HD], 116)
    kT = m.at("r_keysT", [P, PEER_HEADS, P], 120)
    left = m.at("r_left", [P, 4, P], 124)
    best = m.at("r_best", [P, 2, TT, 2, TOPK], 126)
    where = m.at("r_where", [P, 2, TT, 2, TOPK], 128, U32)
    cand = m.at("r_cand", [P, 2, TOPK * TOPK], 130)
    cleft = m.at("r_cand_left", [P, 2, TOPK * TOPK], 132)
    top = m.at("r_top", [P, 2, TT, TOPK], 134)
    pos = m.at("r_pos", [P, 2, TT, TOPK], 135, U32)
    ab = m.at("r_ab", [P, 2, P], 136, U32)
    abf = m.at("r_ab_float", [P, 2, P], 137)
    wf = m.at("r_where_float", [P, TT, 2, TOPK], 138)
    less = m.at("r_less", [P, TT, TOPK], 139)
    ex = m.at("r_exp", [P, TT, TOPK], 139.5)
    rsum = m.at("r_sum", [P, TT], 140)
    rinv = m.at("r_inv", [P, TT], 140.25)
    kst = m.at("r_keys_staged", [P, 2, P], 141)
    hot = m.at("r_hot", [P, 2, TT * TOPK, TOPK], 142)
    landed = [m.sem(f"r_w_landed{i}") for i in range(2)]
    keysl = m.sem("r_keys_landed")
    kturned = m.sem("r_keys_turned")
    kcopied = m.sem("r_keys_copied")
    kstaged = m.sem("r_keys_staged_done")
    hi = m.sem("r_hi_done")
    lo = m.sem("r_lo_done")
    produced = m.sem("r_produced")
    drained = m.sem("r_drained")
    scored = m.sem("r_scored")
    v1 = m.sem("r_first_values")
    x1 = m.sem("r_first_places")
    l1 = m.sem("r_left_made")
    v2 = m.sem("r_second_values")
    x2 = m.sem("r_second_places")
    cd = m.sem("r_cands")
    cv1 = m.sem("r_cand_first")
    cx1 = m.sem("r_cand_first_places")
    cl1 = m.sem("r_cand_left_made")
    cv2 = m.sem("r_cand_second")
    cx2 = m.sem("r_cand_second_places")
    ints = m.sem("r_ints")
    floats = m.sem("r_floats")
    lessd = m.sem("r_lessed")
    expd = m.sem("r_expd")
    sums = m.sem("r_sums")
    invd = m.sem("r_invd")
    hotd = m.sem("r_hotd")
    vald = m.sem("r_vald")
    outd = m.sem("r_outd")
    H = PEER_HEADS
    N = TT * TOPK
    PAIRS_T = TT // 2
    UNITS = 6
    END_UNIT = H * UNITS

    def score_at(i, s):
        return m.psum[:, 4 + 2 * ((i // 2) % 2) + s, (i % 2) * P:(i % 2 + 1) * P]

    def last(g):
        return isinstance(g, int) and g == H - 1

    with nc.Block() as block:
        @block.sync
        def _(sp):
            sp.dma_start(knat[:], a.sub_keys[0].rearrange("h s k d -> k (h s) d")).then_inc(keysl, 16)
            w_q = a.w_query[0].rearrange("(k p) (c n) -> c p k n", p=P, n=P)

            def load_w(g, u):
                at_least(sp, lo, g - 1)
                sp.dma_start(raw[:, u], w_q[g]).then_inc(landed[u], 16)

            def head(g, u):
                if not (isinstance(g, int) and g >= H - 2):
                    load_w(g + 2, u)
                ah.load(sp, g * 2 + 2, 0)
                ah.store(sp, g * 2, 0)
                ah.load(sp, g * 2 + 3, 1)
                ah.store(sp, g * 2 + 1, 1)
            load_w(0, 0)
            load_w(1, 1)
            ah.load(sp, 0, 0)
            ah.load(sp, 1, 1)
            steps(sp, 0, H, 2, head)
            for n in range(AHEAD_HEADS, AHEAD_ROUTING):
                if n + 2 < AHEAD_ROUTING:
                    ah.load(sp, n + 2, n % 2)
                ah.store(sp, n, n % 2)
            ah.finish(sp)

        @block.tensor
        def _(pe):
            pe.wait_ge(keysl, 16)
            for q in range(2):
                for i in range(4):
                    h = 4 * q + i
                    mm = nc.tensor.transpose(m.psum[:, 2 + q, i * P:(i + 1) * P],
                                             knat[:, 2 * h:2 * h + 2].rearrange("p s d -> p (s d)"), t.ident[:])
                mm.then_inc(kturned, 1)
            pe.wait_ge(kcopied, 2)

            def query(g, u, unit):
                pe.wait_ge(lo, g + 1)
                for h in range(NH):
                    at_least(pe, drained, unit + (h - 1))
                    cols = slice(h * HALF, (h + 1) * HALF)
                    three_pass(nc, m.psum[:, h], lambda k: w_hi[:, u, k], lambda k: w_lo[:, u, k],
                               lambda k: t.hT_hi[:, k, cols], lambda k: t.hT_lo[:, k, cols], KT) \
                        .then_inc(produced, 1)

            def ahead_half(n, u, h, unit):
                if h == 0:
                    pe.wait_ge(ah.lo_done, n + 1)
                pe.wait_ge(drained, unit - 1)
                for k in range(KT):
                    mm = ah.product(m.psum[:, h], u, h, k)
                mm.then_inc(produced, 1)

            def score(g, u, pair):
                if pair == 0:
                    pe.wait_ge(kstaged, g + 1)
                    pe.wait_ge(drained, g * UNITS + 2)
                if not (isinstance(g, int) and g == 0 and pair < 2):
                    pe.wait_ge(x1, g * 2 * TT + (4 * pair - 4))
                    pe.wait_ge(l1, g * 2 * TT + (4 * pair - 4))
                for i in (2 * pair, 2 * pair + 1):
                    for s in range(2):
                        rows = slice(s * HD, (s + 1) * HD)
                        mm = nc.tensor.matmul(score_at(i, s), qT[rows, u, i * P:(i + 1) * P], kst[rows, u],
                                              start=True, stop=True)
                mm.then_inc(scored, 1)

            def head(g, u):
                unit = g * UNITS + 2
                ah.turn(pe, g * 2 + 1, 1)
                score(g, u, 0)
                score(g, u, 1)
                ahead_half(g * 2, 0, 0, unit)
                score(g, u, 2)
                ahead_half(g * 2, 0, 1, unit + 1)
                ah.turn(pe, g * 2 + 2, 0)
                score(g, u, 3)
                ahead_half(g * 2 + 1, 1, 0, unit + 2)
                ahead_half(g * 2 + 1, 1, 1, unit + 3)
                if not last(g):
                    query(g + 1, 1 - u, unit + 4)
            query(0, 0, 0)
            ah.turn(pe, 0, 0)
            steps(pe, 0, H, 2, head)
            for n in range(AHEAD_HEADS, AHEAD_ROUTING):
                if n + 1 < AHEAD_ROUTING:
                    ah.turn(pe, n + 1, (n + 1) % 2)
                for h in range(NH):
                    ahead_half(n, n % 2, h, END_UNIT + NH * (n - AHEAD_HEADS) + h)

        @block.scalar
        def _(act):
            for q in range(2):
                act.wait_ge(kturned, q + 1)
                nc.scalar.activation(kT[:, 4 * q:4 * q + 4], m.psum[:, 2 + q].rearrange("p (h k) -> p h k", k=P),
                                     ACT.Copy).then_inc(kcopied, 1)

            def split(g, u, unit):
                act.wait_ge(landed[u], (g - u) * 8 + 16)
                at_least(act, produced, unit)
                nc.scalar.activation(w_hi[:, u], raw[:, u], ACT.Copy).then_inc(hi, 1)

            def queries(g, u, unit):
                if not (isinstance(g, int) and g < 2):
                    act.wait_ge(scored, g * PAIRS_T - PAIRS_T)
                hold(act, t)
                nc.scalar.activation(kst[:, u], kT[:, g], ACT.Copy).then_inc(kstaged, 1)
                for h in range(NH):
                    act.wait_ge(produced, unit + (h + 1))
                    nc.scalar.activation(qT[:, u, h * HALF:(h + 1) * HALF], m.psum[:, h], ACT.Copy) \
                        .then_inc(drained, 1)

            def gelu(n, u, h, unit):
                act.wait_ge(produced, unit + 1)
                ah.gelu(act, m.psum[:, h], n, u, h)
                act.wait_ge(ah.gelued, n * 2 + (h + 1))
                act.sem_inc(drained, 1)

            def softmax_exp(g):
                act.wait_ge(lessd, g + 1)
                nc.scalar.activation(ex[:], less[:], ACT.Exp).then_inc(expd, 1)

            def head(g, u):
                unit = g * UNITS + 2
                if not (isinstance(g, int) and g >= H - 2):
                    split(g + 2, u, unit)
                ah.split(act, g * 2 + 1, 1)
                gelu(g * 2, 0, 0, unit)
                gelu(g * 2, 0, 1, unit + 1)
                ah.split(act, g * 2 + 2, 0)
                gelu(g * 2 + 1, 1, 0, unit + 2)
                if not (isinstance(g, int) and g == 0):
                    softmax_exp(g - 1)
                gelu(g * 2 + 1, 1, 1, unit + 3)
                if not last(g):
                    queries(g + 1, 1 - u, unit + 4)
            act.wait_ge(kcopied, 2)
            split(0, 0, 0)
            split(1, 1, 0)
            queries(0, 0, 0)
            ah.split(act, 0, 0)
            steps(act, 0, H, 2, head)
            for n in range(AHEAD_HEADS, AHEAD_ROUTING):
                if n + 1 < AHEAD_ROUTING:
                    ah.split(act, n + 1, (n + 1) % 2)
                for h in range(NH):
                    gelu(n, n % 2, h, END_UNIT + NH * (n - AHEAD_HEADS) + h)
                    if n == AHEAD_ROUTING - 2 and h == 0:
                        softmax_exp(H - 1)

        @block.vector
        def _(dve):
            def held(g):
                if not isinstance(g, int):
                    hold(dve, t)

            def first_level(g, u, pair):
                jobs = [(i, s) for i in (2 * pair, 2 * pair + 1) for s in range(2)]

                def n(i, s):
                    return g * 2 * TT + (2 * i + s + 1)
                lf = {(i, s): left[:, 2 * (i % 2) + s] for i, s in jobs}
                if not (isinstance(g, int) and g < 2) and pair == 0:
                    dve.wait_ge(outd, g * 3 - 3)
                for i, s in jobs:
                    if s == 0 and i % 2 == 0:
                        dve.wait_ge(scored, g * PAIRS_T + (pair + 1))
                        held(g)
                    nc.vector.max(best[:, u, i, s, 0:8], score_at(i, s)).then_inc(v1, 1)
                for i, s in jobs:
                    dve.wait_ge(v1, n(i, s))
                    held(g)
                    nc.vector.max_index(where[:, u, i, s, 0:8], best[:, u, i, s, 0:8], score_at(i, s)) \
                        .then_inc(x1, 1)
                for i, s in jobs:
                    if not (isinstance(g, int) and g == 0 and pair == 0):
                        dve.wait_ge(x2, n(i, s) - 4)
                        held(g)
                    nc.vector.match_replace(lf[i, s], best[:, u, i, s, 0:8], score_at(i, s), TAKEN).then_inc(l1, 1)
                for i, s in jobs:
                    dve.wait_ge(l1, n(i, s))
                    held(g)
                    nc.vector.max(best[:, u, i, s, 8:16], lf[i, s]).then_inc(v2, 1)
                for i, s in jobs:
                    dve.wait_ge(v2, n(i, s))
                    held(g)
                    nc.vector.max_index(where[:, u, i, s, 8:16], best[:, u, i, s, 8:16], lf[i, s]).then_inc(x2, 1)

            def second_level(g, u, pair):
                tiles = (2 * pair, 2 * pair + 1)

                def n(i):
                    return g * TT + (i + 1)
                dve.wait_ge(v2, g * 2 * TT + (4 * pair + 4))
                for i in tiles:
                    if not (isinstance(g, int) and g == 0 and pair == 0):
                        dve.wait_ge(cl1, n(i) - 2)
                        dve.wait_ge(cx1, n(i) - 2)
                    s1 = best[:, u, i, 0, :].unsqueeze(2).to_broadcast([P, TOPK, TOPK])
                    s2 = best[:, u, i, 1, :].unsqueeze(1).to_broadcast([P, TOPK, TOPK])
                    nc.vector.tensor_tensor(cand[:, i % 2].rearrange("p (x y) -> p x y", y=TOPK), s1, s2,
                                            ALU.add).then_inc(cd, 1)
                for i in tiles:
                    dve.wait_ge(cd, n(i))
                    held(g)
                    nc.vector.max(top[:, u, i, 0:8], cand[:, i % 2]).then_inc(cv1, 1)
                for i in tiles:
                    dve.wait_ge(cv1, n(i))
                    held(g)
                    nc.vector.max_index(pos[:, u, i, 0:8], top[:, u, i, 0:8], cand[:, i % 2]).then_inc(cx1, 1)
                for i in tiles:
                    if not (isinstance(g, int) and g == 0 and pair == 0):
                        dve.wait_ge(cx2, n(i) - 2)
                        held(g)
                    nc.vector.match_replace(cleft[:, i % 2], top[:, u, i, 0:8], cand[:, i % 2], TAKEN) \
                        .then_inc(cl1, 1)
                for i in tiles:
                    dve.wait_ge(cl1, n(i))
                    held(g)
                    nc.vector.max(top[:, u, i, 8:16], cleft[:, i % 2]).then_inc(cv2, 1)
                for i in tiles:
                    dve.wait_ge(cv2, n(i))
                    held(g)
                    nc.vector.max_index(pos[:, u, i, 8:16], top[:, u, i, 8:16], cleft[:, i % 2]).then_inc(cx2, 1)

            def places(g, u):
                dve.wait_ge(cv2, g * TT + TT)
                nc.vector.tensor_tensor(less[:], top[:, u], top[:, u, :, 0:1].to_broadcast([P, TT, TOPK]),
                                        ALU.subtract).then_inc(lessd, 1)
                dve.wait_ge(cx2, g * TT + TT)
                flatpos = pos[:, u].rearrange("p i k -> p (i k)")
                nc.vector.tensor_scalar(ab[:, 0], flatpos, 4, None, ALU.logical_shift_right).then_inc(ints, 1)
                nc.vector.tensor_scalar(ab[:, 1], flatpos, 15, None, ALU.bitwise_and).then_inc(ints, 1)
                dve.wait_ge(x2, g * 2 * TT + 2 * TT)
                nc.vector.tensor_copy(wf[:], where[:, u]).then_inc(floats, 1)
                dve.wait_ge(ints, g * 2 + 2)
                nc.vector.tensor_copy(abf[:], ab[:]).then_inc(floats, 1)
                dve.wait_ge(floats, g * 2 + 2)
                for s in range(2):
                    row = t.iota[:, 0:TOPK].unsqueeze(1).to_broadcast([P, N, TOPK])
                    mine = abf[:, s].unsqueeze(2).to_broadcast([P, N, TOPK])
                    nc.vector.tensor_tensor(hot[:, s], mine, row, ALU.is_equal).then_inc(hotd, 1)

            def results(g):
                dve.wait_ge(expd, g + 1)
                nc.vector.tensor_reduce(rsum[:], ex[:], AX.X, ALU.add).then_inc(sums, 1)
                dve.wait_ge(sums, g + 1)
                nc.vector.reciprocal(rinv[:], rsum[:]).then_inc(invd, 1)
                dve.wait_ge(invd, g + 1)
                nc.vector.tensor_tensor(t.route[:, 2, :, bass.ds(g * TOPK, TOPK)], ex[:],
                                        rinv[:].unsqueeze(2).to_broadcast([P, TT, TOPK]), ALU.mult) \
                    .then_inc(outd, 1)
                for s in range(2):
                    dve.wait_ge(vald, g * 2 + (s + 1))
                    nc.vector.tensor_reduce(t.route[:, s, :, bass.ds(g * TOPK, TOPK)],
                                            hot[:, s].rearrange("p (i k) j -> p i k j", k=TOPK), AX.X, ALU.add) \
                        .then_inc(outd, 1)

            def head(g, u):
                before = not (isinstance(g, int) and g == 0)
                first_level(g, u, 0)
                first_level(g, u, 1)
                second_level(g, u, 0)
                if before:
                    places(g - 1, 1 - u)
                first_level(g, u, 2)
                second_level(g, u, 1)
                first_level(g, u, 3)
                second_level(g, u, 2)
                if before:
                    results(g - 1)
                second_level(g, u, 3)
            steps(dve, 0, H, 2, head)
            places(H - 1, (H - 1) % 2)
            results(H - 1)

        @block.gpsimd
        def _(pool):
            def rest(g, u):
                pool.wait_ge(hi, g + 1)
                nc.gpsimd.tensor_tensor(w_lo[:, u], raw[:, u], w_hi[:, u].bitcast(F32), ALU.subtract) \
                    .then_inc(lo, 1)

            def chosen(g):
                for s in range(2):
                    pool.wait_ge(hotd, g * 2 + (s + 1))
                    lists = wf[:, :, s, :].unsqueeze(2).to_broadcast([P, TT, TOPK, TOPK])
                    both = hot[:, s].rearrange("p (i k) j -> p i k j", k=TOPK)
                    nc.gpsimd.tensor_tensor(both, both, lists, ALU.mult).then_inc(vald, 1)

            def head(g, u):
                ah.rest(pool, g * 2 + 1, 1)
                if not (isinstance(g, int) and g >= H - 2):
                    rest(g + 2, u)
                ah.rest(pool, g * 2 + 2, 0)
                if not (isinstance(g, int) and g == 0):
                    chosen(g - 1)
            rest(0, 0)
            rest(1, 1)
            ah.rest(pool, 0, 0)
            steps(pool, 0, H, 2, head)
            for n in range(AHEAD_HEADS + 1, AHEAD_ROUTING):
                ah.rest(pool, n, n % 2)
            chosen(H - 1)


def gate_table(nc, m, t, a):
    ah = Ahead(nc, m, t, a, "ga_", AHEAD_ROUTING, AHEAD_TABLE)
    TB = TABLE_TOKENS
    GT = 4
    STEPS = AHEAD_TABLE
    GS = S // GT // STEPS
    BS = TB // GT // GS
    out = m.at("g_table", [P, 2, P, TB], 84)
    rT = m.at("g_routeT", [P, 3, S], 148)
    g_hi = m.at("g_hi", [P, S], 160, F32R)
    g_lo = m.at("g_lo", [P, S], 164, F32R)
    hot = m.at("g_hot", [P, 2, 3, GT, P], 192, F32R)
    hot1 = m.at("g_hot1", [P, 2, GT, P], 204, BF16)
    turned = m.sem("g_turned")
    copied = m.sem("g_copied")
    hi = m.sem("g_hi_done")
    lo = m.sem("g_lo_done")
    hot1_d = m.sem("g_hot1_done")
    hot_d = m.sem("g_hot_done")
    hot_hi_d = m.sem("g_hot_hi_done")
    hotlo_d = m.sem("g_hotlo_done")
    done = m.sem("g_done")
    out_s = m.sem("g_out")
    a_done = m.sem("g_ahead_done")
    stored = t.table_stored

    def last(n):
        return isinstance(n, int) and n == STEPS - 1

    def cols(x, tok, n):
        return x[:, tok:tok + n] if isinstance(tok, int) else x[:, bass.ds(tok, n)]

    with nc.Block() as block:
        @block.tensor
        def _(pe):
            for x in range(6):
                c, h = divmod(x, NH)
                if x >= 4:
                    pe.wait_ge(copied, x - 3)
                for i in range(4):
                    mm = nc.tensor.transpose(m.psum[:, 4 + x % 4, i * P:(i + 1) * P], t.route[:, c, 4 * h + i],
                                             t.ident[:])
                mm.then_inc(turned, 1)
            ah.turn(pe, 0, 0)
            pe.wait_ge(copied, 6)

            def group(g, y):
                pe.wait_ge(hot_hi_d, g + 1)
                pe.wait_ge(hotlo_d, g + 1)
                at_least(pe, out_s, g - 3)
                for c in range(GT):
                    o = m.psum[:, 4 + y % 4, c * P:(c + 1) * P]
                    nc.tensor.matmul(o, hot[:, y % 2, 0, c], hot[:, y % 2, 1, c], start=True, stop=False)
                    mm = nc.tensor.matmul(o, hot[:, y % 2, 0, c], hot[:, y % 2, 2, c], start=False, stop=True)
                mm.then_inc(done, 1)

            def step(n, u):
                if not last(n):
                    ah.turn(pe, n + 1, 1 - u)
                pe.wait_ge(ah.lo_done, n + 1)
                for h in range(NH):
                    at_least(pe, ah.gelued, n * 2 + (h - 1))
                    for k in range(KT):
                        mm = ah.product(m.psum[:, h], u, h, k)
                        if k == KT - 1:
                            mm.then_inc(a_done, 1)
                        if k % 2:
                            y = h * 4 + k // 2
                            group(n * GS + y, y)
            steps(pe, 0, STEPS, 2, step)

        @block.vector
        def _(dve):
            for x in range(6):
                c, h = divmod(x, NH)
                dve.wait_ge(turned, x + 1)
                nc.vector.tensor_copy(rT[:, c, h * HALF:(h + 1) * HALF], m.psum[:, 4 + x % 4]).then_inc(copied, 1)
            dve.wait_ge(hi, 1)
            nc.vector.tensor_tensor(g_lo[:], rT[:, 2], g_hi[:].bitcast(F32), ALU.subtract).then_inc(lo, 1)

            def one_hots(g, y):
                row = t.iota[:].unsqueeze(1).to_broadcast([P, GT, P])
                tok = g * GT
                at_least(dve, hotlo_d, g - 1)
                nc.vector.tensor_tensor(hot1[:, y % 2], row,
                                        cols(rT[:, 0], tok, GT).unsqueeze(2).to_broadcast([P, GT, P]),
                                        ALU.is_equal).then_inc(hot1_d, 1)
                at_least(dve, done, g - 1)
                nc.vector.tensor_tensor(hot[:, y % 2, 0], row,
                                        cols(rT[:, 1], tok, GT).unsqueeze(2).to_broadcast([P, GT, P]),
                                        ALU.is_equal).then_inc(hot_d, 1)

            def step(n, u):
                for y in range(GS):
                    g = n * GS + y
                    dve.wait_ge(hot1_d, g + 1)
                    nc.vector.tensor_tensor(hot[:, y % 2, 1], hot1[:, y % 2],
                                            cols(g_hi[:].bitcast(F32), g * GT, GT).unsqueeze(2)
                                            .to_broadcast([P, GT, P]), ALU.mult).then_inc(hot_hi_d, 1)
                    if not (last(n) and y == GS - 1):
                        one_hots(g + 1, y + 1)
            one_hots(0, 0)
            steps(dve, 0, STEPS, 2, step)

        @block.gpsimd
        def _(pool):
            ah.rest(pool, 0, 0)
            pool.wait_ge(lo, 1)

            def step(n, u):
                for y in range(GS):
                    g = n * GS + y
                    pool.wait_ge(hot1_d, g + 1)
                    at_least(pool, done, g - 1)
                    if not isinstance(g, int):
                        hold(pool, t)
                    nc.gpsimd.tensor_tensor(hot[:, y % 2, 2], hot1[:, y % 2],
                                            cols(g_lo[:].bitcast(F32), g * GT, GT).unsqueeze(2)
                                            .to_broadcast([P, GT, P]), ALU.mult).then_inc(hotlo_d, 1)
                    if y == 3 and not last(n):
                        ah.rest(pool, n + 1, 1 - u)
            steps(pool, 0, STEPS, 2, step)

        @block.scalar
        def _(act):
            ah.split(act, 0, 0)
            act.wait_ge(copied, 6)
            nc.scalar.activation(g_hi[:], rT[:, 2], ACT.Copy).then_inc(hi, 1)

            def step(n, q):
                u, buf = q % 2, q // BS
                if q % BS == 0:
                    at_least(act, stored[buf], (n - q) * (16 // (2 * BS)))
                for y in range(GS):
                    g = n * GS + y
                    act.wait_ge(done, g + 1)
                    tok = (q % BS) * GS * GT + y * GT
                    nc.scalar.activation(out[:, buf, :, tok:tok + GT],
                                         m.psum[:, 4 + y % 4].rearrange("p (c e) -> p e c", e=P), ACT.Copy) \
                        .then_inc(out_s, 1)
                    if y == 1 and not last(n):
                        ah.split(act, n + 1, 1 - u)
                    if y % 4 == 3:
                        act.wait_ge(a_done, n * 2 + (y // 4 + 1))
                        ah.gelu(act, m.psum[:, y // 4], n, u, y // 4)
            steps(act, 0, STEPS, 2 * BS, step)

        @block.sync
        def _(sp):
            def step(n, q):
                u, buf = q % 2, q // BS
                if not (isinstance(n, int) and n >= STEPS - 2):
                    ah.load(sp, n + 2, u)
                ah.store(sp, n, u)
                if q % BS == BS - 1:
                    sp.wait_ge(out_s, n * GS + GS)
                    tok = (n + 1) * (GS * GT) - TB
                    words = slice(tok * P, (tok + TB) * P) if isinstance(tok, int) else bass.ds(tok * P, TB * P)
                    sp.dma_start(t.table[:, words], out[:, buf].rearrange("p e c -> p (e c)")) \
                        .then_inc(stored[buf], 16)
            ah.load(sp, 0, 0)
            ah.load(sp, 1, 1)
            steps(sp, 0, STEPS, 2 * BS, step)
            ah.finish(sp)


def experts(nc, m, t, a):
    acc = t.acc
    W_hi = m.at("e_w_hi", [P, 4, S], 116, F32R)
    W_lo = m.at("e_w_lo", [P, 4, S], 132, F32R)
    U_hi = m.at("e_u_hi", [P, 4, D], 148, F32R)
    U_lo = m.at("e_u_lo", [P, 4, D], 164, F32R)
    left = m.at("e_left", [P, 2, D], 180)
    DT_hi = m.at("e_downT_hi", [P, KT, P], 188, F32R)
    DT_lo = m.at("e_downT_lo", [P, KT, P], 192, F32R)
    Uraw = m.at("e_up", [P, 2, D], 196)
    Gc = m.at("e_table", [P, 2, S], 7)
    Wg = m.at("e_gelu", [P, S], 15)
    l_land = [m.sem(f"e_left_landed{i}") for i in range(2)]
    u_land = [m.sem(f"e_up_landed{i}") for i in range(2)]
    g_land = [m.sem(f"e_table_landed{i}") for i in range(2)]
    turned = m.sem("e_turned")
    dt_hi = m.sem("e_dt_hi")
    dt_lo = m.sem("e_dt_lo")
    a_done = m.sem("e_a_done")
    gelu = m.sem("e_gelu_done")
    mul = m.sem("e_mul")
    w_hi = m.sem("e_w_hi_done")
    w_lo = m.sem("e_w_lo_done")
    u_hi = m.sem("e_u_hi_done")
    u_lo = m.sem("e_u_lo_done")
    b_grp = m.sem("e_b_group")
    acc_d = m.sem("e_acc")
    NG = N_CHUNKS
    GROUPS = 16

    FRESH = NG - AHEAD

    def both(eng, body):
        steps(eng, 0, FRESH, 4, lambda g, q: body(g, q, False))
        steps(eng, FRESH, AHEAD, 4, lambda g, q: body(g, q, True))

    def chunk(g, ahead):
        return g - FRESH if ahead else g + AHEAD

    def next_turns(g, ahead):
        return not ahead and not (isinstance(g, int) and g == FRESH - 1)

    with nc.Block() as block:
        @block.sync
        def _(sp):
            def rows(src, g):
                return src[0, g * P:(g + 1) * P, :] if isinstance(g, int) else src[0, bass.ds(g * P, P), :]

            def plane(src, g):
                return src[g] if isinstance(g, int) else src[bass.ds(g, 1), :, :].rearrange("o p c -> (o p) c")

            def load_left(g, u, ahead):
                if ahead and not (isinstance(g, int) and g < FRESH + 2):
                    sp.wait_ge(mul, g * 2 - 2)
                else:
                    at_least(sp, turned, g - 1)
                src = plane(t.gelus, chunk(g, True)) if ahead else rows(a.expert_down, chunk(g, False))
                sp.dma_start(left[:, u], src).then_inc(l_land[u], 16)

            def load_up(g, u, ahead):
                at_least(sp, u_lo, g - 1)
                sp.dma_start(Uraw[:, u], rows(a.expert_up, chunk(g, ahead))).then_inc(u_land[u], 16)

            def load_table(g, u, ahead):
                at_least(sp, w_lo, g - 1)
                blocks = t.table.rearrange("p (b e c) -> p b e c", e=N_CHUNKS, c=TABLE_TOKENS)
                c = chunk(g, ahead)
                part = blocks[:, :, c] if isinstance(c, int) else \
                    blocks[:, :, bass.ds(c, 1)].rearrange("p b o c -> p b (o c)")
                sp.dma_start(Gc[:, u].rearrange("p (b c) -> p b c", c=TABLE_TOKENS), part).then_inc(g_land[u], 16)

            def step(g, q, ahead):
                u = q % 2
                if not (isinstance(g, int) and g == NG - 1):
                    load_left(g + 1, 1 - u, ahead or (isinstance(g, int) and g == FRESH - 1))
                if isinstance(g, int) and g == 0:
                    load_up(g, u, ahead)
                    for buf in range(2):
                        sp.wait_ge(t.table_stored[buf], 16 * S // TABLE_TOKENS // 2)
                    load_table(g, u, ahead)
                else:
                    load_table(g, u, ahead)
                    load_up(g, u, ahead)
            load_left(0, 0, False)
            both(sp, step)

        @block.tensor
        def _(pe):
            def turn(g, u):
                pe.wait_ge(l_land[u], (g - u) * 8 + 16)
                for k in range(KT):
                    mm = nc.tensor.transpose(m.psum[:, 2 + k // 4, (k % 4) * P:(k % 4 + 1) * P],
                                             left[:, u, k * P:(k + 1) * P], t.ident[:])
                mm.then_inc(turned, 1)

            def activations(g):
                pe.wait_ge(dt_lo, g + 1)
                for h in range(NH):
                    at_least(pe, gelu, g * 2 + (h - 1))
                    cols = slice(h * HALF, (h + 1) * HALF)
                    three_pass(nc, m.psum[:, h], lambda k: DT_hi[:, k], lambda k: DT_lo[:, k],
                               lambda k: t.hT_hi[:, k, cols], lambda k: t.hT_lo[:, k, cols], KT) \
                        .then_inc(a_done, 1)

            def up_part(g, q):
                c, pair = q % 2, 2 * ((q // 2) ^ 1)
                pe.wait_ge(w_lo, g - c)
                pe.wait_ge(u_lo, g - c)
                for j in range(8 * c, 8 * c + 8):
                    at_least(pe, acc_d, g * 8 + (j - 3 - 8 * (c + 2)))
                    rows = slice((j // 2) * P, (j // 2 + 1) * P)
                    cols = slice((j % 2) * HALF, (j % 2 + 1) * HALF)
                    three_pass(nc, m.psum[:, 4 + j % 4], lambda k: W_hi[:, pair + k, rows],
                               lambda k: W_lo[:, pair + k, rows], lambda k: U_hi[:, pair + k, cols],
                               lambda k: U_lo[:, pair + k, cols], 2).then_inc(b_grp, 1)

            def step(g, q, ahead):
                if not ahead:
                    activations(g)
                if next_turns(g, ahead):
                    turn(g + 1, (q + 1) % 2)
                if not (isinstance(g, int) and g < 2):
                    up_part(g, q)
            turn(0, 0)
            both(pe, step)
            up_part(NG, 0)
            up_part(NG + 1, 1)

        @block.scalar
        def _(act):
            def downT(g):
                act.wait_ge(turned, g + 1)
                at_least(act, a_done, g * 2)
                nc.scalar.activation(DT_hi[:].rearrange("p k n -> p (k n)"),
                                     m.psum[:, 2:4].rearrange("p b n -> p (b n)"), ACT.Copy).then_inc(dt_hi, 1)

            def step(g, q, ahead):
                if not ahead:
                    for h in range(NH):
                        act.wait_ge(a_done, g * 2 + (h + 1))
                        at_least(act, mul, g * 2 + (h - 1))
                        nc.scalar.activation(Wg[:, h * HALF:(h + 1) * HALF], m.psum[:, h], ACT.Gelu) \
                            .then_inc(gelu, 1)
                if next_turns(g, ahead):
                    downT(g + 1)
                act.wait_ge(mul, g * 2 + 2)
                if not (isinstance(g, int) and g < 4):
                    act.wait_ge(b_grp, g * 8 - 8 * (q % 2 + 2))
                nc.scalar.activation(W_hi[:, q], Gc[:, q % 2], ACT.Copy).then_inc(w_hi, 1)
                act.wait_ge(u_land[q % 2], (g - q % 2) * 8 + 16)
                nc.scalar.activation(U_hi[:, q], Uraw[:, q % 2], ACT.Copy).then_inc(u_hi, 1)
            downT(0)
            both(act, step)

        @block.vector
        def _(dve):
            def downT(g):
                dve.wait_ge(dt_hi, g + 1)
                nc.vector.tensor_tensor(DT_lo[:].rearrange("p k n -> p (k n)"),
                                        m.psum[:, 2:4].rearrange("p b n -> p (b n)"),
                                        DT_hi[:].rearrange("p k n -> p (k n)").bitcast(F32),
                                        ALU.subtract).then_inc(dt_lo, 1)

            def add_part(g, q):
                c = q % 2
                for j in range(8 * c, 8 * c + 8):
                    J = g * 8 + (j - 8 * (c + 2))
                    dve.wait_ge(b_grp, J + 1)
                    at_least(dve, acc_d, J - (GROUPS - 1))
                    out = acc[:, j // 2, (j % 2) * HALF:(j % 2 + 1) * HALF]
                    if isinstance(g, int) and g < 4:
                        nc.vector.tensor_copy(out, m.psum[:, 4 + j % 4]).then_inc(acc_d, 1)
                    else:
                        nc.vector.tensor_tensor(out, out, m.psum[:, 4 + j % 4], ALU.add).then_inc(acc_d, 1)

            def step(g, q, ahead):
                u = q % 2
                dve.wait_ge(g_land[u], (g - u) * 8 + 16)
                if ahead:
                    dve.wait_ge(l_land[u], (g - u) * 8 + 16)
                for h in range(NH):
                    if not ahead:
                        dve.wait_ge(gelu, g * 2 + (h + 1))
                    cols = slice(h * HALF, (h + 1) * HALF)
                    act_out = left[:, u, cols] if ahead else Wg[:, cols]
                    nc.vector.tensor_tensor(Gc[:, u, cols], act_out, Gc[:, u, cols], ALU.mult).then_inc(mul, 1)
                if next_turns(g, ahead):
                    downT(g + 1)
                if not (isinstance(g, int) and g < 2):
                    add_part(g, q)
            downT(0)
            both(dve, step)
            add_part(NG, 0)
            add_part(NG + 1, 1)

        @block.gpsimd
        def _(pool):
            def step(g, q, ahead):
                pool.wait_ge(w_hi, g + 1)
                nc.gpsimd.tensor_tensor(W_lo[:, q], Gc[:, q % 2], W_hi[:, q].bitcast(F32), ALU.subtract) \
                    .then_inc(w_lo, 1)
                pool.wait_ge(u_hi, g + 1)
                nc.gpsimd.tensor_tensor(U_lo[:, q], Uraw[:, q % 2], U_hi[:, q].bitcast(F32), ALU.subtract) \
                    .then_inc(u_lo, 1)
            both(pool, step)


def final(nc, m, t, a, out):
    xin = m.at("f_x", [P, 4, D], 20)
    prod = m.at("f_prod", [P, 2, D], 36)
    junk = m.at("f_junk", [P, 2, D], 44)
    res = m.at("f_out", [P, 2, D], 52)
    gf = m.at("f_gain", [P, D], 60)
    ssq = m.at("f_ssq", [P, TT], 64)
    mean = m.at("f_mean", [P, TT], 64.25)
    std = m.at("f_std", [P, TT], 64.5)
    rstd = m.at("f_rstd", [P, TT], 64.75)
    landed = [m.sem(f"f_landed{i}") for i in range(4)]
    gl = m.sem("f_gain_landed")
    gated = m.sem("f_gated")
    added = m.sem("f_added")
    squared = m.sem("f_squared")
    meand = m.sem("f_meaned")
    root = m.sem("f_root")
    inv = m.sem("f_inv")
    ready = m.sem("f_ready")
    stored = [m.sem(f"f_stored{i}") for i in range(2)]
    with nc.Block() as block:
        @block.sync
        def _(sp):
            sp.dma_start(gf[:], a.final_norm_g.rearrange("(o d) -> o d", o=1).partition_broadcast(P)) \
                .then_inc(gl, 16)
            for i in range(TT):
                if i >= 4:
                    sp.wait_ge(added, i - 3)
                sp.dma_start(xin[:, i % 4], t.x1[i * P:(i + 1) * P, :]).then_inc(landed[i % 4], 16)
            for i in range(TT):
                sp.wait_ge(ready, i + 1)
                sp.dma_start(out[0, i * P:(i + 1) * P, :], res[:, i % 2]).then_inc(stored[i % 2], 16)
            for s in range(2):
                sp.wait_ge(stored[s], 16 * TT // 2)

        @block.scalar
        def _(act):
            for i in range(TT):
                act.wait_ge(added, i + 1)
                if i >= 2:
                    act.wait_ge(squared, i - 1)
                nc.scalar.activation(junk[:, i % 2], t.acc[:, i], ACT.Square, accum_out=ssq[:, i:i + 1]) \
                    .then_inc(squared, 1)
            act.wait_ge(meand, 1)
            nc.scalar.activation(std[:], mean[:], ACT.Sqrt).then_inc(root, 1)

        @block.vector
        def _(dve):
            for i in range(TT):
                if i >= 2:
                    dve.wait_ge(added, i - 1)
                nc.vector.tensor_tensor(prod[:, i % 2], t.acc[:, i], t.gate2[:], ALU.mult).then_inc(gated, 1)
                dve.wait_ge(gated, i + 1)
                dve.wait_ge(landed[i % 4], 16 * (i // 4 + 1))
                nc.vector.tensor_tensor(t.acc[:, i], prod[:, i % 2], xin[:, i % 4], ALU.add).then_inc(added, 1)
            dve.wait_ge(squared, TT)
            nc.vector.tensor_scalar(mean[:], ssq[:], 1.0 / D, EPS, ALU.mult, ALU.add).then_inc(meand, 1)
            dve.wait_ge(root, 1)
            nc.vector.reciprocal(rstd[:], std[:]).then_inc(inv, 1)
            dve.wait_ge(inv, 1)
            dve.wait_ge(gl, 16)
            for i in range(TT):
                if i >= 2:
                    dve.wait_ge(stored[i % 2], 16 * (i // 2))
                nc.vector.scalar_tensor_tensor(out=res[:, i % 2], in0=t.acc[:, i], scalar=rstd[:, i:i + 1],
                                               in1=gf[:], op0=ALU.mult, op1=ALU.mult).then_inc(ready, 1)


class Arrays:

    def __init__(self, args, line_const):
        self.x = args["x"]
        self.c = args["c"]
        self.norm_mix_g = args["norm_mix_g"]
        self.norm_ffn_g = args["norm_ffn_g"]
        self.w_ada = args["w_ada"]
        self.b_ada = args["b_ada"]
        self.w_in = args["w_in"]
        self.b_forget = args["b_forget"]
        self.sinks = args["sinks"]
        self.w_branch_a = args["w_branch_a"]
        self.w_branch_b = args["w_branch_b"]
        self.w_out = args["w_out"]
        self.rel_bias = args["rel_bias"]
        self.w_query = args["w_query"]
        self.sub_keys = args["sub_keys"]
        self.expert_down = args["expert_down"]
        self.expert_up = args["expert_up"]
        self.final_norm_g = args["final_norm_g"]
        self.line_const = line_const


class Tensors:
    pass


def build(nc, args, line_const, out):
    a = Arrays(args, line_const)
    with ExitStack() as ctx:
        m = Memory(nc, ctx)
        t = Tensors()
        t.passed = m.sem("passed_waits")
        t.table_stored = [m.sem(f"table_stored{i}") for i in range(2)]
        t.ident = m.at("ident", [P, P], 0)
        t.ones = m.at("ones", [P, P], 0.5)
        t.iota = m.at("iota", [P, P], 1)
        t.mask = m.at("mask", [P, P], 1.5)
        t.cols = m.at("cols", [P, 9 * KT], 2)
        t.ccol = t.cols[:, 0:KT]
        t.bcol = t.cols[:, KT:7 * KT]
        t.gcol = t.cols[:, 7 * KT:9 * KT].rearrange("p (n k) -> p n k", k=KT)
        t.cact = m.at("cact", [P, KT], 2.3125)
        t.shift = m.at("shift", [P, 2, KT], 2.5)
        t.gain = m.at("gain", [P, 2, KT], 2.625)
        t.negsink = m.at("negsink", [P, FOX_HEADS], 2.75)
        t.bfl = m.at("bfl", [FOX_HEADS, 1], 2.8125)
        t.gate2 = m.at("gate2", [P, D], 3)
        t.gate1 = m.at("gate1", [P, D], 7)
        t.negF = m.at("negF", [FOX_HEADS, S], 15)
        t.hT_hi = m.at("hT_hi", [P, KT, S], 20, F32R)
        t.hT_lo = m.at("hT_lo", [P, KT, S], 52, F32R)
        t.qkvT = m.at("qkvT", [P, QKV_CHUNKS, S], 84)
        t.v = m.at("v", [P, TT, 5 * P], 156)
        t.kdup = m.at("kdup", [P, 2, S], 68)
        t.band = m.at("band", [P, FOX_HEADS, 2 * P], 76)
        t.o = m.at("o", [P, 2, TT, HALF], 20)
        t.mixT_hi = m.at("mixT_hi", [P, KT, S], 116, F32R)
        t.mixT_lo = m.at("mixT_lo", [P, KT, S], 148, F32R)
        t.route = m.at("route", [P, 3, TT, P], 192)
        t.acc = m.at("acc", [P, TT, D], 84)
        t.gates = m.dram("gates", [2 * KT, P, S])
        t.line_dram = m.dram("bias_line", [FOX_HEADS, P, LINE])
        t.negf_dram = m.dram("negf_rows", [FOX_HEADS, S])
        t.x1 = m.dram("x1", [S, D])
        t.gelus = m.dram("gelus_ahead", [AHEAD, P, S])
        t.table = m.dram("gate_table", [P, S // TABLE_TOKENS * N_CHUNKS * TABLE_TOKENS])

        m.stage(constants, t)
        m.stage(modulation, t, a)
        m.stage(norm, t, 0, a.x[0])
        m.stage(projections, t, a)
        m.stage(values, t, a)
        m.stage(attention, t)
        m.stage(mixing, t, a)
        m.stage(out_projection, t, a)
        m.stage(norm, t, 1, t.x1)
        m.stage(routing, t, a)
        m.stage(gate_table, t, a)
        m.stage(experts, t, a)
        m.stage(final, t, a, out)


_INS = ["x", "c", "norm_mix_g", "norm_ffn_g", "w_ada", "b_ada", "w_in", "b_forget", "sinks", "w_branch_a",
        "w_branch_b", "w_out", "rel_bias", "w_query", "sub_keys", "expert_down", "expert_up", "final_norm_g"]


def kernel(**inputs):
    import numpy as _np
    import concourse.bacc as _bacc
    from concourse import mybir as _mybir
    from concourse.bass_utils import run_bass_kernel_spmd as _run

    nc = _bacc.Bacc("TRN2", target_bir_lowering=False, num_devices=1)
    arrays, args = {}, {}
    for name in _INS:
        arr = _np.ascontiguousarray(inputs[name])
        arrays[f"in_{name}"] = arr
        args[name] = nc.dram_tensor(f"in_{name}", arr.shape, _mybir.dt.from_np(arr.dtype),
                                    kind="ExternalInput").ap()
    line = line_constants()
    arrays["line_const"] = line
    lc = nc.dram_tensor("line_const", line.shape, _mybir.dt.float32, kind="ExternalInput").ap()
    out = nc.dram_tensor("out", (1, S, D), _mybir.dt.float32, kind="ExternalOutput").ap()
    build(nc, args, lc, out)
    r = _run(nc, [arrays], core_ids=[0])
    return r.results[0]["out"]
```

```python
from contextlib import ExitStack

import numpy as np

import concourse.bass as bass
from concourse import mybir

F32 = mybir.dt.float32
F32R = mybir.dt.float32r
U32 = mybir.dt.uint32
BF16 = mybir.dt.bfloat16
ALU = mybir.AluOpType
ACT = mybir.ActivationFunctionType
AX = mybir.AxisListType

P = 128
D = 1024
KT = D // P
S = 1024
TT = S // P
HALF = 512
NH = S // HALF
HD = 64
QKV_CHUNKS = 18
FL_COL = 2304
GATE_COL = 2312
FOX_HEADS = 8
PAIRS = 4
WINDOW = 128
BUCKETS = 32
LINE = 384
PEER_HEADS = 8
TOPK = 16
N_KEYS = 128
TABLE_TOKENS = 64
N_CHUNKS = N_KEYS
EPS = 1e-6
NEG = -1e30
TAKEN = -3e38
SCALE = HD ** -0.5

SBUF_BASE = 16512


def bucket_of_line():
    dist = 255 - np.arange(LINE)
    ok = (dist >= 0) & (dist < WINDOW)
    d = np.clip(dist, 0, None)
    exact = BUCKETS // 2
    large = exact + (np.log(np.maximum(d, 1) / exact) / np.log(128 / exact) * (BUCKETS - exact)).astype(np.int32)
    return np.where(d < exact, d, np.minimum(large, BUCKETS - 1)).astype(np.int32), ok


def line_constants():
    bucket, ok = bucket_of_line()
    c = np.zeros((BUCKETS + 1, LINE), np.float32)
    for m in range(LINE):
        if ok[m]:
            c[bucket[m], m] = 1.0
        else:
            c[BUCKETS, m] = NEG
    return c


class Memory:

    def __init__(self, nc, ctx):
        self.nc, self.ctx = nc, ctx
        self.psum = ctx.enter_context(nc.psum_tensor("psum", [P, 8, HALF], F32))
        self.count = 0

    def at(self, name, shape, kb, dt=F32):
        return self.nc.alloc_sbuf_tensor_at(name, shape, dt, offset=SBUF_BASE + int(kb * 1024))

    def sem(self, name):
        return self.nc.alloc_semaphore(name)

    def stage(self, fn, *args):
        with self.nc.cleanup_on_exit():
            fn(self.nc, self, *args)

    def dram(self, name, shape):
        return self.nc.dram_tensor(name, shape, F32, kind="Internal").ap()


def peeled(eng, first, count, unroll, body):
    for u in range(unroll):
        body(first + u, u)
    with eng.Fori(1, count // unroll) as i:
        for u in range(unroll):
            body(i * unroll + (first + u), u)


def looped(eng, first, count, unroll, body):
    with eng.Fori(0, count // unroll) as i:
        for u in range(unroll):
            body(i * unroll + (first + u), u)


def constants(nc, m, t):
    zeroed = m.sem("const_zeroed")
    made = m.sem("const_made")
    with nc.Block() as block:
        @block.gpsimd
        def _(pool):
            nc.gpsimd.memset(t.ident[:], 0.0).then_inc(zeroed, 1)
            nc.gpsimd.memset(t.mask[:], 0.0).then_inc(zeroed, 1)
            nc.gpsimd.memset(t.ones[:], 1.0).then_inc(zeroed, 1)
            pool.wait_ge(zeroed, 3)
            nc.gpsimd.affine_select(out=t.ident[:], in_=t.ident[:], compare_op=ALU.not_equal, fill=1.0, base=0,
                                    pattern=[[-1, P]], channel_multiplier=1).then_inc(made, 1)
            nc.gpsimd.affine_select(out=t.mask[:], in_=t.mask[:], compare_op=ALU.is_ge, fill=NEG, base=0,
                                    pattern=[[-1, P]], channel_multiplier=1).then_inc(made, 1)
            nc.gpsimd.iota(t.iota[:], pattern=[[1, P]], base=0, channel_multiplier=0,
                           allow_small_or_imprecise_dtypes=True).then_inc(made, 1)
            pool.wait_ge(made, 3)


class NormEnd:
    UNITS = NH * KT
    FULL = 4
    GRP = TT // NH

    def __init__(self, nc, m, t, name, which, rows, scaled, banks, kb):
        self.nc, self.m, self.t, self.which = nc, m, t, which
        self.rows, self.scaled, self.banks = rows, scaled, banks
        self.full = m.at(name + "full", [P, self.FULL, HALF], kb)
        self.turned = m.sem(name + "turned")
        self.affine = m.sem(name + "affine")
        self.hi = m.sem(name + "hi")
        self.lo_pool = m.sem(name + "lo_pool")
        self.lo_dve = m.sem(name + "lo_dve")

    def turn(self, pe, u):
        g, k = divmod(u, KT)
        if k == 0:
            pe.wait_ge(self.scaled, self.GRP * (g + 1))
        if u >= self.banks:
            pe.wait_ge(self.affine, u - self.banks + 1)
        for i in range(self.GRP):
            mm = self.nc.tensor.transpose(self.m.psum[:, u % self.banks, i * P:(i + 1) * P],
                                          self.rows[:, self.GRP * g + i, k * P:(k + 1) * P], self.t.ident[:])
        mm.then_inc(self.turned, 1)

    def lo(self, eng, engine, sem, u):
        g, k = divmod(u, KT)
        cols = slice(g * HALF, (g + 1) * HALF)
        eng.wait_ge(self.hi, u + 1)
        engine.tensor_tensor(self.t.hT_lo[:, k, cols], self.full[:, u % self.FULL],
                             self.t.hT_hi[:, k, cols].bitcast(F32), ALU.subtract).then_inc(sem, 1)

    def scalar(self, act):
        t = self.t
        for u in range(self.UNITS):
            k = u % KT
            act.wait_ge(self.turned, u + 1)
            if u >= self.FULL:
                act.wait_ge(self.lo_dve if u % 2 else self.lo_pool, (u - self.FULL) // 2 + 1)
            self.nc.scalar.activation(self.full[:, u % self.FULL], self.m.psum[:, u % self.banks], ACT.Identity,
                                      bias=t.shift[:, self.which, k:k + 1], scale=t.gain[:, self.which, k:k + 1]) \
                .then_inc(self.affine, 1)

    def vector(self, dve, between=None):
        for u in range(self.UNITS):
            g, k = divmod(u, KT)
            dve.wait_ge(self.affine, u + 1)
            self.nc.vector.tensor_copy(self.t.hT_hi[:, k, g * HALF:(g + 1) * HALF], self.full[:, u % self.FULL]) \
                .then_inc(self.hi, 1)
            if u % 2:
                self.lo(dve, self.nc.vector, self.lo_dve, u)
            if u == 1 and between:
                between()

    def pool(self, pool):
        for u in range(0, self.UNITS, 2):
            self.lo(pool, self.nc.gpsimd, self.lo_pool, u)


def first_norm(nc, m, t, a):
    SLOTS = 4
    BANKS = 6
    x = m.at("fn_x", [P, TT, D], 84)
    w = m.at("fn_w", [P, SLOTS, 2 * D], 116)
    acc = m.at("fn_acc", [P, 2, D], 148)
    sig = m.at("fn_sig", [P, KT], 156)
    junk = m.at("fn_junk", [P, 2, D], 158)
    ssq = m.at("fn_ssq", [P, TT], 166)
    std = m.at("fn_std", [P, TT], 166.25)
    rstd = m.at("fn_rstd", [P, TT], 166.5)
    rows = m.at("fn_rows", [9 * KT, P], 167)
    x_landed = [m.sem(f"fn_x_landed{i}") for i in range(TT)]
    w_landed = [m.sem(f"fn_w_landed{i}") for i in range(SLOTS)]
    small = m.sem("fn_small_landed")
    act_sig = m.sem("fn_sigmoid")
    silu = m.sem("fn_silu")
    step = m.sem("fn_acc_step")
    summed = m.sem("fn_summed")
    cols = m.sem("fn_cols")
    cturned = m.sem("fn_columns_turned")
    columns = m.sem("fn_columns")
    squared = m.sem("fn_squared")
    mean = m.sem("fn_mean")
    root = m.sem("fn_root")
    inv = m.sem("fn_inv")
    scaled = m.sem("fn_scaled")
    end = NormEnd(nc, m, t, "fn_", 0, x, scaled, BANKS, 168)
    GRP = end.GRP
    with nc.Block() as block:
        @block.sync
        def _(sp):
            def load_x(i):
                sp.dma_start(x[:, i], a.x[0, i * P:(i + 1) * P, :]).then_inc(x_landed[i], 16)

            def load_w(k):
                if k >= SLOTS:
                    sp.wait_ge(step, 2 * (k - SLOTS + 1))
                sp.dma_start(w[:, k % SLOTS], a.w_ada[0, k * P:(k + 1) * P, 0:2 * D]) \
                    .then_inc(w_landed[k % SLOTS], 16)
            at = 0
            for src, n in ((a.c, 1), (a.b_ada, 6), (a.norm_mix_g, 1), (a.norm_ffn_g, 1)):
                sp.dma_start(rows[at:at + n * KT, :], src[0].rearrange("(k p) -> k p", p=P)).then_inc(small, 16)
                at += n * KT
            for k in range(2):
                load_w(k)
            for i in range(GRP):
                load_x(i)
            for k in range(2, 4):
                load_w(k)
            for i in range(GRP, TT):
                load_x(i)
            for k in range(4, KT):
                load_w(k)

        @block.gpsimd
        def _(pool):
            end.pool(pool)

        @block.scalar
        def _(act):
            act.wait_ge(cturned, 1)
            nc.scalar.activation(t.cols[:], m.psum[:, 6, 0:9 * KT], ACT.Copy).then_inc(columns, 1)
            act.wait_ge(columns, 1)
            nc.scalar.activation(sig[:], t.ccol[:], ACT.Sigmoid).then_inc(act_sig, 1)
            for g in range(NH):
                for i in range(GRP * g, GRP * g + GRP):
                    act.wait_ge(x_landed[i], 16)
                    if i >= 2:
                        act.wait_ge(squared, i - 1)
                    nc.scalar.activation(junk[:, i % 2], x[:, i], ACT.Square, accum_out=ssq[:, i:i + 1]) \
                        .then_inc(squared, 1)
                act.wait_ge(mean, g + 1)
                nc.scalar.activation(std[:, GRP * g:GRP * g + GRP], ssq[:, GRP * g:GRP * g + GRP], ACT.Sqrt) \
                    .then_inc(root, 1)
            act.wait_ge(cols, 3)
            end.scalar(act)

        @block.vector
        def _(dve):
            def scale(g):
                c = slice(GRP * g, GRP * g + GRP)
                dve.wait_ge(squared, GRP * (g + 1))
                nc.vector.tensor_scalar(ssq[:, c], ssq[:, c], 1.0 / D, EPS, ALU.mult, ALU.add).then_inc(mean, 1)
                dve.wait_ge(root, g + 1)
                nc.vector.reciprocal(rstd[:, c], std[:, c]).then_inc(inv, 1)
                dve.wait_ge(inv, g + 1)
                for i in range(GRP * g, GRP * g + GRP):
                    nc.vector.tensor_scalar(x[:, i], x[:, i], rstd[:, i:i + 1], None, ALU.mult) \
                        .then_inc(scaled, 1)
            dve.wait_ge(act_sig, 1)
            nc.vector.tensor_tensor(t.cact[:], t.ccol[:], sig[:], ALU.mult).then_inc(silu, 1)
            dve.wait_ge(silu, 1)
            for k in range(KT):
                for j in range(2):
                    part = w[:, k % SLOTS, j * D:(j + 1) * D]
                    if k == 0:
                        if j == 0:
                            dve.wait_ge(w_landed[0], 16)
                        nc.vector.tensor_scalar(acc[:, j], part, t.cact[:, k:k + 1], None, ALU.mult) \
                            .then_inc(step, 1)
                    else:
                        if j == 0:
                            dve.wait_ge(w_landed[k % SLOTS], 16 * (k // SLOTS + 1))
                        dve.wait_ge(step, 2 * k - 1 + j)
                        nc.vector.scalar_tensor_tensor(out=acc[:, j], in0=part, scalar=t.cact[:, k:k + 1],
                                                       in1=acc[:, j], op0=ALU.mult, op1=ALU.add).then_inc(step, 1)
                if k == 3 or k == 7:
                    scale(k // 4)
            dve.wait_ge(summed, 1)
            nc.vector.tensor_tensor(t.shift[:, 0], m.psum[:, 7, 0:KT], t.bcol[:, 0:KT], ALU.add).then_inc(cols, 1)
            nc.vector.tensor_tensor(t.gain[:, 0], m.psum[:, 7, KT:2 * KT], t.bcol[:, KT:2 * KT], ALU.add) \
                .then_inc(cols, 1)
            dve.wait_ge(cols, 2)
            nc.vector.scalar_tensor_tensor(out=t.gain[:, 0], in0=t.gain[:, 0], scalar=1.0, in1=t.gcol[:, 0],
                                           op0=ALU.add, op1=ALU.mult).then_inc(cols, 1)
            end.vector(dve)

        @block.tensor
        def _(pe):
            pe.wait_ge(small, 64)
            nc.tensor.transpose(m.psum[:, 6, 0:9 * KT], rows[:], t.ident[0:9 * KT, 0:9 * KT]).then_inc(cturned, 1)
            for u in range(BANKS):
                end.turn(pe, u)
            pe.wait_ge(step, 2 * KT)
            for j in range(2):
                for k in range(KT):
                    mm = nc.tensor.matmul(m.psum[:, 7, j * KT + k:j * KT + k + 1], acc[:, j, k * P:(k + 1) * P],
                                          t.ones[:, 0:1], start=True, stop=True)
            mm.then_inc(summed, 1)
            for u in range(BANKS, end.UNITS):
                end.turn(pe, u)


def three_pass(nc, out, l_hi, l_lo, r_hi, r_lo, steps):
    for k in range(steps):
        nc.tensor.matmul(out, l_hi(k), r_hi(k), start=k == 0, stop=False)
        nc.tensor.matmul(out, l_hi(k), r_lo(k), start=False, stop=False)
        mm = nc.tensor.matmul(out, l_lo(k), r_hi(k), start=False, stop=k == steps - 1)
    return mm


def projections(nc, m, t, a):
    raw = m.at("pw_raw", [P, 2, KT, P], 156)
    w_hi = m.at("pw_hi", [P, 2, KT, P], 164, F32R)
    w_lo = m.at("pw_lo", [P, 2, KT, P], 172, F32R)
    adaw = m.at("p_adaw", [P, 2, D], 180)
    acc = [t.gate1, m.at("p_acc_shift", [P, D], 188), m.at("p_acc_scale", [P, D], 192), t.gate2]
    sg = m.at("p_sigmoid", [P, 2, D], 196)
    tmp = m.at("p_adatmp", [P, 896], 204)
    bfl = t.bfl
    landed = [m.sem(f"p_w_landed{i}") for i in range(2)]
    hi = m.sem("p_hi")
    lo = m.sem("p_lo")
    done = m.sem("p_done")
    out = m.sem("p_out")
    stored = [m.sem(f"p_stored{i}") for i in range(2)]
    ada_landed = [m.sem(f"p_ada_landed{i}") for i in range(2)]
    weighed = m.sem("p_weighed")
    added = m.sem("p_added")
    summed = m.sem("p_summed")
    taken = m.sem("p_taken")
    small = m.sem("p_small")
    MODS = 4
    NQ, NG = QKV_CHUNKS, 2 * KT
    FL = NQ + NG
    PART = 512

    with nc.Block() as block:
        @block.sync
        def _(sp):
            w_q = a.w_in[0, :, 0:NQ * P].rearrange("(k p) (c n) -> c p k n", p=P, n=P)
            w_g = a.w_in[0, :, GATE_COL:GATE_COL + NG * P].rearrange("(k p) (c n) -> c p k n", p=P, n=P)

            def load_q(g, u):
                if isinstance(g, int):
                    pass
                else:
                    sp.wait_ge(lo, g - 1)
                sp.dma_start(raw[:, u], w_q[g]).then_inc(landed[u], 16)

            def load_g(g, u):
                sp.wait_ge(lo, g - 1)
                sp.dma_start(raw[:, u], w_g[g - NQ]).then_inc(landed[u], 16)

            peeled(sp, 0, NQ, 2, load_q)
            looped(sp, NQ, NG, 2, load_g)
            sp.wait_ge(lo, FL - 1)
            sp.dma_start(raw[:, 0, :, 0:FOX_HEADS],
                         a.w_in[0, :, FL_COL:FL_COL + FOX_HEADS].rearrange("(k p) n -> p k n", p=P)) \
                .then_inc(landed[0], 16)

        @block.scalar
        def _(act):
            def split(g, u, n=P):
                act.wait_ge(landed[u], (g - u) * 8 + 16)
                if not (isinstance(g, int) and g < 2):
                    act.wait_ge(done, g - 1)
                nc.scalar.activation(w_hi[:, u, :, 0:n], raw[:, u, :, 0:n], ACT.Copy).then_inc(hi, 1)

            def q_step(g, u):
                split(g + 1, 1 - u)
                act.wait_ge(done, g + 1)
                nc.scalar.activation(t.qkvT[:, g], m.psum[:, 2 * u:2 * u + 2], ACT.Copy).then_inc(out, 1)

            def g_step(g, u, last=False):
                if not last:
                    split(g + 1, 1 - u)
                act.wait_ge(done, g + 1)
                if not (isinstance(g, int) and g < NQ + 2):
                    act.wait_ge(stored[u], (g - u - NQ) * 8)
                nc.scalar.activation(sg[:, u], m.psum[:, 2 * u:2 * u + 2], ACT.Sigmoid).then_inc(out, 1)
                act.wait_ge(out, g + 1)
                act.dma_start(t.gates[g - NQ], sg[:, u]).then_inc(stored[u], 16)

            split(0, 0)
            peeled(act, 0, NQ, 2, q_step)
            g_step(NQ, 0)
            g_step(NQ + 1, 1)
            with act.Fori(1, NG // 2 - 1) as i:
                for u in range(2):
                    g_step(i * 2 + (NQ + u), u)
            g_step(FL - 2, 0)
            g_step(FL - 1, 1, last=True)
            split(FL, 0, FOX_HEADS)
            for u in range(2):
                act.wait_ge(stored[u], NG * 8)

        @block.vector
        def _(dve):
            def rest(g, u, n=P):
                dve.wait_ge(hi, g + 1)
                nc.vector.tensor_tensor(w_lo[:, u, :, 0:n], raw[:, u, :, 0:n], w_hi[:, u, :, 0:n].bitcast(F32),
                                        ALU.subtract).then_inc(lo, 1)
            looped(dve, 0, FL, 2, rest)
            rest(FL, 0, FOX_HEADS)
            dve.wait_ge(summed, 1)
            nc.vector.tensor_tensor(t.shift[:, 1], m.psum[:, 4, 0:KT], t.bcol[:, 3 * KT:4 * KT], ALU.add) \
                .then_inc(taken, 1)
            nc.vector.tensor_tensor(t.gain[:, 1], m.psum[:, 4, KT:2 * KT], t.bcol[:, 4 * KT:5 * KT], ALU.add) \
                .then_inc(taken, 1)
            dve.wait_ge(taken, 2)
            nc.vector.scalar_tensor_tensor(out=t.gain[:, 1], in0=t.gain[:, 1], scalar=1.0, in1=t.gcol[:, 1],
                                           op0=ALU.add, op1=ALU.mult).then_inc(taken, 1)
            dve.wait_ge(small, 48)
            dve.wait_ge(summed, 2)
            nc.vector.tensor_tensor(t.gate1[:], adaw[:, 0], m.psum[:, 5:7], ALU.add).then_inc(taken, 1)
            dve.wait_ge(summed, 3)
            nc.vector.tensor_tensor(t.gate2[:], adaw[:, 1], m.psum[:, 2:4], ALU.add).then_inc(taken, 1)

        @block.gpsimd
        def _(pool):
            order = [2, 3, 4, 5]
            pool.dma_start(bfl[:, 0:1], a.b_forget.rearrange("a h -> h a")).then_inc(small, 16)

            def load(n):
                j, k = divmod(n, KT)
                pool.dma_start(adaw[:, n % 2], a.w_ada[0, k * P:(k + 1) * P, order[j] * D:(order[j] + 1) * D]) \
                    .then_inc(ada_landed[n % 2], 16)
            load(0)
            steps = 0
            for n in range(MODS * KT):
                j, k = divmod(n, KT)
                if n + 1 < MODS * KT:
                    if n >= 1:
                        pool.wait_ge(weighed, 2 * n)
                    load(n + 1)
                pool.wait_ge(ada_landed[n % 2], 16 * (n // 2 + 1))
                for h in range(2):
                    cols = slice(h * PART, (h + 1) * PART)
                    if k == 0:
                        nc.gpsimd.tensor_scalar(acc[j][:, cols], adaw[:, n % 2, cols], t.cact[:, k:k + 1], None,
                                                ALU.mult).then_inc(weighed, 1)
                        continue
                    if steps >= 1:
                        pool.wait_ge(added, steps)
                    nc.gpsimd.tensor_scalar(tmp[:, 0:PART], adaw[:, n % 2, cols], t.cact[:, k:k + 1], None,
                                            ALU.mult).then_inc(weighed, 1)
                    pool.wait_ge(weighed, 2 * n + h + 1)
                    nc.gpsimd.tensor_tensor(acc[j][:, cols], acc[j][:, cols], tmp[:, 0:PART], ALU.add) \
                        .then_inc(added, 1)
                    steps += 1
            pool.wait_ge(weighed, 2 * MODS * KT)
            for s, j in ((0, 2), (1, 5)):
                pool.dma_start(adaw[:, s], a.b_ada[:, j * D:(j + 1) * D].partition_broadcast(P)) \
                    .then_inc(small, 16)
            pool.wait_ge(small, 48)

        @block.tensor
        def _(pe):
            def chunk(g, u, n=P):
                pe.wait_ge(lo, g + 1)
                if not (isinstance(g, int) and g < 2):
                    pe.wait_ge(out, g - 1)
                for h in range(NH):
                    cols = slice(h * HALF, (h + 1) * HALF)
                    mm = three_pass(nc, m.psum[0:n, 2 * u + h], lambda k: w_hi[:, u, k, 0:n],
                                    lambda k: w_lo[:, u, k, 0:n], lambda k: t.hT_hi[:, k, cols],
                                    lambda k: t.hT_lo[:, k, cols], KT)
                mm.then_inc(done, 1)
            peeled(pe, 0, FL, 2, chunk)
            chunk(FL, 0, FOX_HEADS)
            pe.wait_ge(weighed, 2 * MODS * KT)
            pe.wait_ge(added, 2 * MODS * (KT - 1))
            for j in range(2):
                for k in range(KT):
                    mm = nc.tensor.matmul(m.psum[:, 4, j * KT + k:j * KT + k + 1],
                                          acc[1 + j][:, k * P:(k + 1) * P], t.ones[:, 0:1], start=True, stop=True)
            mm.then_inc(summed, 1)
            for n, gate in enumerate((t.gate1, t.gate2)):
                if n:
                    pe.wait_ge(out, FL)
                for h in range(2):
                    mm = nc.tensor.matmul(m.psum[:, (5, 2)[n] + h], t.ones[:], gate[:, h * HALF:(h + 1) * HALF],
                                          start=True, stop=True)
                mm.then_inc(summed, 1)


def values(nc, m, t, a):
    fl = m.at("v_forget", [FOX_HEADS, S], 188)
    fe = m.at("v_forget_exp", [FOX_HEADS, S], 192)
    one = m.at("v_ones", [FOX_HEADS, S], 196)
    fx = m.sem("v_forget_act")
    fv = m.sem("v_forget_dve")
    fo = m.sem("v_forget_ones")
    pick = m.at("v_pick", [BUCKETS, LINE], 178)
    outside = m.at("v_outside", [FOX_HEADS, LINE], 180)
    rel = m.at("v_rel", [BUCKETS, FOX_HEADS], 182)
    line = m.at("v_line", [FOX_HEADS, LINE], 183)
    small = m.sem("v_small")
    turned = m.sem("v_turned")
    copied = m.sem("v_copied")
    lined = m.sem("v_lined")
    linec = m.sem("v_line_copied")
    wrote = m.sem("v_line_written")
    bands = m.sem("v_bands")
    vchunks = [5, 14, 15, 16, 17]
    with nc.Block() as block:
        @block.sync
        def _(sp):
            sp.dma_start(pick[:], a.line_const[0:BUCKETS, :]).then_inc(small, 16)
            sp.dma_start(outside[:], a.line_const[BUCKETS:BUCKETS + 1, :].partition_broadcast(FOX_HEADS)) \
                .then_inc(small, 16)
            sp.dma_start(rel[:], a.rel_bias).then_inc(small, 16)
            for g in range(2):
                for half in range(2):
                    sp.dma_start(t.kdup[half * HD:(half + 1) * HD, g], t.qkvT[g * HD:(g + 1) * HD, 4]) \
                        .then_inc(bands, 16)
            sp.dma_start(t.negsink[:], a.sinks.partition_broadcast(P)).then_inc(bands, 16)
            sp.wait_ge(linec, 1)
            sp.dma_start(t.line_dram, line[:].unsqueeze(1).to_broadcast([FOX_HEADS, P, LINE])).then_inc(wrote, 16)
            sp.wait_ge(wrote, 16)
            for h in range(FOX_HEADS):
                src = bass.AP(t.line_dram.tensor, h * P * LINE + P - 1, [[LINE - 1, P], [1, 2 * P]])
                sp.dma_start(t.band[:, h], src).then_inc(bands, 16)
            sp.wait_ge(bands, 16 * (5 + FOX_HEADS))

        @block.tensor
        def _(pe):
            pe.wait_ge(small, 48)
            nc.tensor.matmul(m.psum[0:FOX_HEADS, 7, 0:LINE], rel[:], pick[:], start=True, stop=True) \
                .then_inc(lined, 1)
            for n, c in enumerate(vchunks):
                for q in range(2):
                    u = 2 * n + q
                    if u >= 4:
                        pe.wait_ge(copied, u - 3)
                    for i in range(4):
                        mm = nc.tensor.transpose(m.psum[:, 2 + u % 4, i * P:(i + 1) * P],
                                                 t.qkvT[:, c, (4 * q + i) * P:(4 * q + i + 1) * P], t.ident[:])
                    mm.then_inc(turned, 1)

        @block.scalar
        def _(act):
            act.wait_ge(fv, 1)
            nc.scalar.activation(fe[:], fl[:], ACT.Abs).then_inc(fx, 1)
            act.wait_ge(fx, 1)
            nc.scalar.activation(fe[:], fe[:], ACT.Exp, scale=-1.0).then_inc(fx, 1)
            act.wait_ge(fx, 2)
            nc.scalar.activation(fe[:], fe[:], ACT.Ln, bias=1.0).then_inc(fx, 1)

        @block.gpsimd
        def _(pool):
            nc.gpsimd.memset(one[:], 1.0).then_inc(fo, 1)

        @block.vector
        def _(dve):
            z = m.psum[0:FOX_HEADS, 0:2]
            nc.vector.tensor_scalar(fl[:], z, t.bfl[:, 0:1], None, ALU.add).then_inc(fv, 1)
            dve.wait_ge(lined, 1)
            dve.wait_ge(small, 48)
            nc.vector.tensor_tensor(line[:], m.psum[0:FOX_HEADS, 7, 0:LINE], outside[:], ALU.add) \
                .then_inc(linec, 1)
            dve.wait_ge(fv, 1)
            dve.wait_ge(fx, 1)
            nc.vector.tensor_scalar(fl[:], fl[:], -1.0, 0.0, ALU.mult, ALU.max).then_inc(fv, 1)
            for n in range(len(vchunks)):
                for q in range(2):
                    u = 2 * n + q
                    dve.wait_ge(turned, u + 1)
                    nc.vector.tensor_copy(t.v[:, 4 * q:4 * q + 4, n * P:(n + 1) * P],
                                          m.psum[:, 2 + u % 4].rearrange("p (i c) -> p i c", c=P)).then_inc(copied, 1)
            dve.wait_ge(fv, 2)
            dve.wait_ge(fx, 3)
            nc.vector.tensor_tensor(fe[:], fe[:], fl[:], ALU.add).then_inc(fv, 1)
            dve.wait_ge(fv, 3)
            dve.wait_ge(fo, 1)
            nc.vector.tensor_tensor_scan(t.negF[:], one[:], fe[:], 0.0, ALU.mult, ALU.add).then_inc(fv, 1)
            dve.wait_ge(bands, 16 * (5 + FOX_HEADS))
            nc.vector.tensor_scalar(t.negsink[:], t.negsink[:], -1.0, None, ALU.mult).then_inc(copied, 1)


def hold(eng, t):
    eng.sem_inc(t.passed, 1)


def attention(nc, m, t):
    JOBS = [(br, par, n if br or not par else TT - 1 - n) for br in (0, 1) for par in (0, 1) for n in range(TT)]
    NJ = len(JOBS)
    NS = sum(1 for j in JOBS if j[0] == 1)
    FOX = NJ - NS
    AHEAD_S = 3
    q_st = m.at("at_q", [P, 2, 2, S], 140)
    k_st = m.at("at_k", [P, 2, S], 60)
    nf = m.at("at_negF", [P, 2, S], 176)
    scs = [m.at(f"at_scores{x}", [P, S], kb) for x, kb in enumerate((184, 188, 11, 203.75))]
    pT = m.at("at_pT", [P, 2, S], 192)
    b_st = m.at("at_band", [P, 2, 2 * P], 200)
    mx = m.at("at_max", [P, NJ], 202)
    nm = m.at("at_negmax", [P, NJ], 202.25)
    rs = m.at("at_rowsum", [P, NJ], 202.5)
    se = m.at("at_sinkexp", [P, NJ], 202.75)
    dn = m.at("at_denominator", [P, NJ], 203)
    rc = m.at("at_reciprocal", [P, NJ], 203.25)
    flat = m.psum[:].rearrange("p b n -> p (b n)")
    q_zero = m.sem("at_q_zeroed")
    q_fox = m.sem("at_staged_q_fox")
    q_win = m.sem("at_staged_q_window")
    k_fox = m.sem("at_staged_k_fox")
    k_win = m.sem("at_staged_k_window")
    b_win = m.sem("at_staged_band")
    negf_out = m.sem("at_negF_out")
    negf_in = [m.sem(f"at_negF_in{i}") for i in range(2)]
    scored = m.sem("at_scored")
    maxed = m.sem("at_maxed")
    negated = m.sem("at_negated")
    expd = m.sem("at_exp")
    sunk = m.sem("at_sink_exp")
    turned = m.sem("at_turned")
    copied_a = m.sem("at_copied_act")
    copied_v = m.sem("at_copied_dve")
    weighted = m.sem("at_weighted")
    dens = m.sem("at_denominators")
    inv = m.sem("at_inverted")
    normed = m.sem("at_normed")

    def keys(job):
        br, par, n = job
        return list(range(0 if br == 0 else max(n - 1, 0), n + 1))

    groups = [[keys(j)[x:x + 4] for x in range(0, len(keys(j)), 4)] for j in JOBS]
    before = [sum(len(g) for g in groups[:j]) for j in range(NJ + 1)]
    NGR = before[NJ]
    assert NGR % 2 == 0 and NJ % len(scs) == 0
    NC = NGR // 2

    def after(eng, sem, count):
        at_least(eng, sem, count + 1)

    def groups_before(i, j):
        return i * NGR + before[j] if j >= 0 else (i - 1) * NGR + before[NJ + j]

    def copies(eng, copy, mine, sem, i, j):
        for x, grp in enumerate(groups[j]):
            G = before[j] + x
            if G % 2 != mine:
                continue
            after(eng, turned, i * NGR + (G + 1))
            after(eng, weighted, i * NJ + (j - 1))
            w = len(grp) * P
            copy(pT[:, j % 2, x * HALF:x * HALF + w], flat[:, (4 + G % 2) * HALF:(4 + G % 2) * HALF + w]) \
                .then_inc(sem, 1)

    def pairs(eng, body):
        with eng.Fori(0, PAIRS - 1) as i:
            body(i, False)
        body(PAIRS - 1, True)

    def run(i, last, j, *stages):
        for stage, ahead in stages:
            if j + ahead < NJ:
                stage(i, j + ahead)
            elif not last:
                stage(i + 1, j + ahead - NJ)

    with nc.Block() as block:
        @block.sync
        def _(sp):
            def load(i, par):
                h = i * 2 + par
                row = t.negf_dram[h:h + 1, :] if isinstance(h, int) else t.negf_dram[bass.ds(h, 1), :]
                sp.dma_start(nf[:, par], row.partition_broadcast(P)).then_inc(negf_in[par], 16)
            sp.dma_start(t.negf_dram, t.negF[:]).then_inc(negf_out, 16)
            sp.wait_ge(negf_out, 16)
            for par in range(2):
                load(0, par)
            with sp.Fori(0, PAIRS - 1) as i:
                for par in range(2):
                    after(sp, maxed, i * NJ + (par + 1) * TT)
                    load(i + 1, par)

        @block.gpsimd
        def _(pool):
            for par in range(2):
                nc.gpsimd.memset(q_st[(1 - par) * HD:(2 - par) * HD, :, par], 0.0).then_inc(q_zero, 1)
            pool.wait_ge(q_zero, 2)
            nc.gpsimd.tensor_copy(k_st[:, 0], t.qkvT[:, 10]).then_inc(k_fox, 1)

            def pair(i, last):
                after(pool, scored, i * NJ)
                hold(pool, t)
                nc.gpsimd.tensor_copy(k_st[:, 1], t.kdup[:, i // 2]).then_inc(k_win, 1)
                after(pool, maxed, i * NJ)
                hold(pool, t)
                for par in range(2):
                    nc.gpsimd.tensor_copy(b_st[:, par], t.band[:, i * 2 + par]).then_inc(b_win, 1)
                if not last:
                    after(pool, scored, i * NJ + FOX)
                    hold(pool, t)
                    nc.gpsimd.tensor_copy(k_st[:, 0], t.qkvT[:, i + 11]).then_inc(k_fox, 1)
            pairs(pool, pair)

        @block.tensor
        def _(pe):
            for sem in (scored, turned, weighted):
                pe.sem_inc(sem, 1)

            def score(i, j):
                br, par, n = JOBS[j]
                if isinstance(i, int) and i == 0 and j == 0:
                    pe.wait_ge(q_zero, 2)
                if j == 0:
                    pe.wait_ge(q_fox, i * 2 + 2)
                    pe.wait_ge(k_fox, i + 1)
                if j == FOX:
                    pe.wait_ge(q_win, i * 2 + 2)
                    pe.wait_ge(k_win, i + 1)
                after(pe, maxed, i * NJ + (j - 1))
                ks = keys(JOBS[j])
                k0, w = ks[0] * P, len(ks) * P
                for h in range(0, w, HALF):
                    x = min(HALF, w - h)
                    diag = h + x == w and br == 0
                    o = (2 * (j % 2)) * HALF + h
                    mm = nc.tensor.matmul(flat[:, o:o + x], q_st[:, br, par, n * P:(n + 1) * P],
                                          k_st[:, br, k0 + h:k0 + h + x], start=True, stop=not diag)
                    if diag:
                        mm = nc.tensor.matmul(flat[:, o + x - P:o + x], t.ident[:], t.mask[:],
                                              start=False, stop=True)
                mm.then_inc(scored, 1)

            def turn(i, j):
                pe.wait_ge(expd, i * NJ + (j + 1))
                k0 = keys(JOBS[j])[0]
                for x, grp in enumerate(groups[j]):
                    G = before[j] + x
                    after(pe, copied_v if G % 2 else copied_a, i * NC + G // 2)
                    for y, kt in enumerate(grp):
                        o = (4 + G % 2) * HALF + y * P
                        mm = nc.tensor.transpose(flat[:, o:o + P], scs[j % 4][:, (kt - k0) * P:(kt - k0 + 1) * P],
                                                 t.ident[:])
                    mm.then_inc(turned, 1)

            def weigh(i, j):
                br, par, n = JOBS[j]
                G = before[j + 1]
                after(pe, copied_a, i * NC + (G + 1) // 2)
                after(pe, copied_v, i * NC + G // 2)
                after(pe, normed, i * NJ + max(j - 1, 0))
                ks = keys(JOBS[j])
                for y, kt in enumerate(ks):
                    col = i * P + (P + par * HD) if br == 0 else (i // 2) * HD
                    mm = nc.tensor.matmul(m.psum[:, 6 + j % 2, 0:HD], pT[:, j % 2, y * P:(y + 1) * P],
                                          t.v[:, kt, bass.ds(col, HD)], start=y == 0, stop=y == len(ks) - 1)
                mm.then_inc(weighted, 1)

            def pair(i, last):
                for j in range(NJ):
                    run(i, last, j, (score, AHEAD_S), (turn, 1), (weigh, 0))
            for j in range(AHEAD_S):
                score(0, j)
            turn(0, 0)
            pairs(pe, pair)

        @block.scalar
        def _(act):
            act.sem_inc(copied_a, 1)

            def exp(i, j):
                br, par, n = JOBS[j]
                w = len(keys(JOBS[j])) * P
                act.wait_ge(negated, i * NJ + (j + 1))
                nc.scalar.activation(scs[j % 4][:, 0:w], scs[j % 4][:, 0:w], ACT.Exp,
                                     bias=nm[:, j:j + 1], accum_out=rs[:, j:j + 1]).then_inc(expd, 1)
                if br == 1:
                    nc.scalar.activation(se[:, j:j + 1], t.negsink[:, bass.ds(i * 2 + par, 1)], ACT.Exp,
                                         bias=nm[:, j:j + 1], scale=-1.0).then_inc(sunk, 1)

            def copy(i, j):
                copies(act, lambda o, x: nc.scalar.activation(o, x, ACT.Copy), 0, copied_a, i, j)

            def stage(br, c, sem):
                for par in range(2):
                    rows = slice(par * HD, (par + 1) * HD)
                    if not isinstance(c, int):
                        hold(act, t)
                    nc.scalar.activation(q_st[rows, br, par], t.qkvT[rows, c], ACT.Copy, scale=SCALE) \
                        .then_inc(sem, 1)

            def pair(i, last):
                for j in range(NJ):
                    run(i, last, j, (exp, AHEAD_S), (copy, 1))
                    if j == 0:
                        after(act, scored, i * NJ)
                        stage(1, i, q_win)
                    if j == FOX and not last:
                        after(act, scored, i * NJ + FOX)
                        stage(0, i + 7, q_fox)
            stage(0, 6, q_fox)
            for j in range(AHEAD_S):
                exp(0, j)
            copy(0, 0)
            pairs(act, pair)

        @block.vector
        def _(dve):
            for sem in (maxed, copied_v, normed):
                dve.sem_inc(sem, 1)

            def maximum(i, j):
                br, par, n = JOBS[j]
                w = len(keys(JOBS[j])) * P
                if j == par * TT:
                    dve.wait_ge(negf_in[par], i * 16 + 16)
                if j == FOX:
                    dve.wait_ge(b_win, i * 2 + 2)
                after(dve, turned, groups_before(i, j - 3))
                after(dve, scored, i * NJ + (j + 1))
                hold(dve, t)
                bias = nf[:, par, 0:w] if br == 0 else b_st[:, par, 2 * P - w:2 * P]
                nc.vector.tensor_tensor_reduce(scs[j % 4][:, 0:w], flat[:, 2 * (j % 2) * HALF:][:, 0:w], bias,
                                               1.0, -3e38, ALU.add, ALU.max, mx[:, j:j + 1]).then_inc(maxed, 1)

            def negate(i, j):
                br, par, n = JOBS[j]
                after(dve, maxed, i * NJ + (j + 1))
                if br == 0:
                    nc.vector.tensor_scalar(nm[:, j:j + 1], mx[:, j:j + 1], -1.0, None, ALU.mult) \
                        .then_inc(negated, 1)
                else:
                    nc.vector.tensor_scalar(nm[:, j:j + 1], mx[:, j:j + 1], -1.0,
                                            t.negsink[:, bass.ds(i * 2 + par, 1)], ALU.mult, ALU.min) \
                        .then_inc(negated, 1)

            def copy(i, j):
                copies(dve, nc.vector.tensor_copy, 1, copied_v, i, j)

            def denominator(i, j):
                if j >= FOX:
                    dve.wait_ge(sunk, i * NS + (j - FOX + 1))
                    nc.vector.tensor_tensor(dn[:, j:j + 1], rs[:, j:j + 1], se[:, j:j + 1], ALU.add) \
                        .then_inc(dens, 1)

            def invert(i, j):
                if j >= FOX:
                    dve.wait_ge(dens, i * NS + (j - FOX + 1))
                    den = dn
                else:
                    dve.wait_ge(expd, i * NJ + (j + 1))
                    den = rs
                nc.vector.reciprocal(rc[:, j:j + 1], den[:, j:j + 1]).then_inc(inv, 1)

            def divide(i, j):
                br, par, n = JOBS[j]
                dve.wait_ge(inv, i * NJ + (j + 1))
                after(dve, weighted, i * NJ + (j + 1))
                nc.vector.tensor_scalar(t.o[:, 1 - br, n, bass.ds(i * P + par * HD, HD)],
                                        m.psum[:, 6 + j % 2, 0:HD], rc[:, j:j + 1], None, ALU.mult) \
                    .then_inc(normed, 1)

            def pair(i, last):
                for j in range(NJ):
                    run(i, last, j, (maximum, AHEAD_S), (denominator, 0), (negate, AHEAD_S), (invert, 0),
                        (copy, 1), (divide, 0))
            for j in range(AHEAD_S):
                maximum(0, j)
                negate(0, j)
            copy(0, 0)
            pairs(dve, pair)


def mixing(nc, m, t, a):
    KB = 4
    oT_hi = m.at("mx_oT_hi", [P, 2 * KB, S], 52, F32R)
    oT_lo = m.at("mx_oT_lo", [P, 2 * KB, S], 84, F32R)
    raw = m.at("mx_raw", [P, 2, 2 * KB, P], 180)
    w_hi = m.at("mx_w_hi", [P, 2, 2 * KB, P], 188, F32R)
    w_lo = m.at("mx_w_lo", [P, 2, 2 * KB, P], 196, F32R)
    gate = m.at("mx_gate", [P, 2, 2, S], 20)
    part = m.at("mx_part", [P, 2, S], 36)
    mix = m.at("mx_sum", [P, 2, S], 44)
    landed = [m.sem(f"mx_w_landed{i}") for i in range(2)]
    gated = [m.sem(f"mx_gate_landed{i}") for i in range(2)]
    turned = m.sem("mx_turned")
    o_hi = m.sem("mx_o_hi")
    o_lo = m.sem("mx_o_lo")
    hi = m.sem("mx_hi")
    lo = m.sem("mx_lo")
    done = m.sem("mx_done")
    scaled = m.sem("mx_scaled")
    summed = m.sem("mx_summed")
    m_hi = m.sem("mx_m_hi")
    m_lo = m.sem("mx_m_lo")
    UNITS = 2 * KB * NH
    with nc.Block() as block:
        @block.sync
        def _(sp):
            w_a = a.w_branch_a[0].rearrange("(k p) (c n) -> c p k n", p=P, n=P)
            w_b = a.w_branch_b[0].rearrange("(k p) (c n) -> c p k n", p=P, n=P)

            def load(g, u):
                if not isinstance(g, int):
                    sp.wait_ge(lo, g - 1)
                sp.dma_start(raw[:, u, 0:KB], w_a[g]).then_inc(landed[u], 16)
                sp.dma_start(raw[:, u, KB:2 * KB], w_b[g]).then_inc(landed[u], 16)
                if isinstance(g, int):
                    if g == 0:
                        sp.wait_ge(turned, UNITS)
                else:
                    sp.wait_ge(scaled, g * 2 - 2)
                sp.dma_start(gate[:, u, 0], t.gates[g]).then_inc(gated[u], 16)
                sp.dma_start(gate[:, u, 1], t.gates[g + KT]).then_inc(gated[u], 16)
            peeled(sp, 0, KT, 2, load)

        @block.tensor
        def _(pe):
            for x in range(UNITS):
                c, h = divmod(x, NH)
                if x >= 8:
                    pe.wait_ge(o_lo, x - 7)
                for i in range(4):
                    mm = nc.tensor.transpose(m.psum[:, x % 8, i * P:(i + 1) * P],
                                             t.o[:, c // KB, 4 * h + i, (c % KB) * P:(c % KB + 1) * P], t.ident[:])
                mm.then_inc(turned, 1)
            pe.wait_ge(o_lo, UNITS)

            def chunk(g, u):
                pe.wait_ge(lo, g + 1)
                if not (isinstance(g, int) and g < 2):
                    pe.wait_ge(scaled, g * 2 - 2)
                for br in range(2):
                    for h in range(NH):
                        cols = slice(h * HALF, (h + 1) * HALF)
                        mm = three_pass(nc, m.psum[:, 4 * u + 2 * br + h],
                                        lambda k: w_hi[:, u, br * KB + k], lambda k: w_lo[:, u, br * KB + k],
                                        lambda k: oT_hi[:, br * KB + k, cols],
                                        lambda k: oT_lo[:, br * KB + k, cols], KB)
                mm.then_inc(done, 1)
            peeled(pe, 0, KT, 2, chunk)

        @block.scalar
        def _(act):
            for x in range(UNITS):
                c, h = divmod(x, NH)
                act.wait_ge(turned, x + 1)
                nc.scalar.activation(oT_hi[:, c, h * HALF:(h + 1) * HALF], m.psum[:, x % 8], ACT.Copy) \
                    .then_inc(o_hi, 1)

            def split(g, u):
                act.wait_ge(landed[u], (g - u) * 16 + 32)
                if not (isinstance(g, int) and g < 2):
                    act.wait_ge(done, g - 1)
                nc.scalar.activation(w_hi[:, u], raw[:, u], ACT.Copy).then_inc(hi, 1)

            def step(g, u, last=False):
                if not last:
                    split(g + 1, 1 - u)
                act.wait_ge(summed, g + 1)
                hold(act, t)
                nc.scalar.activation(t.mixT_hi[:, g], mix[:, u], ACT.Copy).then_inc(m_hi, 1)
            split(0, 0)
            step(0, 0)
            step(1, 1)
            with act.Fori(1, KT // 2 - 1) as i:
                for u in range(2):
                    step(i * 2 + u, u)
            step(KT - 2, 0)
            step(KT - 1, 1, last=True)

        @block.vector
        def _(dve):
            for x in range(UNITS):
                c, h = divmod(x, NH)
                cols = slice(h * HALF, (h + 1) * HALF)
                dve.wait_ge(o_hi, x + 1)
                nc.vector.tensor_tensor(oT_lo[:, c, cols], m.psum[:, x % 8], oT_hi[:, c, cols].bitcast(F32),
                                        ALU.subtract).then_inc(o_lo, 1)

            def step(g, u):
                dve.wait_ge(done, g + 1)
                dve.wait_ge(gated[u], (g - u) * 16 + 32)
                for br in range(2):
                    if not (isinstance(g, int) and g == 0):
                        dve.wait_ge(summed, g)
                    b = 4 * u + 2 * br
                    nc.vector.tensor_tensor(part[:, br], m.psum[:, b:b + 2].rearrange("p b n -> p (b n)"),
                                            gate[:, u, br], ALU.mult).then_inc(scaled, 1)
                dve.wait_ge(scaled, g * 2 + 2)
                if not (isinstance(g, int) and g < 2):
                    dve.wait_ge(m_lo, g - 1)
                nc.vector.tensor_tensor(mix[:, u], part[:, 0], part[:, 1], ALU.add).then_inc(summed, 1)
            peeled(dve, 0, KT, 2, step)

        @block.gpsimd
        def _(pool):
            def rest(g, u):
                pool.wait_ge(hi, g + 1)
                nc.gpsimd.tensor_tensor(w_lo[:, u], raw[:, u], w_hi[:, u].bitcast(F32), ALU.subtract) \
                    .then_inc(lo, 1)

            def step(g, u, last=False):
                if not last:
                    rest(g + 1, 1 - u)
                pool.wait_ge(m_hi, g + 1)
                hold(pool, t)
                nc.gpsimd.tensor_tensor(t.mixT_lo[:, g], mix[:, u], t.mixT_hi[:, g].bitcast(F32), ALU.subtract) \
                    .then_inc(m_lo, 1)
            rest(0, 0)
            looped(pool, 0, KT - 2, 2, step)
            step(KT - 2, 0)
            step(KT - 1, 1, last=True)


def out_and_norm(nc, m, t, a):
    SLOTS = 4
    GRP = TT // NH
    w_hi = m.at("op_hi", [P, KT, D], 20, F32R)
    w_lo = m.at("op_lo", [P, KT, D], 52, F32R)
    x = m.at("op_x", [P, TT, D], 84)
    raw = m.at("op_raw", [P, SLOTS, D], 180)
    y = m.at("op_y", [P, 2, HALF], 196)
    junk = m.at("op_junk", [P, D], 200)
    ssq = m.at("op_ssq", [P, TT], 204)
    mean = m.at("op_mean", [P, TT], 204.25)
    std = m.at("op_std", [P, TT], 204.5)
    rstd = m.at("op_rstd", [P, TT], 204.75)
    w_landed = [m.sem(f"op_w_landed{i}") for i in range(SLOTS)]
    x_landed = [m.sem(f"op_x_landed{i}") for i in range(NH)]
    hi = m.sem("op_w_hi")
    lo = m.sem("op_w_lo")
    done = m.sem("op_done")
    gated = m.sem("op_gated")
    added = m.sem("op_added")
    squared = m.sem("op_squared")
    meaned = m.sem("op_mean_done")
    root = m.sem("op_root")
    inv = m.sem("op_inv")
    scaled = m.sem("op_scaled")
    stored = [m.sem(f"op_stored{i}") for i in range(TT)]
    end = NormEnd(nc, m, t, "op_n_", 1, x, scaled, 8, 180)
    with nc.Block() as block:
        @block.sync
        def _(sp):
            for k in range(KT):
                if k >= SLOTS:
                    sp.wait_ge(lo, k - SLOTS + 1)
                sp.dma_start(raw[:, k % SLOTS], a.w_out[0, k * P:(k + 1) * P, :]).then_inc(w_landed[k % SLOTS], 16)
                if k >= KT - NH:
                    h = k - (KT - NH)
                    rows = slice(h * GRP * P, (h + 1) * GRP * P)
                    sp.dma_start(x[:, h * GRP:(h + 1) * GRP], a.x[0, rows, :].rearrange("(i p) n -> p i n", p=P)) \
                        .then_inc(x_landed[h], 16)
            for i in range(TT):
                sp.wait_ge(added, 2 * i + 2)
                sp.dma_start(t.x1[i * P:(i + 1) * P, :], x[:, i]).then_inc(stored[i], 16)
            for i in range(TT):
                sp.wait_ge(stored[i], 16)

        @block.scalar
        def _(act):
            for k in range(KT):
                act.wait_ge(w_landed[k % SLOTS], 16 * (k // SLOTS + 1))
                nc.scalar.activation(w_hi[:, k], raw[:, k % SLOTS], ACT.Copy).then_inc(hi, 1)
            for i in range(TT):
                act.wait_ge(added, 2 * i + 2)
                if i >= 1:
                    act.wait_ge(squared, i)
                nc.scalar.activation(junk[:], x[:, i], ACT.Square, accum_out=ssq[:, i:i + 1]).then_inc(squared, 1)
                if i % GRP == GRP - 1:
                    g = i // GRP
                    act.wait_ge(meaned, g + 1)
                    nc.scalar.activation(std[:, GRP * g:GRP * g + GRP], mean[:, GRP * g:GRP * g + GRP], ACT.Sqrt) \
                        .then_inc(root, 1)
            act.wait_ge(done, NH * TT)
            end.scalar(act)

        @block.gpsimd
        def _(pool):
            for k in range(KT):
                pool.wait_ge(hi, k + 1)
                nc.gpsimd.tensor_tensor(w_lo[:, k], raw[:, k % SLOTS], w_hi[:, k].bitcast(F32), ALU.subtract) \
                    .then_inc(lo, 1)
            end.pool(pool)

        @block.tensor
        def _(pe):
            def product(b, i, h, k):
                rows = slice(i * P, (i + 1) * P)
                cols = slice(h * HALF, (h + 1) * HALF)
                out = m.psum[:, b]
                nc.tensor.matmul(out, t.mixT_hi[:, k, rows], w_hi[:, k, cols], start=k == 0, stop=False)
                nc.tensor.matmul(out, t.mixT_hi[:, k, rows], w_lo[:, k, cols], start=False, stop=False)
                return nc.tensor.matmul(out, t.mixT_lo[:, k, rows], w_hi[:, k, cols], start=False,
                                        stop=k == KT - 1)
            for k in range(KT):
                pe.wait_ge(lo, k + 1)
                for b in range(NH * GRP):
                    mm = product(b, b // NH, b % NH, k)
                    if k == KT - 1:
                        mm.then_inc(done, 1)
            for g in range(NH * GRP, NH * TT):
                pe.wait_ge(gated, g - 7)
                for k in range(KT):
                    mm = product(g - NH * GRP, g // NH, g % NH, k)
                mm.then_inc(done, 1)
            pe.wait_ge(gated, NH * TT)
            for u in range(end.UNITS):
                end.turn(pe, u)

        @block.vector
        def _(dve):
            def scale(g):
                c = slice(GRP * g, GRP * g + GRP)
                dve.wait_ge(squared, GRP * (g + 1))
                nc.vector.tensor_scalar(mean[:, c], ssq[:, c], 1.0 / D, EPS, ALU.mult, ALU.add) \
                    .then_inc(meaned, 1)
                dve.wait_ge(root, g + 1)
                nc.vector.reciprocal(rstd[:, c], std[:, c]).then_inc(inv, 1)
                dve.wait_ge(inv, g + 1)
                for i in range(GRP * g, GRP * g + GRP):
                    dve.wait_ge(stored[i], 16)
                    nc.vector.tensor_scalar(x[:, i], x[:, i], rstd[:, i:i + 1], None, ALU.mult) \
                        .then_inc(scaled, 1)
            for g in range(NH * TT):
                i, h = divmod(g, NH)
                cols = slice(h * HALF, (h + 1) * HALF)
                dve.wait_ge(done, g + 1)
                if g >= 2:
                    dve.wait_ge(added, g - 1)
                nc.vector.tensor_tensor(y[:, g % 2], m.psum[:, g % 8], t.gate1[:, cols], ALU.mult) \
                    .then_inc(gated, 1)
                dve.wait_ge(gated, g + 1)
                dve.wait_ge(x_landed[i // GRP], 16)
                nc.vector.tensor_tensor(x[:, i, cols], x[:, i, cols], y[:, g % 2], ALU.add).then_inc(added, 1)
                if g == NH * TT - 4:
                    scale(0)
            scale(1)
            end.vector(dve)


def steps(eng, first, count, unroll, body):
    for u in range(unroll):
        body(first + u, u)
    if count > 2 * unroll:
        with eng.Fori(1, count // unroll - 1) as i:
            for u in range(unroll):
                body(i * unroll + (first + u), u)
    for u in range(unroll):
        body(first + count - unroll + u, u)


def at_least(eng, sem, value):
    if not (isinstance(value, int) and value <= 0):
        eng.wait_ge(sem, value)


class Ahead:

    def __init__(self, nc, m, t, a, name, first, count):
        self.nc, self.m, self.t, self.a = nc, m, t, a
        self.first, self.count = first, count
        self.full = m.at(name + "downT", [P, D], 168)
        self.raw = m.at(name + "down", [P, 2, D], 172)
        self.hi = m.at(name + "downT_hi", [P, 2, KT, P], 180, F32R)
        self.lo = [m.at(name + "downT_lo0", [P, KT, P], 188, F32R), m.at(name + "downT_lo1", [P, KT, P], 15, F32R)]
        self.out = m.at(name + "gelu", [P, 2, S], 7)
        self.landed = [m.sem(f"{name}down_landed{i}") for i in range(2)]
        self.turned = m.sem(name + "turned")
        self.hi_done = m.sem(name + "downT_hi_done")
        self.lo_done = m.sem(name + "downT_lo_done")
        self.gelued = m.sem(name + "gelu_done")
        self.stored = [m.sem(f"{name}gelu_stored{i}") for i in range(2)]

    def load(self, sp, n, u):
        at_least(sp, self.turned, n - 1)
        e = n + self.first
        rows = slice(e * P, (e + 1) * P) if isinstance(e, int) else bass.ds(e * P, P)
        sp.dma_start(self.raw[:, u], self.a.expert_down[0, rows, :]).then_inc(self.landed[u], 16)

    def store(self, sp, n, u):
        sp.wait_ge(self.gelued, n * 2 + 2)
        e = n + self.first
        dst = self.t.gelus[e] if isinstance(e, int) else self.t.gelus[bass.ds(e, 1), :, :].rearrange("o p c -> (o p) c")
        sp.dma_start(dst, self.out[:, u]).then_inc(self.stored[u], 16)

    def turn(self, pe, n, u):
        pe.wait_ge(self.landed[u], (n - u) * 8 + 16)
        at_least(pe, self.lo_done, n)
        for k in range(KT):
            mm = self.nc.tensor.transpose(self.m.psum[:, 2 + k // 4, (k % 4) * P:(k % 4 + 1) * P],
                                          self.raw[:, u, k * P:(k + 1) * P], self.t.ident[:])
        mm.then_inc(self.turned, 1)

    def split(self, act, n, u):
        act.wait_ge(self.turned, n + 1)
        at_least(act, self.lo_done, n)
        turned = self.m.psum[:, 2:4].rearrange("p b n -> p (b n)")
        self.nc.scalar.activation(self.full[:], turned, ACT.Copy).then_inc(self.hi_done, 1)
        at_least(act, self.gelued, n * 2 - 2)
        self.nc.scalar.activation(self.hi[:, u].rearrange("p k n -> p (k n)"), turned, ACT.Copy) \
            .then_inc(self.hi_done, 1)

    def rest(self, pool, n, u):
        pool.wait_ge(self.hi_done, n * 2 + 2)
        self.nc.gpsimd.tensor_tensor(self.lo[u][:].rearrange("p k n -> p (k n)"), self.full[:],
                                     self.hi[:, u].rearrange("p k n -> p (k n)").bitcast(F32), ALU.subtract) \
            .then_inc(self.lo_done, 1)

    def product(self, out, u, h, k):
        cols = slice(h * HALF, (h + 1) * HALF)
        mm = self.nc.tensor.matmul
        mm(out, self.hi[:, u, k], self.t.hT_hi[:, k, cols], start=k == 0, stop=False)
        mm(out, self.hi[:, u, k], self.t.hT_lo[:, k, cols], start=False, stop=False)
        return mm(out, self.lo[u][:, k], self.t.hT_hi[:, k, cols], start=False, stop=k == KT - 1)

    def gelu(self, act, psum, n, u, h):
        if h == 0:
            at_least(act, self.stored[u], (n - u) * 8)
        self.nc.scalar.activation(self.out[:, u, h * HALF:(h + 1) * HALF], psum, ACT.Gelu) \
            .then_inc(self.gelued, 1)

    def finish(self, sp):
        for u in range(2):
            sp.wait_ge(self.stored[u], 16 * (self.count // 2))


AHEAD_HEADS = 2 * PEER_HEADS
AHEAD_ROUTING = AHEAD_HEADS + 4
AHEAD_TABLE = 32
AHEAD = AHEAD_ROUTING + AHEAD_TABLE


def routing(nc, m, t, a):
    ah = Ahead(nc, m, t, a, "ra_", 0, AHEAD_ROUTING)
    raw = m.at("r_raw", [P, 2, KT, P], 84)
    w_hi = m.at("r_hi", [P, 2, KT, P], 92, F32R)
    w_lo = m.at("r_lo", [P, 2, KT, P], 100, F32R)
    qT = m.at("r_qT", [P, 2, S], 108)
    knat = m.at("r_keys", [P, 2 * PEER_HEADS, HD], 116)
    kT = m.at("r_keysT", [P, PEER_HEADS, P], 120)
    left = m.at("r_left", [P, 4, P], 124)
    best = m.at("r_best", [P, 2, TT, 2, TOPK], 126)
    where = m.at("r_where", [P, 2, TT, 2, TOPK], 128, U32)
    cand = m.at("r_cand", [P, 2, TOPK * TOPK], 130)
    cleft = m.at("r_cand_left", [P, 2, TOPK * TOPK], 132)
    top = m.at("r_top", [P, 2, TT, TOPK], 134)
    pos = m.at("r_pos", [P, 2, TT, TOPK], 135, U32)
    ab = m.at("r_ab", [P, 2, P], 136, U32)
    abf = m.at("r_ab_float", [P, 2, P], 137)
    wf = m.at("r_where_float", [P, TT, 2, TOPK], 138)
    less = m.at("r_less", [P, TT, TOPK], 139)
    ex = m.at("r_exp", [P, TT, TOPK], 139.5)
    rsum = m.at("r_sum", [P, TT], 140)
    rinv = m.at("r_inv", [P, TT], 140.25)
    kst = m.at("r_keys_staged", [P, 2, P], 141)
    hot = m.at("r_hot", [P, 2, TT * TOPK, TOPK], 142)
    landed = [m.sem(f"r_w_landed{i}") for i in range(2)]
    keysl = m.sem("r_keys_landed")
    kturned = m.sem("r_keys_turned")
    kcopied = m.sem("r_keys_copied")
    kstaged = m.sem("r_keys_staged_done")
    hi = m.sem("r_hi_done")
    lo = m.sem("r_lo_done")
    produced = m.sem("r_produced")
    drained = m.sem("r_drained")
    scored = m.sem("r_scored")
    v1 = m.sem("r_first_values")
    x1 = m.sem("r_first_places")
    l1 = m.sem("r_left_made")
    v2 = m.sem("r_second_values")
    x2 = m.sem("r_second_places")
    cd = m.sem("r_cands")
    cv1 = m.sem("r_cand_first")
    cx1 = m.sem("r_cand_first_places")
    cl1 = m.sem("r_cand_left_made")
    cv2 = m.sem("r_cand_second")
    cx2 = m.sem("r_cand_second_places")
    ints = m.sem("r_ints")
    floats = m.sem("r_floats")
    lessd = m.sem("r_lessed")
    expd = m.sem("r_expd")
    sums = m.sem("r_sums")
    invd = m.sem("r_invd")
    hotd = m.sem("r_hotd")
    vald = m.sem("r_vald")
    outd = m.sem("r_outd")
    H = PEER_HEADS
    N = TT * TOPK
    PAIRS_T = TT // 2
    UNITS = 6
    END_UNIT = H * UNITS

    def score_at(i, s):
        return m.psum[:, 4 + 2 * ((i // 2) % 2) + s, (i % 2) * P:(i % 2 + 1) * P]

    def last(g):
        return isinstance(g, int) and g == H - 1

    with nc.Block() as block:
        @block.sync
        def _(sp):
            sp.dma_start(knat[:], a.sub_keys[0].rearrange("h s k d -> k (h s) d")).then_inc(keysl, 16)
            w_q = a.w_query[0].rearrange("(k p) (c n) -> c p k n", p=P, n=P)

            def load_w(g, u):
                at_least(sp, lo, g - 1)
                sp.dma_start(raw[:, u], w_q[g]).then_inc(landed[u], 16)

            def head(g, u):
                if not (isinstance(g, int) and g >= H - 2):
                    load_w(g + 2, u)
                ah.load(sp, g * 2 + 2, 0)
                ah.store(sp, g * 2, 0)
                ah.load(sp, g * 2 + 3, 1)
                ah.store(sp, g * 2 + 1, 1)
            load_w(0, 0)
            load_w(1, 1)
            ah.load(sp, 0, 0)
            ah.load(sp, 1, 1)
            steps(sp, 0, H, 2, head)
            for n in range(AHEAD_HEADS, AHEAD_ROUTING):
                if n + 2 < AHEAD_ROUTING:
                    ah.load(sp, n + 2, n % 2)
                ah.store(sp, n, n % 2)
            ah.finish(sp)

        @block.tensor
        def _(pe):
            pe.wait_ge(keysl, 16)
            for q in range(2):
                for i in range(4):
                    h = 4 * q + i
                    mm = nc.tensor.transpose(m.psum[:, 2 + q, i * P:(i + 1) * P],
                                             knat[:, 2 * h:2 * h + 2].rearrange("p s d -> p (s d)"), t.ident[:])
                mm.then_inc(kturned, 1)
            pe.wait_ge(kcopied, 2)

            def query(g, u, unit):
                pe.wait_ge(lo, g + 1)
                for h in range(NH):
                    at_least(pe, drained, unit + (h - 1))
                    cols = slice(h * HALF, (h + 1) * HALF)
                    three_pass(nc, m.psum[:, h], lambda k: w_hi[:, u, k], lambda k: w_lo[:, u, k],
                               lambda k: t.hT_hi[:, k, cols], lambda k: t.hT_lo[:, k, cols], KT) \
                        .then_inc(produced, 1)

            def ahead_half(n, u, h, unit):
                if h == 0:
                    pe.wait_ge(ah.lo_done, n + 1)
                pe.wait_ge(drained, unit - 1)
                for k in range(KT):
                    mm = ah.product(m.psum[:, h], u, h, k)
                mm.then_inc(produced, 1)

            def score(g, u, pair):
                if pair == 0:
                    pe.wait_ge(kstaged, g + 1)
                    pe.wait_ge(drained, g * UNITS + 2)
                if not (isinstance(g, int) and g == 0 and pair < 2):
                    pe.wait_ge(x1, g * 2 * TT + (4 * pair - 4))
                    pe.wait_ge(l1, g * 2 * TT + (4 * pair - 4))
                for i in (2 * pair, 2 * pair + 1):
                    for s in range(2):
                        rows = slice(s * HD, (s + 1) * HD)
                        mm = nc.tensor.matmul(score_at(i, s), qT[rows, u, i * P:(i + 1) * P], kst[rows, u],
                                              start=True, stop=True)
                mm.then_inc(scored, 1)

            def head(g, u):
                unit = g * UNITS + 2
                ah.turn(pe, g * 2 + 1, 1)
                score(g, u, 0)
                score(g, u, 1)
                ahead_half(g * 2, 0, 0, unit)
                score(g, u, 2)
                ahead_half(g * 2, 0, 1, unit + 1)
                ah.turn(pe, g * 2 + 2, 0)
                score(g, u, 3)
                ahead_half(g * 2 + 1, 1, 0, unit + 2)
                ahead_half(g * 2 + 1, 1, 1, unit + 3)
                if not last(g):
                    query(g + 1, 1 - u, unit + 4)
            query(0, 0, 0)
            ah.turn(pe, 0, 0)
            steps(pe, 0, H, 2, head)
            for n in range(AHEAD_HEADS, AHEAD_ROUTING):
                if n + 1 < AHEAD_ROUTING:
                    ah.turn(pe, n + 1, (n + 1) % 2)
                for h in range(NH):
                    ahead_half(n, n % 2, h, END_UNIT + NH * (n - AHEAD_HEADS) + h)

        @block.scalar
        def _(act):
            for q in range(2):
                act.wait_ge(kturned, q + 1)
                nc.scalar.activation(kT[:, 4 * q:4 * q + 4], m.psum[:, 2 + q].rearrange("p (h k) -> p h k", k=P),
                                     ACT.Copy).then_inc(kcopied, 1)

            def split(g, u, unit):
                act.wait_ge(landed[u], (g - u) * 8 + 16)
                at_least(act, produced, unit)
                nc.scalar.activation(w_hi[:, u], raw[:, u], ACT.Copy).then_inc(hi, 1)

            def queries(g, u, unit):
                if not (isinstance(g, int) and g < 2):
                    act.wait_ge(scored, g * PAIRS_T - PAIRS_T)
                hold(act, t)
                nc.scalar.activation(kst[:, u], kT[:, g], ACT.Copy).then_inc(kstaged, 1)
                for h in range(NH):
                    act.wait_ge(produced, unit + (h + 1))
                    nc.scalar.activation(qT[:, u, h * HALF:(h + 1) * HALF], m.psum[:, h], ACT.Copy) \
                        .then_inc(drained, 1)

            def gelu(n, u, h, unit):
                act.wait_ge(produced, unit + 1)
                ah.gelu(act, m.psum[:, h], n, u, h)
                act.wait_ge(ah.gelued, n * 2 + (h + 1))
                act.sem_inc(drained, 1)

            def softmax_exp(g):
                act.wait_ge(lessd, g + 1)
                nc.scalar.activation(ex[:], less[:], ACT.Exp).then_inc(expd, 1)

            def head(g, u):
                unit = g * UNITS + 2
                if not (isinstance(g, int) and g >= H - 2):
                    split(g + 2, u, unit)
                ah.split(act, g * 2 + 1, 1)
                gelu(g * 2, 0, 0, unit)
                gelu(g * 2, 0, 1, unit + 1)
                ah.split(act, g * 2 + 2, 0)
                gelu(g * 2 + 1, 1, 0, unit + 2)
                if not (isinstance(g, int) and g == 0):
                    softmax_exp(g - 1)
                gelu(g * 2 + 1, 1, 1, unit + 3)
                if not last(g):
                    queries(g + 1, 1 - u, unit + 4)
            act.wait_ge(kcopied, 2)
            split(0, 0, 0)
            split(1, 1, 0)
            queries(0, 0, 0)
            ah.split(act, 0, 0)
            steps(act, 0, H, 2, head)
            for n in range(AHEAD_HEADS, AHEAD_ROUTING):
                if n + 1 < AHEAD_ROUTING:
                    ah.split(act, n + 1, (n + 1) % 2)
                for h in range(NH):
                    gelu(n, n % 2, h, END_UNIT + NH * (n - AHEAD_HEADS) + h)
                    if n == AHEAD_ROUTING - 2 and h == 0:
                        softmax_exp(H - 1)

        @block.vector
        def _(dve):
            def held(g):
                if not isinstance(g, int):
                    hold(dve, t)

            def first_level(g, u, pair):
                jobs = [(i, s) for i in (2 * pair, 2 * pair + 1) for s in range(2)]

                def n(i, s):
                    return g * 2 * TT + (2 * i + s + 1)
                lf = {(i, s): left[:, 2 * (i % 2) + s] for i, s in jobs}
                if not (isinstance(g, int) and g < 2) and pair == 0:
                    dve.wait_ge(outd, g * 3 - 3)
                for i, s in jobs:
                    if s == 0 and i % 2 == 0:
                        dve.wait_ge(scored, g * PAIRS_T + (pair + 1))
                        held(g)
                    nc.vector.max(best[:, u, i, s, 0:8], score_at(i, s)).then_inc(v1, 1)
                for i, s in jobs:
                    dve.wait_ge(v1, n(i, s))
                    held(g)
                    nc.vector.max_index(where[:, u, i, s, 0:8], best[:, u, i, s, 0:8], score_at(i, s)) \
                        .then_inc(x1, 1)
                for i, s in jobs:
                    if not (isinstance(g, int) and g == 0 and pair == 0):
                        dve.wait_ge(x2, n(i, s) - 4)
                        held(g)
                    nc.vector.match_replace(lf[i, s], best[:, u, i, s, 0:8], score_at(i, s), TAKEN).then_inc(l1, 1)
                for i, s in jobs:
                    dve.wait_ge(l1, n(i, s))
                    held(g)
                    nc.vector.max(best[:, u, i, s, 8:16], lf[i, s]).then_inc(v2, 1)
                for i, s in jobs:
                    dve.wait_ge(v2, n(i, s))
                    held(g)
                    nc.vector.max_index(where[:, u, i, s, 8:16], best[:, u, i, s, 8:16], lf[i, s]).then_inc(x2, 1)

            def second_level(g, u, pair):
                tiles = (2 * pair, 2 * pair + 1)

                def n(i):
                    return g * TT + (i + 1)
                dve.wait_ge(v2, g * 2 * TT + (4 * pair + 4))
                for i in tiles:
                    if not (isinstance(g, int) and g == 0 and pair == 0):
                        dve.wait_ge(cl1, n(i) - 2)
                        dve.wait_ge(cx1, n(i) - 2)
                    s1 = best[:, u, i, 0, :].unsqueeze(2).to_broadcast([P, TOPK, TOPK])
                    s2 = best[:, u, i, 1, :].unsqueeze(1).to_broadcast([P, TOPK, TOPK])
                    nc.vector.tensor_tensor(cand[:, i % 2].rearrange("p (x y) -> p x y", y=TOPK), s1, s2,
                                            ALU.add).then_inc(cd, 1)
                for i in tiles:
                    dve.wait_ge(cd, n(i))
                    held(g)
                    nc.vector.max(top[:, u, i, 0:8], cand[:, i % 2]).then_inc(cv1, 1)
                for i in tiles:
                    dve.wait_ge(cv1, n(i))
                    held(g)
                    nc.vector.max_index(pos[:, u, i, 0:8], top[:, u, i, 0:8], cand[:, i % 2]).then_inc(cx1, 1)
                for i in tiles:
                    if not (isinstance(g, int) and g == 0 and pair == 0):
                        dve.wait_ge(cx2, n(i) - 2)
                        held(g)
                    nc.vector.match_replace(cleft[:, i % 2], top[:, u, i, 0:8], cand[:, i % 2], TAKEN) \
                        .then_inc(cl1, 1)
                for i in tiles:
                    dve.wait_ge(cl1, n(i))
                    held(g)
                    nc.vector.max(top[:, u, i, 8:16], cleft[:, i % 2]).then_inc(cv2, 1)
                for i in tiles:
                    dve.wait_ge(cv2, n(i))
                    held(g)
                    nc.vector.max_index(pos[:, u, i, 8:16], top[:, u, i, 8:16], cleft[:, i % 2]).then_inc(cx2, 1)

            def places(g, u):
                dve.wait_ge(cv2, g * TT + TT)
                nc.vector.tensor_tensor(less[:], top[:, u], top[:, u, :, 0:1].to_broadcast([P, TT, TOPK]),
                                        ALU.subtract).then_inc(lessd, 1)
                dve.wait_ge(cx2, g * TT + TT)
                flatpos = pos[:, u].rearrange("p i k -> p (i k)")
                nc.vector.tensor_scalar(ab[:, 0], flatpos, 4, None, ALU.logical_shift_right).then_inc(ints, 1)
                nc.vector.tensor_scalar(ab[:, 1], flatpos, 15, None, ALU.bitwise_and).then_inc(ints, 1)
                dve.wait_ge(x2, g * 2 * TT + 2 * TT)
                nc.vector.tensor_copy(wf[:], where[:, u]).then_inc(floats, 1)
                dve.wait_ge(ints, g * 2 + 2)
                nc.vector.tensor_copy(abf[:], ab[:]).then_inc(floats, 1)
                dve.wait_ge(floats, g * 2 + 2)
                for s in range(2):
                    row = t.iota[:, 0:TOPK].unsqueeze(1).to_broadcast([P, N, TOPK])
                    mine = abf[:, s].unsqueeze(2).to_broadcast([P, N, TOPK])
                    nc.vector.tensor_tensor(hot[:, s], mine, row, ALU.is_equal).then_inc(hotd, 1)

            def results(g):
                dve.wait_ge(expd, g + 1)
                nc.vector.tensor_reduce(rsum[:], ex[:], AX.X, ALU.add).then_inc(sums, 1)
                dve.wait_ge(sums, g + 1)
                nc.vector.reciprocal(rinv[:], rsum[:]).then_inc(invd, 1)
                dve.wait_ge(invd, g + 1)
                nc.vector.tensor_tensor(t.route[:, 2, :, bass.ds(g * TOPK, TOPK)], ex[:],
                                        rinv[:].unsqueeze(2).to_broadcast([P, TT, TOPK]), ALU.mult) \
                    .then_inc(outd, 1)
                for s in range(2):
                    dve.wait_ge(vald, g * 2 + (s + 1))
                    nc.vector.tensor_reduce(t.route[:, s, :, bass.ds(g * TOPK, TOPK)],
                                            hot[:, s].rearrange("p (i k) j -> p i k j", k=TOPK), AX.X, ALU.add) \
                        .then_inc(outd, 1)

            def head(g, u):
                before = not (isinstance(g, int) and g == 0)
                first_level(g, u, 0)
                first_level(g, u, 1)
                second_level(g, u, 0)
                if before:
                    places(g - 1, 1 - u)
                first_level(g, u, 2)
                second_level(g, u, 1)
                first_level(g, u, 3)
                second_level(g, u, 2)
                if before:
                    results(g - 1)
                second_level(g, u, 3)
            steps(dve, 0, H, 2, head)
            places(H - 1, (H - 1) % 2)
            results(H - 1)

        @block.gpsimd
        def _(pool):
            def rest(g, u):
                pool.wait_ge(hi, g + 1)
                nc.gpsimd.tensor_tensor(w_lo[:, u], raw[:, u], w_hi[:, u].bitcast(F32), ALU.subtract) \
                    .then_inc(lo, 1)

            def chosen(g):
                for s in range(2):
                    pool.wait_ge(hotd, g * 2 + (s + 1))
                    lists = wf[:, :, s, :].unsqueeze(2).to_broadcast([P, TT, TOPK, TOPK])
                    both = hot[:, s].rearrange("p (i k) j -> p i k j", k=TOPK)
                    nc.gpsimd.tensor_tensor(both, both, lists, ALU.mult).then_inc(vald, 1)

            def head(g, u):
                ah.rest(pool, g * 2 + 1, 1)
                if not (isinstance(g, int) and g >= H - 2):
                    rest(g + 2, u)
                ah.rest(pool, g * 2 + 2, 0)
                if not (isinstance(g, int) and g == 0):
                    chosen(g - 1)
            rest(0, 0)
            rest(1, 1)
            ah.rest(pool, 0, 0)
            steps(pool, 0, H, 2, head)
            for n in range(AHEAD_HEADS + 1, AHEAD_ROUTING):
                ah.rest(pool, n, n % 2)
            chosen(H - 1)


def gate_table(nc, m, t, a):
    ah = Ahead(nc, m, t, a, "ga_", AHEAD_ROUTING, AHEAD_TABLE)
    TB = TABLE_TOKENS
    GT = 4
    STEPS = AHEAD_TABLE
    GS = S // GT // STEPS
    BS = TB // GT // GS
    out = m.at("g_table", [P, 2, P, TB], 84)
    rT = m.at("g_routeT", [P, 3, S], 148)
    g_hi = m.at("g_hi", [P, S], 160, F32R)
    g_lo = m.at("g_lo", [P, S], 164, F32R)
    hot = m.at("g_hot", [P, 2, 3, GT, P], 192, F32R)
    hot1 = m.at("g_hot1", [P, 2, GT, P], 204, BF16)
    turned = m.sem("g_turned")
    copied = m.sem("g_copied")
    hi = m.sem("g_hi_done")
    lo = m.sem("g_lo_done")
    hot1_d = m.sem("g_hot1_done")
    hot_d = m.sem("g_hot_done")
    hot_hi_d = m.sem("g_hot_hi_done")
    hotlo_d = m.sem("g_hotlo_done")
    done = m.sem("g_done")
    out_s = m.sem("g_out")
    a_done = m.sem("g_ahead_done")
    stored = t.table_stored

    def last(n):
        return isinstance(n, int) and n == STEPS - 1

    def cols(x, tok, n):
        return x[:, tok:tok + n] if isinstance(tok, int) else x[:, bass.ds(tok, n)]

    with nc.Block() as block:
        @block.tensor
        def _(pe):
            for x in range(6):
                c, h = divmod(x, NH)
                if x >= 4:
                    pe.wait_ge(copied, x - 3)
                for i in range(4):
                    mm = nc.tensor.transpose(m.psum[:, 4 + x % 4, i * P:(i + 1) * P], t.route[:, c, 4 * h + i],
                                             t.ident[:])
                mm.then_inc(turned, 1)
            ah.turn(pe, 0, 0)
            pe.wait_ge(copied, 6)

            def group(g, y):
                pe.wait_ge(hot_hi_d, g + 1)
                pe.wait_ge(hotlo_d, g + 1)
                at_least(pe, out_s, g - 3)
                for c in range(GT):
                    o = m.psum[:, 4 + y % 4, c * P:(c + 1) * P]
                    nc.tensor.matmul(o, hot[:, y % 2, 0, c], hot[:, y % 2, 1, c], start=True, stop=False)
                    mm = nc.tensor.matmul(o, hot[:, y % 2, 0, c], hot[:, y % 2, 2, c], start=False, stop=True)
                mm.then_inc(done, 1)

            def step(n, u):
                if not last(n):
                    ah.turn(pe, n + 1, 1 - u)
                pe.wait_ge(ah.lo_done, n + 1)
                for h in range(NH):
                    at_least(pe, ah.gelued, n * 2 + (h - 1))
                    for k in range(KT):
                        mm = ah.product(m.psum[:, h], u, h, k)
                        if k == KT - 1:
                            mm.then_inc(a_done, 1)
                        if k % 2:
                            y = h * 4 + k // 2
                            group(n * GS + y, y)
            steps(pe, 0, STEPS, 2, step)

        @block.vector
        def _(dve):
            for x in range(6):
                c, h = divmod(x, NH)
                dve.wait_ge(turned, x + 1)
                nc.vector.tensor_copy(rT[:, c, h * HALF:(h + 1) * HALF], m.psum[:, 4 + x % 4]).then_inc(copied, 1)
            dve.wait_ge(hi, 1)
            nc.vector.tensor_tensor(g_lo[:], rT[:, 2], g_hi[:].bitcast(F32), ALU.subtract).then_inc(lo, 1)

            def one_hots(g, y):
                row = t.iota[:].unsqueeze(1).to_broadcast([P, GT, P])
                tok = g * GT
                at_least(dve, hotlo_d, g - 1)
                nc.vector.tensor_tensor(hot1[:, y % 2], row,
                                        cols(rT[:, 0], tok, GT).unsqueeze(2).to_broadcast([P, GT, P]),
                                        ALU.is_equal).then_inc(hot1_d, 1)
                at_least(dve, done, g - 1)
                nc.vector.tensor_tensor(hot[:, y % 2, 0], row,
                                        cols(rT[:, 1], tok, GT).unsqueeze(2).to_broadcast([P, GT, P]),
                                        ALU.is_equal).then_inc(hot_d, 1)

            def step(n, u):
                for y in range(GS):
                    g = n * GS + y
                    dve.wait_ge(hot1_d, g + 1)
                    nc.vector.tensor_tensor(hot[:, y % 2, 1], hot1[:, y % 2],
                                            cols(g_hi[:].bitcast(F32), g * GT, GT).unsqueeze(2)
                                            .to_broadcast([P, GT, P]), ALU.mult).then_inc(hot_hi_d, 1)
                    if not (last(n) and y == GS - 1):
                        one_hots(g + 1, y + 1)
            one_hots(0, 0)
            steps(dve, 0, STEPS, 2, step)

        @block.gpsimd
        def _(pool):
            ah.rest(pool, 0, 0)
            pool.wait_ge(lo, 1)

            def step(n, u):
                for y in range(GS):
                    g = n * GS + y
                    pool.wait_ge(hot1_d, g + 1)
                    at_least(pool, done, g - 1)
                    if not isinstance(g, int):
                        hold(pool, t)
                    nc.gpsimd.tensor_tensor(hot[:, y % 2, 2], hot1[:, y % 2],
                                            cols(g_lo[:].bitcast(F32), g * GT, GT).unsqueeze(2)
                                            .to_broadcast([P, GT, P]), ALU.mult).then_inc(hotlo_d, 1)
                    if y == 3 and not last(n):
                        ah.rest(pool, n + 1, 1 - u)
            steps(pool, 0, STEPS, 2, step)

        @block.scalar
        def _(act):
            ah.split(act, 0, 0)
            act.wait_ge(copied, 6)
            nc.scalar.activation(g_hi[:], rT[:, 2], ACT.Copy).then_inc(hi, 1)

            def step(n, q):
                u, buf = q % 2, q // BS
                if q % BS == 0:
                    at_least(act, stored[buf], (n - q) * (16 // (2 * BS)))
                for y in range(GS):
                    g = n * GS + y
                    act.wait_ge(done, g + 1)
                    tok = (q % BS) * GS * GT + y * GT
                    nc.scalar.activation(out[:, buf, :, tok:tok + GT],
                                         m.psum[:, 4 + y % 4].rearrange("p (c e) -> p e c", e=P), ACT.Copy) \
                        .then_inc(out_s, 1)
                    if y == 1 and not last(n):
                        ah.split(act, n + 1, 1 - u)
                    if y % 4 == 3:
                        act.wait_ge(a_done, n * 2 + (y // 4 + 1))
                        ah.gelu(act, m.psum[:, y // 4], n, u, y // 4)
            steps(act, 0, STEPS, 2 * BS, step)

        @block.sync
        def _(sp):
            def step(n, q):
                u, buf = q % 2, q // BS
                if not (isinstance(n, int) and n >= STEPS - 2):
                    ah.load(sp, n + 2, u)
                ah.store(sp, n, u)
                if q % BS == BS - 1:
                    sp.wait_ge(out_s, n * GS + GS)
                    tok = (n + 1) * (GS * GT) - TB
                    words = slice(tok * P, (tok + TB) * P) if isinstance(tok, int) else bass.ds(tok * P, TB * P)
                    sp.dma_start(t.table[:, words], out[:, buf].rearrange("p e c -> p (e c)")) \
                        .then_inc(stored[buf], 16)
            ah.load(sp, 0, 0)
            ah.load(sp, 1, 1)
            steps(sp, 0, STEPS, 2 * BS, step)
            ah.finish(sp)


def experts(nc, m, t, a, out):
    acc = t.acc
    W_hi = m.at("e_w_hi", [P, 4, S], 116, F32R)
    W_lo = m.at("e_w_lo", [P, 4, S], 132, F32R)
    U_hi = m.at("e_u_hi", [P, 4, D], 148, F32R)
    U_lo = m.at("e_u_lo", [P, 4, D], 164, F32R)
    left = m.at("e_left", [P, 2, D], 180)
    DT_hi = m.at("e_downT_hi", [P, KT, P], 188, F32R)
    DT_lo = m.at("e_downT_lo", [P, KT, P], 192, F32R)
    Uraw = m.at("e_up", [P, 2, D], 196)
    Gc = m.at("e_table", [P, 2, S], 7)
    Wg = m.at("e_gelu", [P, S], 15)
    l_land = [m.sem(f"e_left_landed{i}") for i in range(2)]
    u_land = [m.sem(f"e_up_landed{i}") for i in range(2)]
    g_land = [m.sem(f"e_table_landed{i}") for i in range(2)]
    turned = m.sem("e_turned")
    dt_hi = m.sem("e_dt_hi")
    dt_lo = m.sem("e_dt_lo")
    a_done = m.sem("e_a_done")
    gelu = m.sem("e_gelu_done")
    mul = m.sem("e_mul")
    w_hi = m.sem("e_w_hi_done")
    w_lo = m.sem("e_w_lo_done")
    u_hi = m.sem("e_u_hi_done")
    u_lo = m.sem("e_u_lo_done")
    b_grp = m.sem("e_b_group")
    acc_d = m.sem("e_acc")
    NG = N_CHUNKS
    GROUPS = 16
    x1 = m.at("f_x1", [P, TT, D], 20)
    gf = m.at("f_gain", [P, D], 52)
    junk = m.at("f_junk", [P, 2, D], 56)
    res = m.at("f_out", [P, 4, D], 64)
    ssq = m.at("f_ssq", [P, TT], 80)
    mean = m.at("f_mean", [P, TT], 80.25)
    std = m.at("f_std", [P, TT], 80.5)
    rstd = m.at("f_rstd", [P, TT], 80.75)
    x_land = [m.sem(f"f_x1_landed{i}") for i in range(TT)]
    gf_land = m.sem("f_gain_landed")
    gated = m.sem("f_gated")
    added = m.sem("f_added")
    squared = m.sem("f_squared")
    meaned = m.sem("f_mean_done")
    root = m.sem("f_root")
    inv = m.sem("f_inv")
    ready = m.sem("f_ready")
    out_stored = [m.sem(f"f_stored{i}") for i in range(4)]
    GRP = TT // NH

    FRESH = NG - AHEAD

    def both(eng, body):
        steps(eng, 0, FRESH, 4, lambda g, q: body(g, q, False))
        steps(eng, FRESH, AHEAD, 4, lambda g, q: body(g, q, True))

    def chunk(g, ahead):
        return g - FRESH if ahead else g + AHEAD

    def next_turns(g, ahead):
        return not ahead and not (isinstance(g, int) and g == FRESH - 1)

    with nc.Block() as block:
        @block.sync
        def _(sp):
            def rows(src, g):
                return src[0, g * P:(g + 1) * P, :] if isinstance(g, int) else src[0, bass.ds(g * P, P), :]

            def plane(src, g):
                return src[g] if isinstance(g, int) else src[bass.ds(g, 1), :, :].rearrange("o p c -> (o p) c")

            def load_left(g, u, ahead):
                if ahead and not (isinstance(g, int) and g < FRESH + 2):
                    sp.wait_ge(mul, g * 2 - 2)
                else:
                    at_least(sp, turned, g - 1)
                src = plane(t.gelus, chunk(g, True)) if ahead else rows(a.expert_down, chunk(g, False))
                sp.dma_start(left[:, u], src).then_inc(l_land[u], 16)

            def load_up(g, u, ahead):
                at_least(sp, u_lo, g - 1)
                sp.dma_start(Uraw[:, u], rows(a.expert_up, chunk(g, ahead))).then_inc(u_land[u], 16)

            def load_table(g, u, ahead):
                at_least(sp, w_lo, g - 1)
                blocks = t.table.rearrange("p (b e c) -> p b e c", e=N_CHUNKS, c=TABLE_TOKENS)
                c = chunk(g, ahead)
                part = blocks[:, :, c] if isinstance(c, int) else \
                    blocks[:, :, bass.ds(c, 1)].rearrange("p b o c -> p b (o c)")
                sp.dma_start(Gc[:, u].rearrange("p (b c) -> p b c", c=TABLE_TOKENS), part).then_inc(g_land[u], 16)

            def step(g, q, ahead):
                u = q % 2
                if not (isinstance(g, int) and g == NG - 1):
                    load_left(g + 1, 1 - u, ahead or (isinstance(g, int) and g == FRESH - 1))
                if isinstance(g, int) and g == 0:
                    load_up(g, u, ahead)
                    for buf in range(2):
                        sp.wait_ge(t.table_stored[buf], 16 * S // TABLE_TOKENS // 2)
                    load_table(g, u, ahead)
                else:
                    load_table(g, u, ahead)
                    load_up(g, u, ahead)
            load_left(0, 0, False)
            both(sp, step)
            sp.wait_ge(a_done, 2 * FRESH)
            sp.dma_start(gf[:], a.final_norm_g.rearrange("(o d) -> o d", o=1).partition_broadcast(P)) \
                .then_inc(gf_land, 16)
            for i in range(TT):
                sp.dma_start(x1[:, i], t.x1[i * P:(i + 1) * P, :]).then_inc(x_land[i], 16)
            for i in range(TT):
                sp.wait_ge(ready, i + 1)
                sp.dma_start(out[0, i * P:(i + 1) * P, :], res[:, i % 4]).then_inc(out_stored[i % 4], 16)
            for s in range(4):
                sp.wait_ge(out_stored[s], 16 * TT // 4)

        @block.tensor
        def _(pe):
            def turn(g, u):
                pe.wait_ge(l_land[u], (g - u) * 8 + 16)
                for k in range(KT):
                    mm = nc.tensor.transpose(m.psum[:, 2 + k // 4, (k % 4) * P:(k % 4 + 1) * P],
                                             left[:, u, k * P:(k + 1) * P], t.ident[:])
                mm.then_inc(turned, 1)

            def activations(g):
                pe.wait_ge(dt_lo, g + 1)
                for h in range(NH):
                    at_least(pe, gelu, g * 2 + (h - 1))
                    cols = slice(h * HALF, (h + 1) * HALF)
                    three_pass(nc, m.psum[:, h], lambda k: DT_hi[:, k], lambda k: DT_lo[:, k],
                               lambda k: t.hT_hi[:, k, cols], lambda k: t.hT_lo[:, k, cols], KT) \
                        .then_inc(a_done, 1)

            def up_part(g, q):
                c, pair = q % 2, 2 * ((q // 2) ^ 1)
                pe.wait_ge(w_lo, g - c)
                pe.wait_ge(u_lo, g - c)
                for j in range(8 * c, 8 * c + 8):
                    at_least(pe, acc_d, g * 8 + (j - 3 - 8 * (c + 2)))
                    rows = slice((j // 2) * P, (j // 2 + 1) * P)
                    cols = slice((j % 2) * HALF, (j % 2 + 1) * HALF)
                    three_pass(nc, m.psum[:, 4 + j % 4], lambda k: W_hi[:, pair + k, rows],
                               lambda k: W_lo[:, pair + k, rows], lambda k: U_hi[:, pair + k, cols],
                               lambda k: U_lo[:, pair + k, cols], 2).then_inc(b_grp, 1)

            def step(g, q, ahead):
                if not ahead:
                    activations(g)
                if next_turns(g, ahead):
                    turn(g + 1, (q + 1) % 2)
                if not (isinstance(g, int) and g < 2):
                    up_part(g, q)
            turn(0, 0)
            both(pe, step)
            up_part(NG, 0)
            up_part(NG + 1, 1)

        @block.scalar
        def _(act):
            def downT(g):
                act.wait_ge(turned, g + 1)
                at_least(act, a_done, g * 2)
                nc.scalar.activation(DT_hi[:].rearrange("p k n -> p (k n)"),
                                     m.psum[:, 2:4].rearrange("p b n -> p (b n)"), ACT.Copy).then_inc(dt_hi, 1)

            def step(g, q, ahead):
                if not ahead:
                    for h in range(NH):
                        act.wait_ge(a_done, g * 2 + (h + 1))
                        at_least(act, mul, g * 2 + (h - 1))
                        nc.scalar.activation(Wg[:, h * HALF:(h + 1) * HALF], m.psum[:, h], ACT.Gelu) \
                            .then_inc(gelu, 1)
                if next_turns(g, ahead):
                    downT(g + 1)
                act.wait_ge(mul, g * 2 + 2)
                if not (isinstance(g, int) and g < 4):
                    act.wait_ge(b_grp, g * 8 - 8 * (q % 2 + 2))
                nc.scalar.activation(W_hi[:, q], Gc[:, q % 2], ACT.Copy).then_inc(w_hi, 1)
                act.wait_ge(u_land[q % 2], (g - q % 2) * 8 + 16)
                nc.scalar.activation(U_hi[:, q], Uraw[:, q % 2], ACT.Copy).then_inc(u_hi, 1)
            downT(0)
            both(act, step)
            for i in range(TT):
                act.wait_ge(added, i + 1)
                if i >= 2:
                    act.wait_ge(squared, i - 1)
                nc.scalar.activation(junk[:, i % 2], acc[:, i], ACT.Square, accum_out=ssq[:, i:i + 1]) \
                    .then_inc(squared, 1)
                if i % GRP == GRP - 1:
                    g = i // GRP
                    act.wait_ge(meaned, g + 1)
                    nc.scalar.activation(std[:, GRP * g:GRP * g + GRP], mean[:, GRP * g:GRP * g + GRP], ACT.Sqrt) \
                        .then_inc(root, 1)

        @block.vector
        def _(dve):
            def downT(g):
                dve.wait_ge(dt_hi, g + 1)
                nc.vector.tensor_tensor(DT_lo[:].rearrange("p k n -> p (k n)"),
                                        m.psum[:, 2:4].rearrange("p b n -> p (b n)"),
                                        DT_hi[:].rearrange("p k n -> p (k n)").bitcast(F32),
                                        ALU.subtract).then_inc(dt_lo, 1)

            def add_part(g, q, behind=None):
                c = q % 2
                for j in range(8 * c, 8 * c + 8):
                    J = g * 8 + (j - 8 * (c + 2))
                    dve.wait_ge(b_grp, J + 1)
                    at_least(dve, acc_d, J - (GROUPS - 1))
                    out = acc[:, j // 2, (j % 2) * HALF:(j % 2 + 1) * HALF]
                    if isinstance(g, int) and g < 4:
                        nc.vector.tensor_copy(out, m.psum[:, 4 + j % 4]).then_inc(acc_d, 1)
                    else:
                        nc.vector.tensor_tensor(out, out, m.psum[:, 4 + j % 4], ALU.add).then_inc(acc_d, 1)
                    if behind and j % 2:
                        behind(j // 2)

            def residual(i):
                dve.wait_ge(gated, i + 1)
                dve.wait_ge(x_land[i], 16)
                nc.vector.tensor_tensor(acc[:, i], acc[:, i], x1[:, i], ALU.add).then_inc(added, 1)

            def means(g):
                c = slice(GRP * g, GRP * g + GRP)
                dve.wait_ge(squared, GRP * (g + 1))
                nc.vector.tensor_scalar(mean[:, c], ssq[:, c], 1.0 / D, EPS, ALU.mult, ALU.add) \
                    .then_inc(meaned, 1)

            def invert(g):
                c = slice(GRP * g, GRP * g + GRP)
                dve.wait_ge(root, g + 1)
                nc.vector.reciprocal(rstd[:, c], std[:, c]).then_inc(inv, 1)

            def results(first, count):
                dve.wait_ge(inv, first // GRP + 1)
                dve.wait_ge(gf_land, 16)
                for i in range(first, first + count):
                    if i >= 4:
                        dve.wait_ge(out_stored[i % 4], 16)
                    nc.vector.scalar_tensor_tensor(out=res[:, i % 4], in0=acc[:, i], scalar=rstd[:, i:i + 1],
                                                   in1=gf[:], op0=ALU.mult, op1=ALU.mult).then_inc(ready, 1)

            def step(g, q, ahead):
                u = q % 2
                dve.wait_ge(g_land[u], (g - u) * 8 + 16)
                if ahead:
                    dve.wait_ge(l_land[u], (g - u) * 8 + 16)
                for h in range(NH):
                    if not ahead:
                        dve.wait_ge(gelu, g * 2 + (h + 1))
                    cols = slice(h * HALF, (h + 1) * HALF)
                    act_out = left[:, u, cols] if ahead else Wg[:, cols]
                    nc.vector.tensor_tensor(Gc[:, u, cols], act_out, Gc[:, u, cols], ALU.mult).then_inc(mul, 1)
                if next_turns(g, ahead):
                    downT(g + 1)
                if not (isinstance(g, int) and g < 2):
                    add_part(g, q)
            downT(0)
            both(dve, step)

            def behind(i):
                if i >= 1:
                    residual(i - 1)
                if i == GRP + 1:
                    means(0)
                if i == GRP + 2:
                    invert(0)
            add_part(NG, 0, behind)
            add_part(NG + 1, 1, behind)
            results(0, 2)
            residual(TT - 1)
            results(2, 1)
            means(1)
            results(3, 1)
            invert(1)
            results(GRP, GRP)

        @block.gpsimd
        def _(pool):
            def step(g, q, ahead):
                pool.wait_ge(w_hi, g + 1)
                nc.gpsimd.tensor_tensor(W_lo[:, q], Gc[:, q % 2], W_hi[:, q].bitcast(F32), ALU.subtract) \
                    .then_inc(w_lo, 1)
                pool.wait_ge(u_hi, g + 1)
                nc.gpsimd.tensor_tensor(U_lo[:, q], Uraw[:, q % 2], U_hi[:, q].bitcast(F32), ALU.subtract) \
                    .then_inc(u_lo, 1)
            both(pool, step)
            for i in range(TT):
                pool.wait_ge(acc_d, NG * 8 - GROUPS + 2 * i + 2)
                nc.gpsimd.tensor_tensor(acc[:, i], acc[:, i], t.gate2[:], ALU.mult).then_inc(gated, 1)


class Arrays:

    def __init__(self, args, line_const):
        self.x = args["x"]
        self.c = args["c"]
        self.norm_mix_g = args["norm_mix_g"]
        self.norm_ffn_g = args["norm_ffn_g"]
        self.w_ada = args["w_ada"]
        self.b_ada = args["b_ada"]
        self.w_in = args["w_in"]
        self.b_forget = args["b_forget"]
        self.sinks = args["sinks"]
        self.w_branch_a = args["w_branch_a"]
        self.w_branch_b = args["w_branch_b"]
        self.w_out = args["w_out"]
        self.rel_bias = args["rel_bias"]
        self.w_query = args["w_query"]
        self.sub_keys = args["sub_keys"]
        self.expert_down = args["expert_down"]
        self.expert_up = args["expert_up"]
        self.final_norm_g = args["final_norm_g"]
        self.line_const = line_const


class Tensors:
    pass


def build(nc, args, line_const, out):
    a = Arrays(args, line_const)
    with ExitStack() as ctx:
        m = Memory(nc, ctx)
        t = Tensors()
        t.passed = m.sem("passed_waits")
        t.table_stored = [m.sem(f"table_stored{i}") for i in range(2)]
        t.ident = m.at("ident", [P, P], 0)
        t.ones = m.at("ones", [P, P], 0.5)
        t.iota = m.at("iota", [P, P], 1)
        t.mask = m.at("mask", [P, P], 1.5)
        t.cols = m.at("cols", [P, 9 * KT], 2)
        t.ccol = t.cols[:, 0:KT]
        t.bcol = t.cols[:, KT:7 * KT]
        t.gcol = t.cols[:, 7 * KT:9 * KT].rearrange("p (n k) -> p n k", k=KT)
        t.cact = m.at("cact", [P, KT], 2.3125)
        t.shift = m.at("shift", [P, 2, KT], 2.5)
        t.gain = m.at("gain", [P, 2, KT], 2.625)
        t.negsink = m.at("negsink", [P, FOX_HEADS], 2.75)
        t.bfl = m.at("bfl", [FOX_HEADS, 1], 2.8125)
        t.gate2 = m.at("gate2", [P, D], 3)
        t.gate1 = m.at("gate1", [P, D], 7)
        t.negF = m.at("negF", [FOX_HEADS, S], 15)
        t.hT_hi = m.at("hT_hi", [P, KT, S], 20, F32R)
        t.hT_lo = m.at("hT_lo", [P, KT, S], 52, F32R)
        t.qkvT = m.at("qkvT", [P, QKV_CHUNKS, S], 84)
        t.v = m.at("v", [P, TT, 5 * P], 156)
        t.kdup = m.at("kdup", [P, 2, S], 68)
        t.band = m.at("band", [P, FOX_HEADS, 2 * P], 76)
        t.o = m.at("o", [P, 2, TT, HALF], 20)
        t.mixT_hi = m.at("mixT_hi", [P, KT, S], 116, F32R)
        t.mixT_lo = m.at("mixT_lo", [P, KT, S], 148, F32R)
        t.route = m.at("route", [P, 3, TT, P], 192)
        t.acc = m.at("acc", [P, TT, D], 84)
        t.gates = m.dram("gates", [2 * KT, P, S])
        t.line_dram = m.dram("bias_line", [FOX_HEADS, P, LINE])
        t.negf_dram = m.dram("negf_rows", [FOX_HEADS, S])
        t.x1 = m.dram("x1", [S, D])
        t.gelus = m.dram("gelus_ahead", [AHEAD, P, S])
        t.table = m.dram("gate_table", [P, S // TABLE_TOKENS * N_CHUNKS * TABLE_TOKENS])

        m.stage(constants, t)
        m.stage(first_norm, t, a)
        m.stage(projections, t, a)
        m.stage(values, t, a)
        m.stage(attention, t)
        m.stage(mixing, t, a)
        m.stage(out_and_norm, t, a)
        m.stage(routing, t, a)
        m.stage(gate_table, t, a)
        m.stage(experts, t, a, out)


_INS = ["x", "c", "norm_mix_g", "norm_ffn_g", "w_ada", "b_ada", "w_in", "b_forget", "sinks", "w_branch_a",
        "w_branch_b", "w_out", "rel_bias", "w_query", "sub_keys", "expert_down", "expert_up", "final_norm_g"]


def kernel(**inputs):
    import numpy as _np
    import concourse.bacc as _bacc
    from concourse import mybir as _mybir
    from concourse.bass_utils import run_bass_kernel_spmd as _run

    nc = _bacc.Bacc("TRN2", target_bir_lowering=False, num_devices=1)
    arrays, args = {}, {}
    for name in _INS:
        arr = _np.ascontiguousarray(inputs[name])
        arrays[f"in_{name}"] = arr
        args[name] = nc.dram_tensor(f"in_{name}", arr.shape, _mybir.dt.from_np(arr.dtype),
                                    kind="ExternalInput").ap()
    line = line_constants()
    arrays["line_const"] = line
    lc = nc.dram_tensor("line_const", line.shape, _mybir.dt.float32, kind="ExternalInput").ap()
    out = nc.dram_tensor("out", (1, S, D), _mybir.dt.float32, kind="ExternalOutput").ap()
    build(nc, args, lc, out)
    r = _run(nc, [arrays], core_ids=[0])
    return r.results[0]["out"]
```
